# Optimizing a Trainium2 kernel written in Bass

```python
import math
import jax, jax.numpy as jnp
from jax import lax
import numpy as np

D_MODEL = 1024
BATCH = 1
SEQ = 1024
DEPTH = 1

HEAD_DIM = 64
N_DIFF_HEADS = 4
DIFF_V_DIM = 2 * HEAD_DIM
N_SB_HEADS = 8
DIFF_QK_WIDTH = N_DIFF_HEADS * 2 * HEAD_DIM
DIFF_V_WIDTH = N_DIFF_HEADS * DIFF_V_DIM
SB_WIDTH = N_SB_HEADS * HEAD_DIM
MIX_WIDTH = DIFF_V_WIDTH + SB_WIDTH
QKV_WIDTH = 2 * DIFF_QK_WIDTH + DIFF_V_WIDTH + 3 * SB_WIDTH
QKV_SPLITS = (DIFF_QK_WIDTH, 2 * DIFF_QK_WIDTH, 2 * DIFF_QK_WIDTH + DIFF_V_WIDTH,
              2 * DIFF_QK_WIDTH + DIFF_V_WIDTH + SB_WIDTH,
              2 * DIFF_QK_WIDTH + DIFF_V_WIDTH + 2 * SB_WIDTH)
D_FF = 2816
CONV_WIDTH = 3
N_BUCKETS = 32
MAX_DISTANCE = 128
Q_BLOCK = 128
RMS_EPS = 1e-6


def _rmsnorm(x, g):
    xf = x.astype(jnp.float32)
    y = xf * lax.rsqrt(jnp.mean(xf * xf, axis=-1, keepdims=True) + RMS_EPS)
    return (y * g.astype(jnp.float32)).astype(x.dtype)

def _lambda_init(layer):
    return 0.8 - 0.6 * math.exp(-0.3 * layer)

def _relative_bucket(rel):
    n = jnp.maximum(rel, 0)
    max_exact = N_BUCKETS // 2
    nf = jnp.maximum(n, 1).astype(jnp.float32)
    large = max_exact + (jnp.log(nf / max_exact) / math.log(MAX_DISTANCE / max_exact)
                         * (N_BUCKETS - max_exact)).astype(jnp.int32)
    large = jnp.minimum(large, N_BUCKETS - 1)
    return jnp.where(n < max_exact, n, large)

def _diff_attention(q, k, v, lam, rel_bias):
    B, H, _, S, d = q.shape
    nb = S // Q_BLOCK
    qb = q.reshape(B, H, 2, nb, Q_BLOCK, d).transpose(3, 0, 1, 2, 4, 5)
    starts = jnp.arange(nb, dtype=jnp.int32) * Q_BLOCK
    k_pos = jnp.arange(S, dtype=jnp.int32)
    scale = d ** -0.5
    table = rel_bias.astype(jnp.float32)

    def one_block(args):
        q_blk, t0 = args
        rel = (t0 + jnp.arange(Q_BLOCK, dtype=jnp.int32))[:, None] - k_pos[None, :]
        bias = jnp.transpose(table[_relative_bucket(rel)], (2, 0, 1))
        logits = jnp.einsum('bhmqd,bhmkd->bhmqk', q_blk, k).astype(jnp.float32) * scale
        logits = logits + bias[None, :, None]
        logits = jnp.where(rel >= 0, logits, -jnp.inf)
        p = jax.nn.softmax(logits, axis=-1)
        w = p[:, :, 0] - lam * p[:, :, 1]
        return jnp.einsum('bhqk,bhkd->bhqd', w.astype(v.dtype), v)

    out = lax.map(one_block, (qb, starts))
    return out.transpose(1, 2, 0, 3, 4).reshape(B, H, S, v.shape[-1])

def _stick_breaking_attention(q, k, v):
    B, H, S, d = q.shape
    nb = S // Q_BLOCK
    qb = q.reshape(B, H, nb, Q_BLOCK, d).transpose(2, 0, 1, 3, 4)
    starts = jnp.arange(nb, dtype=jnp.int32) * Q_BLOCK
    k_pos = jnp.arange(S, dtype=jnp.int32)
    scale = d ** -0.5

    def one_block(args):
        q_blk, t0 = args
        rel = (t0 + jnp.arange(Q_BLOCK, dtype=jnp.int32))[:, None] - k_pos[None, :]
        strict = rel > 0
        z = jnp.einsum('bhqd,bhkd->bhqk', q_blk, k).astype(jnp.float32) * scale
        log_beta = jax.nn.log_sigmoid(z)
        log_1mb = jnp.where(strict, jax.nn.log_sigmoid(-z), 0.0)
        between = lax.cumsum(log_1mb, axis=3, reverse=True) - log_1mb
        a = jnp.where(strict, jnp.exp(log_beta + between), 0.0)
        return jnp.einsum('bhqk,bhkd->bhqd', a.astype(v.dtype), v)

    out = lax.map(one_block, (qb, starts))
    return out.transpose(1, 2, 0, 3, 4).reshape(B, H, S, d)

def _causal_depthwise_conv(u, w, b):
    S = u.shape[1]
    up = jnp.pad(u, ((0, 0), (CONV_WIDTH - 1, 0), (0, 0)))
    y = b
    for i in range(CONV_WIDTH):
        y = y + up[:, i:i + S] * w[i]
    return y

def first_inputs(seed: int = 0) -> dict:
    key = jax.random.key(seed)
    ks = jax.random.split(key, 18)

    def nrm(k, shape, scale):
        return jax.random.normal(k, shape, jnp.float32) * scale

    def gain(k, shape):
        return 1.0 + 0.05 * jax.random.normal(k, shape, jnp.float32)

    return {
        'x': nrm(ks[0], (BATCH, SEQ, D_MODEL), 1.0),
        'attn_pre_norm': gain(ks[1], (DEPTH, D_MODEL)),
        'w_qkv': nrm(ks[2], (DEPTH, D_MODEL, QKV_WIDTH), D_MODEL ** -0.5),
        'lambda_q1': nrm(ks[3], (DEPTH, HEAD_DIM), 0.1),
        'lambda_k1': nrm(ks[4], (DEPTH, HEAD_DIM), 0.1),
        'lambda_q2': nrm(ks[5], (DEPTH, HEAD_DIM), 0.1),
        'lambda_k2': nrm(ks[6], (DEPTH, HEAD_DIM), 0.1),
        'diff_subln': gain(ks[7], (DEPTH, DIFF_V_DIM)),
        'sb_norm': gain(ks[8], (DEPTH, HEAD_DIM)),
        'rel_bias': nrm(ks[9], (N_BUCKETS, N_DIFF_HEADS), 0.5),
        'w_o': nrm(ks[10], (DEPTH, MIX_WIDTH, D_MODEL), MIX_WIDTH ** -0.5),
        'attn_post_norm': gain(ks[11], (DEPTH, D_MODEL)),
        'ffn_pre_norm': gain(ks[12], (DEPTH, D_MODEL)),
        'w_up': nrm(ks[13], (DEPTH, D_MODEL, 2 * D_FF), D_MODEL ** -0.5),
        'conv_w': nrm(ks[14], (DEPTH, CONV_WIDTH, 2 * D_FF), CONV_WIDTH ** -0.5),
        'conv_b': nrm(ks[15], (DEPTH, 2 * D_FF), 0.01),
        'w_down': nrm(ks[16], (DEPTH, D_FF, D_MODEL), D_FF ** -0.5),
        'ffn_post_norm': gain(ks[17], (DEPTH, D_MODEL)),
    }

def first_block(x, attn_pre_norm, w_qkv, lambda_q1, lambda_k1, lambda_q2, lambda_k2,
              diff_subln, sb_norm, rel_bias, w_o, attn_post_norm, ffn_pre_norm,
              w_up, conv_w, conv_b, w_down, ffn_post_norm):
    B, S, _ = x.shape
    for l in range(DEPTH):
        lam_init = _lambda_init(l)
        h = _rmsnorm(x, attn_pre_norm[l])
        qkv = h @ w_qkv[l]
        dq, dk, dv, sq, sk, sv = jnp.split(qkv, QKV_SPLITS, axis=-1)
        dq = dq.reshape(B, S, N_DIFF_HEADS, 2, HEAD_DIM).transpose(0, 2, 3, 1, 4)
        dk = dk.reshape(B, S, N_DIFF_HEADS, 2, HEAD_DIM).transpose(0, 2, 3, 1, 4)
        dv = dv.reshape(B, S, N_DIFF_HEADS, DIFF_V_DIM).transpose(0, 2, 1, 3)
        lam = (jnp.exp(jnp.sum(lambda_q1[l].astype(jnp.float32) * lambda_k1[l].astype(jnp.float32)))
               - jnp.exp(jnp.sum(lambda_q2[l].astype(jnp.float32) * lambda_k2[l].astype(jnp.float32)))
               + lam_init)
        diff_o = _diff_attention(dq, dk, dv, lam, rel_bias)
        diff_o = _rmsnorm(diff_o, diff_subln[l]) * (1.0 - lam_init)
        diff_o = diff_o.transpose(0, 2, 1, 3).reshape(B, S, DIFF_V_WIDTH)

        sq = sq.reshape(B, S, N_SB_HEADS, HEAD_DIM).transpose(0, 2, 1, 3)
        sk = sk.reshape(B, S, N_SB_HEADS, HEAD_DIM).transpose(0, 2, 1, 3)
        sv = sv.reshape(B, S, N_SB_HEADS, HEAD_DIM).transpose(0, 2, 1, 3)
        sb_o = _rmsnorm(_stick_breaking_attention(sq, sk, sv), sb_norm[l])
        sb_o = sb_o.transpose(0, 2, 1, 3).reshape(B, S, SB_WIDTH)

        mix = jnp.concatenate([diff_o, sb_o], axis=-1) @ w_o[l]
        x = x + _rmsnorm(mix, attn_post_norm[l])

        h = _rmsnorm(x, ffn_pre_norm[l])
        u = _causal_depthwise_conv(h @ w_up[l], conv_w[l], conv_b[l])
        gate, val = jnp.split(u, 2, axis=-1)
        y = (jax.nn.gelu(gate, approximate=True) * val) @ w_down[l]
        x = x + _rmsnorm(y, ffn_post_norm[l])
    return x


N_Q_HEADS = 8
N_KV_HEADS = 2
WINDOW = 128
ATTN_BLOCK = WINDOW
ROPE_THETA = 10000.0
MLSTM_HEADS = 4
MLSTM_HEAD_DIM = 128
MLSTM_CHUNK = 64
CONV_WIDTH_2 = 4
D_FF_2 = -(-8 * D_MODEL // (3 * 256)) * 256
NORM_EPS = 1e-6

ATTN_Q_WIDTH = N_Q_HEADS * HEAD_DIM
ATTN_KV_WIDTH = N_KV_HEADS * HEAD_DIM
MLSTM_WIDTH = MLSTM_HEADS * MLSTM_HEAD_DIM
IN_SPLIT_SIZES = (ATTN_Q_WIDTH, ATTN_KV_WIDTH, ATTN_KV_WIDTH,
                  MLSTM_WIDTH, MLSTM_WIDTH, MLSTM_WIDTH, MLSTM_WIDTH,
                  MLSTM_HEADS, MLSTM_HEADS, D_MODEL, D_MODEL)
IN_WIDTH = sum(IN_SPLIT_SIZES)


def rms_norm(x, g):
    xf = x.astype(jnp.float32)
    y = xf * lax.rsqrt(jnp.mean(xf * xf, axis=-1, keepdims=True) + NORM_EPS)
    return (y * g.astype(jnp.float32)).astype(x.dtype)

def modulate(h, shift, scale):
    return h * (1 + scale[:, None, :]) + shift[:, None, :]

def rope(t, positions):
    half = HEAD_DIM // 2
    inv_freq = ROPE_THETA ** (-2.0 * jnp.arange(half, dtype=jnp.float32) / HEAD_DIM)
    ang = positions.astype(jnp.float32)[..., None] * inv_freq
    cos = jnp.cos(ang)[:, :, None, :]
    sin = jnp.sin(ang)[:, :, None, :]
    tf = t.astype(jnp.float32)
    t1, t2 = tf[..., :half], tf[..., half:]
    return jnp.concatenate([t1 * cos - t2 * sin, t2 * cos + t1 * sin], axis=-1).astype(t.dtype)

def causal_depthwise_conv(u, w, b):
    S = u.shape[1]
    up = jnp.pad(u, ((0, 0), (CONV_WIDTH_2 - 1, 0), (0, 0)))
    out = b
    for j in range(CONV_WIDTH_2):
        out = out + up[:, j:j + S] * w[j]
    return out

def sliding_window_attention(q, k, v, sinks):
    B, S = q.shape[0], q.shape[1]
    nb = S // ATTN_BLOCK
    g = N_Q_HEADS // N_KV_HEADS
    qb = q.astype(jnp.float32).reshape(B, nb, ATTN_BLOCK, N_KV_HEADS, g, HEAD_DIM) * (HEAD_DIM ** -0.5)

    def band(t):
        t = t.astype(jnp.float32).reshape(B, nb, ATTN_BLOCK, N_KV_HEADS, HEAD_DIM)
        prev = jnp.pad(t, ((0, 0), (1, 0), (0, 0), (0, 0), (0, 0)))[:, :-1]
        return jnp.concatenate([prev, t], axis=2)

    kb, vb = band(k), band(v)
    s = jnp.einsum('bnqhgd,bnkhd->bnhgqk', qb, kb)
    qi = jnp.arange(ATTN_BLOCK)[:, None]
    kj = jnp.arange(2 * ATTN_BLOCK)[None, :]
    rel = kj - ATTN_BLOCK
    in_band = (rel <= qi) & (qi - rel < WINDOW)
    blk = jnp.arange(nb)[:, None, None]
    mask = in_band[None] & ((blk > 0) | (kj[None] >= ATTN_BLOCK))
    s = jnp.where(mask[None, :, None, None], s, -jnp.inf)
    sink = sinks.astype(jnp.float32).reshape(N_KV_HEADS, g)[None, None, :, :, None, None]
    m = jnp.maximum(jnp.max(s, axis=-1, keepdims=True), sink)
    p = jnp.exp(s - m)
    p = p / (jnp.sum(p, axis=-1, keepdims=True) + jnp.exp(sink - m))
    o = jnp.einsum('bnhgqk,bnkhd->bnqhgd', p, vb)
    return o.reshape(B, S, N_Q_HEADS * HEAD_DIM)

def mlstm_chunkwise(q, k, v, i_pre, f_pre):
    B, S, H, D = q.shape
    L = MLSTM_CHUNK
    nc = S // L

    def chunks(t):
        return t.astype(jnp.float32).reshape(B, nc, L, H, D).transpose(0, 3, 1, 2, 4)

    qc = chunks(q)
    kc = chunks(k) * (D ** -0.5)
    vc = chunks(v)
    ig = i_pre.astype(jnp.float32).reshape(B, nc, L, H).transpose(0, 3, 1, 2)
    logf = jax.nn.log_sigmoid(f_pre.astype(jnp.float32)).reshape(B, nc, L, H).transpose(0, 3, 1, 2)
    b = jnp.cumsum(logf, axis=-1)
    b_last = b[..., -1]
    a = b_last[..., None] - b + ig

    def step(carry, inp):
        C, n, m = carry
        k_c, v_c, a_c, bl_c = inp
        m_new = jnp.maximum(bl_c + m, jnp.max(a_c, axis=-1))
        decay = jnp.exp(bl_c + m - m_new)
        kw = k_c * jnp.exp(a_c - m_new[..., None])[..., None]
        C_new = decay[..., None, None] * C + jnp.einsum('bhld,bhle->bhde', kw, v_c)
        n_new = decay[..., None] * n + jnp.sum(kw, axis=-2)
        return (C_new, n_new, m_new), (C, n, m)

    init = (jnp.zeros((B, H, D, D), jnp.float32), jnp.zeros((B, H, D), jnp.float32),
            jnp.zeros((B, H), jnp.float32))
    xs = (kc.transpose(2, 0, 1, 3, 4), vc.transpose(2, 0, 1, 3, 4),
          a.transpose(2, 0, 1, 3), b_last.transpose(2, 0, 1))
    _, (C_prev, n_prev, m_prev) = lax.scan(step, init, xs)
    C_prev = C_prev.transpose(1, 2, 0, 3, 4)
    n_prev = n_prev.transpose(1, 2, 0, 3)
    m_prev = m_prev.transpose(1, 2, 0)

    causal = jnp.tril(jnp.ones((L, L), dtype=bool))
    d_mat = jnp.where(causal, b[..., :, None] - b[..., None, :] + ig[..., None, :], -jnp.inf)
    inter = b + m_prev[..., None]
    m_t = jnp.maximum(inter, jnp.max(d_mat, axis=-1))
    w_intra = jnp.exp(d_mat - m_t[..., None])
    w_inter = jnp.exp(inter - m_t)
    scores = jnp.einsum('bhctd,bhcsd->bhcts', qc, kc) * w_intra
    num = jnp.einsum('bhcts,bhcsd->bhctd', scores, vc) + \
        w_inter[..., None] * jnp.einsum('bhctd,bhcde->bhcte', qc, C_prev)
    den = jnp.sum(scores, axis=-1) + w_inter * jnp.einsum('bhctd,bhcd->bhct', qc, n_prev)
    h = num / jnp.maximum(jnp.abs(den), jnp.exp(-m_t))[..., None]
    return h.transpose(0, 2, 3, 1, 4).reshape(B, S, H, D)

def head_layer_norm(h, w):
    mu = jnp.mean(h, axis=-1, keepdims=True)
    var = jnp.mean(jnp.square(h - mu), axis=-1, keepdims=True)
    y = (h - mu) * lax.rsqrt(var + NORM_EPS)
    return y.reshape(h.shape[0], h.shape[1], -1) * w.astype(jnp.float32)

def second_inputs(seed: int = 0) -> dict:
    key = jax.random.key(seed)
    ks = jax.random.split(key, 24)
    f32 = jnp.float32

    def dense(k, shape, fan_in, scale=1.0):
        return jax.random.normal(k, shape, f32) * (scale * fan_in ** -0.5)

    def gain(k, width):
        return 1.0 + 0.05 * jax.random.normal(k, (DEPTH, width), f32)

    x = jax.random.normal(ks[0], (BATCH, SEQ, D_MODEL), f32)
    c = jax.random.normal(ks[1], (BATCH, D_MODEL), f32)
    offsets = jax.random.randint(ks[2], (BATCH, 1), 0, 4096, dtype=jnp.int32)
    positions = (offsets + jnp.arange(SEQ, dtype=jnp.int32)[None, :]).astype(jnp.int32)
    w_ada = dense(ks[3], (DEPTH, D_MODEL, 6 * D_MODEL), D_MODEL, 0.5)
    b_ada = 0.02 * jax.random.normal(ks[4], (DEPTH, 6 * D_MODEL), f32)
    g_pre_mix = gain(ks[5], D_MODEL)
    g_post_mix = gain(ks[6], D_MODEL)
    w_in = dense(ks[7], (DEPTH, D_MODEL, IN_WIDTH), D_MODEL)
    b_i = 0.1 * jax.random.normal(ks[8], (DEPTH, MLSTM_HEADS), f32)
    b_f = jnp.linspace(3.0, 6.0, MLSTM_HEADS, dtype=f32)[None, :] + \
        0.1 * jax.random.normal(ks[9], (DEPTH, MLSTM_HEADS), f32)
    b_if = jnp.concatenate([b_i, b_f], axis=-1)
    conv_w = dense(ks[10], (DEPTH, CONV_WIDTH_2, 2 * MLSTM_WIDTH), CONV_WIDTH_2)
    conv_b = 0.02 * jax.random.normal(ks[11], (DEPTH, 2 * MLSTM_WIDTH), f32)
    attn_sinks = 0.5 * jax.random.normal(ks[12], (DEPTH, N_Q_HEADS), f32)
    mlstm_norm_w = gain(ks[13], MLSTM_WIDTH)
    w_branch_attn = dense(ks[14], (DEPTH, ATTN_Q_WIDTH, D_MODEL), ATTN_Q_WIDTH)
    w_branch_mlstm = dense(ks[15], (DEPTH, MLSTM_WIDTH, D_MODEL), MLSTM_WIDTH)
    w_out = dense(ks[16], (DEPTH, D_MODEL, D_MODEL), D_MODEL)
    g_pre_ffn = gain(ks[17], D_MODEL)
    g_post_ffn = gain(ks[18], D_MODEL)
    w_ffn_gate = dense(ks[19], (DEPTH, D_MODEL, D_FF_2), D_MODEL)
    w_ffn_up = dense(ks[20], (DEPTH, D_MODEL, D_FF_2), D_MODEL)
    w_ffn_down = dense(ks[21], (DEPTH, D_FF_2, D_MODEL), D_FF_2)
    return {'x': x, 'c': c, 'positions': positions, 'w_ada': w_ada, 'b_ada': b_ada,
            'g_pre_mix': g_pre_mix, 'g_post_mix': g_post_mix, 'w_in': w_in, 'b_if': b_if,
            'conv_w': conv_w, 'conv_b': conv_b, 'attn_sinks': attn_sinks,
            'mlstm_norm_w': mlstm_norm_w, 'w_branch_attn': w_branch_attn,
            'w_branch_mlstm': w_branch_mlstm, 'w_out': w_out, 'g_pre_ffn': g_pre_ffn,
            'g_post_ffn': g_post_ffn, 'w_ffn_gate': w_ffn_gate, 'w_ffn_up': w_ffn_up,
            'w_ffn_down': w_ffn_down}

def second_block(x, c, positions, w_ada, b_ada, g_pre_mix, g_post_mix, w_in, b_if, conv_w, conv_b,
              attn_sinks, mlstm_norm_w, w_branch_attn, w_branch_mlstm, w_out, g_pre_ffn,
              g_post_ffn, w_ffn_gate, w_ffn_up, w_ffn_down):
    B, S, _ = x.shape
    split_points = np.cumsum(IN_SPLIT_SIZES)[:-1].tolist()
    for l in range(DEPTH):
        mod = c @ w_ada[l] + b_ada[l]
        shift_m, scale_m, gate_m, shift_f, scale_f, gate_f = jnp.split(mod, 6, axis=-1)

        h = modulate(rms_norm(x, g_pre_mix[l]), shift_m, scale_m)
        proj = h @ w_in[l]
        q_a, k_a, v_a, q_m, k_m, v_m, o_m, i_m, f_m, g_a, g_m = jnp.split(proj, split_points, axis=-1)

        q_a = rope(q_a.reshape(B, S, N_Q_HEADS, HEAD_DIM), positions)
        k_a = rope(k_a.reshape(B, S, N_KV_HEADS, HEAD_DIM), positions)
        v_a = v_a.reshape(B, S, N_KV_HEADS, HEAD_DIM)
        y_a = sliding_window_attention(q_a, k_a, v_a, attn_sinks[l]).astype(x.dtype)

        qk_m = jax.nn.silu(causal_depthwise_conv(jnp.concatenate([q_m, k_m], axis=-1), conv_w[l], conv_b[l]))
        q_m, k_m = jnp.split(qk_m, 2, axis=-1)
        i_pre = i_m + b_if[l][:MLSTM_HEADS]
        f_pre = f_m + b_if[l][MLSTM_HEADS:]
        h_m = mlstm_chunkwise(q_m.reshape(B, S, MLSTM_HEADS, MLSTM_HEAD_DIM),
                              k_m.reshape(B, S, MLSTM_HEADS, MLSTM_HEAD_DIM),
                              v_m.reshape(B, S, MLSTM_HEADS, MLSTM_HEAD_DIM), i_pre, f_pre)
        y_m = (jax.nn.sigmoid(o_m.astype(jnp.float32)) * head_layer_norm(h_m, mlstm_norm_w[l])).astype(x.dtype)

        merged = jax.nn.sigmoid(g_a) * (y_a @ w_branch_attn[l]) + jax.nn.sigmoid(g_m) * (y_m @ w_branch_mlstm[l])
        mix = merged @ w_out[l]
        x = x + gate_m[:, None, :] * rms_norm(mix, g_post_mix[l])

        h2 = modulate(rms_norm(x, g_pre_ffn[l]), shift_f, scale_f)
        ff = (jax.nn.silu(h2 @ w_ffn_gate[l]) * (h2 @ w_ffn_up[l])) @ w_ffn_down[l]
        x = x + gate_f[:, None, :] * rms_norm(ff, g_post_ffn[l])
    return x


def setup_inputs(seed=0):
    out = dict(first_inputs(seed))
    for name, value in second_inputs(seed + 1).items():
        if name != "x":
            out[name + "_2"] = value
    return out


def reference(
    x, attn_pre_norm, w_qkv, lambda_q1, lambda_k1, lambda_q2, lambda_k2, diff_subln, sb_norm,
    rel_bias, w_o, attn_post_norm, ffn_pre_norm, w_up, conv_w, conv_b, w_down, ffn_post_norm,
    c_2, positions_2, w_ada_2, b_ada_2, g_pre_mix_2, g_post_mix_2, w_in_2, b_if_2, conv_w_2,
    conv_b_2, attn_sinks_2, mlstm_norm_w_2, w_branch_attn_2, w_branch_mlstm_2, w_out_2,
    g_pre_ffn_2, g_post_ffn_2, w_ffn_gate_2, w_ffn_up_2, w_ffn_down_2,
):
    x = first_block(
        x, attn_pre_norm, w_qkv, lambda_q1, lambda_k1, lambda_q2, lambda_k2, diff_subln,
        sb_norm, rel_bias, w_o, attn_post_norm, ffn_pre_norm, w_up, conv_w, conv_b, w_down,
        ffn_post_norm,
    )
    return second_block(
        x, c_2, positions_2, w_ada_2, b_ada_2, g_pre_mix_2, g_post_mix_2, w_in_2, b_if_2,
        conv_w_2, conv_b_2, attn_sinks_2, mlstm_norm_w_2, w_branch_attn_2, w_branch_mlstm_2,
        w_out_2, g_pre_ffn_2, g_post_ffn_2, w_ffn_gate_2, w_ffn_up_2, w_ffn_down_2,
    )


_drawn_inputs = setup_inputs


def setup_inputs(seed=0):
    import zlib

    import numpy as np

    out = dict(_drawn_inputs(seed))
    spreads = {}
    factors = {'lambda_q1': 3.807,
     'lambda_k1': 2.765,
     'lambda_q2': 36.486,
     'conv_b': 6.666,
     'b_ada_2': 2.702,
     'g_pre_mix_2': 3.89,
     'g_post_mix_2': 4.034,
     'conv_b_2': 64.0,
     'attn_sinks_2': 60.403,
     'mlstm_norm_w_2': 5.517,
     'g_pre_ffn_2': 3.221,
     'g_post_ffn_2': 4.134}
    for name, (base, spread) in spreads.items():
        noise = np.random.default_rng([zlib.crc32(name.encode()), seed]).standard_normal(out[name].shape)
        drawn = base * np.exp(spread * noise) if base else spread * noise
        out[name] = __import__('jax').numpy.asarray(drawn.astype(out[name].dtype))
    for name, factor in factors.items():
        out[name] = (out[name] * factor).astype(out[name].dtype)
    return out
```

```python
import math
from contextlib import ExitStack
from collections import namedtuple

import numpy as np

import concourse.bass as bass
from concourse import mybir

F32 = mybir.dt.float32
F32R = mybir.dt.float32r
I32 = mybir.dt.int32
ALU = mybir.AluOpType
ACT = mybir.ActivationFunctionType
AX = mybir.AxisListType.X

P = 128
S = 1024
D = 1024
HALF = 512
KT = D // P
NB = S // P
DFF = 2816
NJ = DFF // P
EPS = 1e-6
NEG = -1e30
SP_CAP = 30.0
LAM_INIT = 0.8 - 0.6 * math.exp(0.0)
DH = 64
HD_DIFF = 4
HD_SB = 8
HD_ML = 4
ML_D = 128

NormBuffers = namedtuple("NormBuffers", "sq rstd tmp")
Arrays = namedtuple("Arrays", "x w cols mats onehot table table31 w_ada positions out")

N_QKV, N_MIX, N_FFN, N_IN = 24, 8, 3 * NJ, 39
C_QKV = 0
C_WO = C_QKV + N_QKV
C_FFN1 = C_WO + N_MIX
C_IN = C_FFN1 + N_FFN
C_BR = C_IN + N_IN
C_OUT = C_BR + N_MIX
C_FFN2 = C_OUT + N_MIX
N_CHUNKS = C_FFN2 + N_FFN
RAW = 2
SL = 3

COLS, _at = {}, 0
for _name, _n in (
    ("attn_pre", KT), ("attn_post", KT), ("ffn_pre", KT), ("ffn_post", KT), ("subln", 1), ("sbnorm", 1),
    ("conv1", NJ * 8), ("b_ada", 48), ("c", KT), ("lq", 2), ("lk", 2), ("pre_mix", KT), ("post_mix", KT),
    ("pre_ffn", KT), ("post_ffn", KT), ("mconv", 8 * 5), ("mnorm", 4), ("b_if", 1), ("sinks", 8),
    ("eps", 1), ("invf", 1), ("sgn", 1),
):
    COLS[_name] = (_at, _n)
    _at += _n
N_COLS = _at
MATS, _at = {}, 0
for _name, _n in (("ident", P), ("mean", P), ("negtri", P), ("negones", P), ("mean64", P),
                  ("strict", P), ("negstrict", P), ("negcausal", P), ("band", 2 * P)):
    MATS[_name] = (_at, _n)
    _at += _n
N_MATS = _at
ONEHOT_W = 384


def host_matrices():
    i = np.arange(P)
    q, k = i[:, None], i[None, :]
    m = np.zeros((P, N_MATS), np.float32)

    def put(name, value):
        o, n = MATS[name]
        m[:, o:o + n] = value

    put("ident", np.eye(P))
    put("mean", 1.0 / D)
    put("negtri", -(q >= k).astype(np.float32))
    put("negones", -1.0)
    put("mean64", (q // DH == k // DH) / float(DH))
    put("strict", (q < k))
    put("negstrict", np.where(q < k, 0.0, NEG))
    put("negcausal", np.where(q <= k, 0.0, NEG))
    j = np.arange(2 * P)[None, :] - P
    put("band", np.where((j <= q) & (q - j < P), 0.0, NEG))
    rel = 255 - np.arange(ONEHOT_W)
    n = np.maximum(rel, 0)
    large = 16 + (np.log(np.maximum(n, 1).astype(np.float32) / np.float32(16))
                  / np.float32(math.log(8.0)) * np.float32(16)).astype(np.int32)
    bucket = np.where(n < 16, n, np.minimum(large, 31))
    bucket = np.where(rel < 0, 32, bucket)
    onehot = (np.arange(33)[:, None] == bucket[None, :]).astype(np.float32)
    return m, onehot


def build(nc, A):
    ctx = ExitStack()
    with ctx:
        at = [-(-nc.sbuf_base // 32) * 32]

        def place(name, shape, dt=F32, offset=None):
            if offset is None:
                offset = at[0]
                at[0] += -(-4 * int(np.prod(shape[1:])) // 32) * 32
            return nc.alloc_sbuf_tensor_at(name, shape, dt, offset=offset, align_bytes=32)

        raw = place("raw", [P, RAW, 1024])
        wh = place("wh", [P, SL, 1024], F32R)
        wl = place("wl", [P, SL, 1024], F32R)
        HH_AT = at[0]
        hh = place("hh", [P, KT, S], F32R)
        hl = place("hl", [P, KT, S], F32R)
        hhf = place("hhf", [P, KT, S], F32, HH_AT)
        hlf = place("hlf", [P, KT, S], F32, HH_AT + 4 * KT * S)
        hh_read = hh[:].bitcast(F32)
        ARENA = 26 * S + 64
        ARENA_AT = at[0]
        arena = place("arena", [P, ARENA])
        ah = place("ah", [P, KT, S], F32R, ARENA_AT)
        al = place("al", [P, KT, S], F32R, ARENA_AT + 4 * KT * S)
        gated = place("gated", [P, 2, 2, S], F32R, ARENA_AT + 4 * 16 * S)
        cols = place("cols", [P, N_COLS])
        mats = place("mats", [P, N_MATS])
        modc = place("modc", [P, 48])
        foldc = place("foldc", [P, 32])
        small = place("small", [P, P])
        dsm = place("dsm", [P, 64])
        ps = ctx.enter_context(nc.psum_tensor("ps", [P, 8 * HALF], F32))

        def T(n, k=1):
            return arena[:, n * S:(n + k) * S]

        def col(name, i=0, n=1):
            o, _ = COLS[name]
            return cols[:, o + i:o + i + n]

        def mat(name):
            o, n = MATS[name]
            return mats[:, o:o + n]

        def bank(b, n=1):
            return ps[:, b * HALF:(b + n) * HALF]


        names = """
        raw0 raw1 wt_hi split_done chunk_done pool_pace act_pace
        consts x_in tab table2 tabx tb_ready e_ps e_sb e_out bias_in
        mod_in0 mod_in1 mod_in2 mod_in3 mod_acc mod_ps mod_col fold lam_p lam_ps lam_e lam_v
        n_sq n_ss n_ln n_rstd n_t n_hi n_lo f_sq f_ss f_ln f_rstd f_y f_x
        q_ev vt_ev vT v_cp
        d_qk d_near d_max d_nmx d_exp d_r d_w d_T d_wt d_pv d_post d_ln d_rs d_on d_hT d_hi d_lo
        s_z s_capped s_e s_L s_m s_mk s_zero s_cy s_c s_a s_pv s_o s_sq s_ss s_ln s_rs s_t s_hi s_lo
        y_cp x_re
        g_lin g_act v_lin g_cv v_cv f_prod a_hi a_lo dn_done dn_free y_zero
        pos_in trig trig_sin spill if_ev if_ch if_act rope_raw rope_sw0 rope_sw1 rope_t rope_done cv_lin cv_t cv_done sg_ev sg_out0 sg_out1
        m_sel m_mb m_mbc m_tp m_tpc m_S m_d m_E m_A m_pv m_U l_ch l_act l_T l_t l_hi l_lo so_in
        w_qk w_a w_nm w_exp w_b w_pn w_T w_pt w_pv w_hi w_lo
        gate0 gate1 b_a b_m b_s b_hi b_lo x2_in out_d
        """.split()
        Z = namedtuple("Semaphores", names)(*[ctx.enter_context(nc.semaphore(n)) for n in names])

        e_dram = nc.dram_tensor("e_scratch", (HD_DIFF, P, ONEHOT_W), F32, kind="Internal").ap()
        x2_dram = nc.dram_tensor("x2_scratch", (P, KT * S), F32, kind="Internal").ap()
        sg_dram = nc.dram_tensor("gate_scratch", (20, P, S), F32, kind="Internal").ap()

        block = ctx.enter_context(nc.Block())

        X1 = T(8, 8)
        Y1 = T(0, 8)
        NRM1 = NormBuffers(sq=[T(16), T(17)], rstd=T(18), tmp=[T(19), T(20)])
        HL_TMP = NormBuffers(sq=[hlf[:, 0], hlf[:, 1]], rstd=hlf[:, 2], tmp=[hlf[:, 3], hlf[:, 4]])
        SPLIT_H = ([hh[:, f] for f in range(KT)], [hl[:, f] for f in range(KT)])
        SPLIT_A = ([ah[:, f] for f in range(KT)], [al[:, f] for f in range(KT)])
        V1 = T(16, 8).rearrange("p (b n) -> p b n", b=NB)
        VT1 = T(24)
        MOD_ACC = [T(20), T(21), T(25), T(24)]
        V2_AT, V2_W = 13 * S, P + HD_ML * (ML_D + 1)
        V2 = arena[:, V2_AT:V2_AT + NB * V2_W].rearrange("p (b n) -> p b n", b=NB)
        R4 = V2_AT + NB * V2_W
        COS, SIN = arena[:, R4:R4 + S], arena[:, R4 + S:R4 + 2 * S]
        RING = [[arena[:, R4 + (2 + 2 * r + i) * S:R4 + (3 + 2 * r + i) * S] for i in range(2)] for r in range(2)]
        ROW1, ROW2 = arena[:, R4 + 6 * S:R4 + 7 * S], arena[:, R4 + 7 * S:R4 + 8 * S]
        NEGMB = arena[:, R4:R4 + 4 * S].rearrange("p (h t) -> p h t", h=HD_ML)
        U_AT = R4 + 4 * S
        U = arena[:, U_AT:U_AT + 32 * 129].rearrange("p (i n) -> p i n", n=129)
        GT, EMT = small[:, 0:32], small[:, 32:64]
        D_PAIRS = [(h, b) for h in range(HD_DIFF) for b in range(NB)]
        D_P0, D_P1 = [hhf[:, 4], hhf[:, 5], hhf[:, 6]], [hhf[:, 7], hlf[:, 4]]
        D_WT = [hlf[:, 5], hlf[:, 6]]
        D_O, D_ON = T(24), hlf[:, 7]
        D_BIAS, D_JUNK = T(25), small[:, 0:P]
        D_MAX, D_NEG = dsm[:, 0:4], dsm[:, 4:8]
        D_SUM, D_REC = dsm[:, 8:16], dsm[:, 16:24]
        D_MIX = dsm[:, 24:28]
        D_SS, D_LN, D_RS = dsm[:, 32:40], dsm[:, 40:48], dsm[:, 48:56]
        D_BANKS = [(v % 4, 1) if D_PAIRS[v // 2][1] < 4 else (2 * (v % 2), 2) for v in range(2 * len(D_PAIRS))]
        D_BEFORE = [max([u + 1 for u in range(v) if max(D_BANKS[u][0], D_BANKS[v][0])
                         < min(sum(D_BANKS[u]), sum(D_BANKS[v]))], default=0) for v in range(len(D_BANKS))]
        D_STEPS = len(D_PAIRS) + 4

        def d_head_end(s):
            return (s - 11) // NB if s >= 11 and (s - 11) % NB == 0 else None

        SB_UNITS = [(hd, c, k, max(0, (k - 4 * c) * P)) for hd in range(HD_SB) for c in range(2)
                    for k in range(4 * c + 3, -1, -1)]
        SB_CHAIN = [2 * hd + c for hd, c, k, lo in SB_UNITS]
        SB_DIAG = np.cumsum([0] + [k >= 4 * c for hd, c, k, lo in SB_UNITS]).tolist()
        SB_CHAIN_END = [max(u for u, (hd, c, k, lo) in enumerate(SB_UNITS) if 2 * (hd // 2) + c == n) for n in range(8)]
        halves = lambda n: [T(n)[:, 0:HALF], T(n)[:, HALF:S]]
        S_SP, S_M, S_CY, S_A = halves(0), halves(1), halves(2), halves(3)
        S_O = T(8, 4).rearrange("p (j t) -> p j t", j=4)
        S_SQ, S_RS, S_T = [T(12), T(13)], [T(14), T(15)], [T(4), T(5)]
        GATED = [(gated[:, b, 0], gated[:, b, 1]) for b in range(2)]
        CG, CV = [T(20), T(21)], [T(22), T(23)]
        NRM2 = NRM1
        ML_SUBS = [(2 * h + c, h, c, k, max(0, (k - 4 * c) * P)) for h in range(HD_ML) for c in range(2)
                   for k in range(4 * c + 4)]
        ML_LAST = [max(s for s, x in enumerate(ML_SUBS) if x[0] == w) for w in range(8)]
        ML_DIAG_OF = [s for s, (w, h, c, k, lo) in enumerate(ML_SUBS) if k >= 4 * c]
        ML_DIAG = {s: i for i, s in enumerate(ML_DIAG_OF)}
        ML_E = np.cumsum([1 + (k >= 4 * c and lo + P < HALF) for w, h, c, k, lo in ML_SUBS]).tolist()
        M_SEL = hhf[:, 7, 0:HALF]
        M_E = [hhf[:, 4, 0:HALF], hhf[:, 4, HALF:S]]
        M_D = [hhf[:, 5, 0:P], hhf[:, 5, P:2 * P]]
        M_A = [t[:, 0:4].rearrange("p f t -> p (f t)").rearrange("p (k t) -> p k t", k=NB) for t in (hhf, hlf)]
        L_SQ = hlf[:, 4:8].rearrange("p f t -> p (f t)").rearrange("p (i n) -> p i n", n=P)
        L_T = [hhf[:, 0], hhf[:, 1]]
        LN_LAST = 9
        W_P, W_PT = [T(5), T(6)], [T(7), T(8)]
        W_SM = [small[:, 0:20], small[:, 20:40]]
        B_G = [[arena[:, R4 + (2 * r + i) * S:R4 + (2 * r + i + 1) * S] for i in range(2)] for r in range(2)]
        B_T = [[arena[:, U_AT + (2 * r + i) * S:U_AT + (2 * r + i + 1) * S] for i in range(2)] for r in range(2)]

        def ffn_gate(c0, j):
            return c0 + 3 * j - 1

        def ffn_down_last(c0):
            return c0 + 3 * NJ - 1


        @block.sync
        def _(sp):
            for c in range(RAW):
                sp.dma_start(raw[:, c], A.w[c]).then_inc((Z.raw0, Z.raw1)[c], 16)

            def load(c, s, n):
                sp.wait_ge(Z.split_done, n)
                sp.dma_start(raw[:, s], A.w[bass.ds(c, 1)].rearrange("a p n -> p (a n)")).then_inc(
                    (Z.raw0, Z.raw1)[s], 16)

            loops = (N_CHUNKS - RAW) // RAW
            with sp.Fori(0, loops) as i:
                for s in range(RAW):
                    load(i * RAW + (RAW + s), s, i * RAW + (s + 1))
            for c in range(RAW + loops * RAW, N_CHUNKS):
                sp.wait_ge(Z.split_done, c - RAW + 1)
                sp.dma_start(raw[:, c % RAW], A.w[c]).then_inc((Z.raw0, Z.raw1)[c % RAW], 16)

        @block.gpsimd
        def _(pool):
            def split(r, s, loaded, n):
                pool.wait_ge((Z.raw0, Z.raw1)[r], loaded)
                pool.sem_inc(Z.pool_pace, 1)
                pool.tensor_copy(wh[:, s], raw[:, r]).then_inc(Z.wt_hi, 1)
                pool.wait_ge(Z.wt_hi, n + 1)
                pool.tensor_tensor(wl[:, s], raw[:, r], wh[:, s].bitcast(F32), ALU.subtract).then_inc(Z.split_done, 1)

            for c in range(SL):
                split(c % RAW, c % SL, 16 * (c // RAW + 1), c)
            UN = RAW * SL
            loops = (N_CHUNKS - SL) // UN
            with pool.Fori(0, loops) as i:
                for u in range(UN):
                    c = SL + u
                    pool.wait_ge(Z.chunk_done, i * UN + (u + 1))
                    split(c % RAW, c % SL, i * (16 * SL) + 16 * (c // RAW + 1), i * UN + c)
            for c in range(SL + loops * UN, N_CHUNKS):
                pool.wait_ge(Z.chunk_done, c - SL + 1)
                split(c % RAW, c % SL, 16 * (c // RAW + 1), c)

        @block.tensor
        def _(pe):
            def product(out, slot, k, xh, xl, start, stop):
                w = slice(k * P, (k + 1) * P)
                pe.matmul(out, wh[:, slot, w], xh, start=start, stop=False)
                pe.matmul(out, wh[:, slot, w], xl, start=False, stop=False)
                return pe.matmul(out, wl[:, slot, w], xh, start=False, stop=stop)

            def tile(slot, b, x):
                for half in range(2):
                    t = slice(half * HALF, (half + 1) * HALF)
                    for k in range(KT):
                        last = product(bank(b + half), slot, k, x[0][k][:, t], x[1][k][:, t], k == 0, k == KT - 1)
                last.then_inc(Z.chunk_done, 1)

            def mean_of_squares(sq_sem, ss_sem, sq, f, n, out=6):
                pe.wait_ge(sq_sem, n + 1)
                for half in range(2):
                    last = pe.matmul(bank(out + half), mat("mean"), sq[f % 2][:, half * HALF:(half + 1) * HALF],
                                     start=(f == 0), stop=(f == KT - 1))
                last.then_inc(ss_sem, 1)

            def norm(use, nrm):
                for f in range(KT):
                    mean_of_squares(Z.n_sq, Z.n_ss, nrm.sq, f, 8 * use + f)

            def post(use, nrm):
                for f in range(KT):
                    mean_of_squares(Z.f_sq, Z.f_ss, nrm.sq, f, 8 * use + f)

            pe.wait_ge(Z.consts, 48)
            pe.wait_ge(Z.lam_p, 1)
            pe.matmul(bank(4)[:, 0:2], mat("mean"), small[:, 64:66], start=True, stop=True).then_inc(Z.lam_ps, 1)
            norm(0, NRM1)

            pe.wait_ge(Z.n_lo, 8)
            for n in range(3):
                pe.wait_ge(Z.split_done, C_QKV + n + 1)
                if n == 2:
                    pe.wait_ge(Z.lam_e, 1)
                tile((C_QKV + n) % SL, 2 * n, SPLIT_H)

            def qkv_loop(first):
                with pe.Fori(0, 2) as i:
                    for u in range(3):
                        n = first + u
                        pe.wait_ge(Z.split_done, i * 3 + (C_QKV + n + 1))
                        pe.wait_ge(Z.q_ev, i * 3 + (n - 2))
                        tile((C_QKV + n) % SL, 2 * (n % 3), SPLIT_H)

            def modulation(g):
                pe.wait_ge(Z.mod_acc, 8 * (g + 1))
                for f in range(8):
                    last = pe.matmul(bank(7)[:, g * 8 + f:g * 8 + f + 1], MOD_ACC[g % 4][:, f * P:(f + 1) * P],
                                     mat("mean")[:, 0:1], start=True, stop=True)
                last.then_inc(Z.mod_ps, 1)

            qkv_loop(3)
            pe.wait_ge(Z.n_ln, 1)
            modulation(0)
            modulation(1)
            qkv_loop(9)
            for h in range(HD_DIFF):
                pe.wait_ge(Z.tb_ready, h + 1)
                if h:
                    pe.wait_ge(Z.e_sb, h)
                pe.matmul(bank(6)[:, 0:ONEHOT_W], T(22)[0:33, h * P:(h + 1) * P], T(23)[0:33, 0:ONEHOT_W],
                          start=True, stop=True).then_inc(Z.e_ps, 1)
            for g in range(2, 6):
                modulation(g)
            pe.wait_ge(Z.mod_col, 1)
            pe.wait_ge(Z.e_sb, 4)

            def v_transposes(n, vt, sem_ev, sem_T, sem_cp):
                for half in range(2):
                    pe.wait_ge(sem_ev, 2 * n + half + 1)
                    if n:
                        pe.wait_ge(sem_cp, 2 * n + half - 1)
                    for b in range(4):
                        t = slice(half * HALF + b * P, half * HALF + (b + 1) * P)
                        last = pe.transpose(bank(6 + half)[:, b * P:(b + 1) * P], vt[:, t], mat("ident"))
                    last.then_inc(sem_T, 1)

            for n in range(15, N_QKV):
                pe.wait_ge(Z.split_done, C_QKV + n + 1)
                if n <= 18:
                    pe.wait_ge(Z.q_ev, n - 2)
                else:
                    pe.wait_ge(Z.vt_ev, 2 * (n - 18))
                tile((C_QKV + n) % SL, 2 * (n % 3), SPLIT_H)
                if n > 16:
                    v_transposes(n - 17, VT1, Z.vt_ev, Z.vT, Z.v_cp)
            v_transposes(7, VT1, Z.vt_ev, Z.vT, Z.v_cp)

            pe.wait_ge(Z.vt_ev, 16)
            pe.wait_ge(Z.v_cp, 16)

            def d_scores(p, m):
                h, b = D_PAIRS[p]
                v = 2 * p + m
                if D_BEFORE[v]:
                    pe.wait_ge(Z.d_exp, D_BEFORE[v])
                w = (b + 1) * P
                r = slice(DH * m, DH * (m + 1))
                for c in range(0, w, HALF):
                    e = min(w, c + HALF)
                    last = pe.matmul(bank(*D_BANKS[v])[:, c:e], T(h)[r, b * P:(b + 1) * P], T(8 + h)[r, c:e],
                                     start=True, stop=True)
                last.then_inc(Z.d_qk, 1)

            def d_transposes(p):
                h, b = D_PAIRS[p]
                pe.wait_ge(Z.d_w, p + 1)
                if p:
                    pe.wait_ge(Z.d_wt, p)
                if d_head_end(p + 1) is not None:
                    pe.wait_ge(Z.d_lo, d_head_end(p + 1) + 1)
                for k in range(b + 1):
                    last = pe.transpose(bank(4, 2)[:, k * P:(k + 1) * P], D_P0[p % 3][:, k * P:(k + 1) * P], mat("ident"))
                last.then_inc(Z.d_T, 1)

            def d_values(p):
                h, b = D_PAIRS[p]
                pe.wait_ge(Z.d_wt, p + 1)
                if p >= 2:
                    pe.wait_ge(Z.d_post, p - 1)
                for k in range(b + 1):
                    last = pe.matmul(bank(6 + p % 2)[:, 0:P], D_WT[p % 2][:, k * P:(k + 1) * P],
                                     V1[:, k, h * P:(h + 1) * P], start=(k == 0), stop=(k == b))
                last.then_inc(Z.d_pv, 1)

            def d_out_transposes(h):
                pe.wait_ge(Z.d_on, h + 1)
                pe.wait_ge(Z.d_wt, min(len(D_PAIRS), NB * h + 10))
                for b in range(NB):
                    last = pe.transpose(bank(4, 2)[:, b * P:(b + 1) * P], D_ON[:, b * P:(b + 1) * P], mat("ident"))
                last.then_inc(Z.d_hT, 1)

            for s in range(D_STEPS):
                if s < len(D_PAIRS):
                    d_scores(s, 0)
                    d_scores(s, 1)
                if 0 <= s - 2 < len(D_PAIRS):
                    d_transposes(s - 2)
                if 0 <= s - 3 < len(D_PAIRS):
                    d_values(s - 3)
                if d_head_end(s) is not None:
                    d_out_transposes(d_head_end(s))

            pe.wait_ge(Z.d_exp, 64)
            pe.wait_ge(Z.d_lo, 4)
            pe.wait_ge(Z.d_post, 32)

            def s_scores(u):
                hd, c, k, lo = SB_UNITS[u]
                if u >= 4:
                    pe.wait_ge(Z.s_a, u - 3)
                r = slice(DH * (hd % 2), DH * (hd % 2) + DH)
                pe.matmul(bank(u % 4)[:, lo:], T(12 + hd // 2)[r, k * P:(k + 1) * P],
                          T(4 + hd // 2)[r, c * HALF + lo:(c + 1) * HALF],
                          start=True, stop=False, skip_group_check=True).then_inc(Z.s_z, 1)

            def s_sums(u):
                hd, c, k, lo = SB_UNITS[u]
                z = bank(u % 4)
                diag, first = k >= 4 * c, k == 4 * c + 3
                pe.wait_ge(Z.s_m, u + 1)
                pe.matmul(z[:, lo:], mat("negtri"), S_M[u % 2][:, lo:], start=False, stop=False, skip_group_check=True)
                if not first:
                    pe.wait_ge(Z.s_cy, u)
                    last = pe.matmul(z[:, lo:], mat("negones"), S_CY[u % 2][:, lo:], start=False, stop=not diag,
                                     skip_group_check=True)
                if diag:
                    last = pe.matmul(z[:, lo:lo + P], mat("ident"), mat("negstrict"), start=False, stop=True,
                                     skip_group_check=True)
                last.then_inc(Z.s_c, 1)

            def s_values(u):
                hd, c, k, lo = SB_UNITS[u]
                pe.wait_ge(Z.s_a, u + 1)
                chain = 2 * (hd // 2) + c
                r = DH * (hd % 2)
                first = k == 4 * c + 3
                if first and chain >= 4:
                    pe.wait_ge(Z.s_o, chain - 3)
                pe.matmul(bank(4 + chain % 4)[r:r + DH, lo:], V1[:, k, HD_DIFF * P + hd * DH:HD_DIFF * P + (hd + 1) * DH],
                          S_A[u % 2][:, lo:], start=first, stop=(k == 0), skip_group_check=True).then_inc(Z.s_pv, 1)

            for u in range(len(SB_UNITS) + 3):
                if u < len(SB_UNITS):
                    s_scores(u)
                if 0 <= u - 2 < len(SB_UNITS):
                    s_sums(u - 2)
                if 0 <= u - 3:
                    s_values(u - 3)
            for j in range(4):
                pe.wait_ge(Z.s_sq, j + 1)
                if j == 0:
                    pe.wait_ge(Z.s_a, len(SB_UNITS))
                if j >= 2:
                    pe.wait_ge(Z.s_ln, j - 1)
                for half in range(2):
                    last = pe.matmul(bank(2 * (j % 2) + half), mat("mean64"),
                                     S_SQ[j % 2][:, half * HALF:(half + 1) * HALF], start=True, stop=True)
                last.then_inc(Z.s_ss, 1)

            pe.wait_ge(Z.s_lo, 4)
            pe.wait_ge(Z.s_ln, 4)
            pe.wait_ge(Z.s_o, 8)
            pe.wait_ge(Z.d_lo, 4)

            def eight_tiles(c0, use, x, nrm):
                for f in range(KT):
                    pe.wait_ge(Z.split_done, c0 + f + 1)
                    if f >= 3:
                        pe.wait_ge(Z.y_cp, 8 * (use // 2) + f - 2)
                    tile((c0 + f) % SL, 2 * (f % 3), x)
                    if f:
                        mean_of_squares(Z.f_sq, Z.f_ss, nrm.sq, f - 1, 8 * use + f - 1)
                mean_of_squares(Z.f_sq, Z.f_ss, nrm.sq, KT - 1, 8 * use + KT - 1)

            eight_tiles(C_WO, 0, SPLIT_H, NRM1)
            norm(1, NRM1)

            def ffn(c0, use, x, act):
                fb = NJ * use
                gate_free = (Z.g_cv, 2) if use == 0 else (Z.g_lin, 1)
                val_free = (Z.v_cv, 2) if use == 0 else (Z.f_prod, 1)
                gate_base, val_base = (0, 0) if use == 0 else (fb, fb)

                def up(j, c, first=False):
                    pe.wait_ge(Z.split_done, c + 1)
                    if not first:
                        pe.wait_ge(gate_free[0], j * gate_free[1] + gate_base)
                    tile(slot_of[0], 0, x)
                    pe.wait_ge(Z.split_done, c + 2)
                    if not first:
                        pe.wait_ge(val_free[0], j * val_free[1] + val_base)
                    tile(slot_of[1], 2, x)

                def down(j, b, c, slot):
                    pe.wait_ge(Z.split_done, c + 1)
                    pe.wait_ge(Z.a_lo, j + (fb + 1))
                    for o in range(16):
                        f, half = o // 2, o % 2
                        pe.wait_ge(Z.dn_free, j * 16 + (16 * fb + o + 1))
                        t = slice(half * HALF, (half + 1) * HALF)
                        last = product(bank(4 + o % 4), slot, f, act[b][0][:, t], act[b][1][:, t], True, True)
                        last.then_inc(Z.dn_done if o < 15 else Z.chunk_done, 1)

                slot_of = [c0 % SL, (c0 + 1) % SL]
                up(0, c0, first=True)
                slot_of = [(c0 + 2) % SL, (c0 + 3) % SL]
                down_slot = (c0 + 4) % SL
                with pe.Fori(0, (NJ - 2) // 2) as i:
                    for u in range(2):
                        j = i * 2 + (1 + u)
                        c = i * 6 + (c0 + 2 + 3 * u)
                        up(j, c)
                        down(i * 2 + u, u, c + 2, down_slot)
                up(NJ - 1, ffn_gate(c0, NJ - 1))
                down(NJ - 2, 0, ffn_gate(c0, NJ - 1) + 2, down_slot)
                down(NJ - 1, 1, ffn_down_last(c0), ffn_down_last(c0) % SL)

            pe.wait_ge(Z.n_lo, 16)
            pe.wait_ge(Z.n_ln, 2)
            pe.wait_ge(Z.y_cp, 8)
            ffn(C_FFN1, 0, SPLIT_H, GATED)
            post(1, NRM1)
            norm(2, NRM1)

            pe.wait_ge(Z.n_lo, 24)
            pe.wait_ge(Z.n_ln, 3)
            for n in range(6):
                pe.wait_ge(Z.split_done, C_IN + n + 1)
                if n >= 3:
                    pe.wait_ge(Z.vt_ev, 16 + 2 * (n - 2))
                tile((C_IN + n) % SL, 2 * (n % 3), SPLIT_H)
                if n:
                    v_transposes(8 + n - 1, RING[(n - 1) % 2][0], Z.vt_ev, Z.vT, Z.v_cp)
            with pe.Fori(0, (N_IN - 6) // 3) as i:
                for u in range(3):
                    n = 6 + u
                    pe.wait_ge(Z.split_done, i * 3 + (C_IN + n + 1))
                    pe.wait_ge(Z.if_ev, i * 3 + (n - 2))
                    tile((C_IN + n) % SL, 2 * u, SPLIT_H)

            pe.wait_ge(Z.if_ev, N_IN)
            pe.wait_ge(Z.m_sel, 1)
            pe.wait_ge(Z.if_act, 4)
            for h in range(HD_ML):
                for half in range(2):
                    i = 2 * h + half
                    if i >= 2:
                        pe.wait_ge(Z.m_mbc, i - 1)
                    pe.matmul(bank(i % 2), M_SEL[32:36, h * P:(h + 1) * P], ROW1[32:36, half * HALF:(half + 1) * HALF],
                              start=True, stop=True).then_inc(Z.m_mb, 1)
            for b in range(NB):
                pe.matmul(bank(2)[:, b * 4:b * 4 + 4], ROW1[0:4, b * P:(b + 1) * P], mat("ident")[0:4, 0:4],
                          start=True, stop=True)
                last = pe.matmul(bank(3)[:, b * 4:b * 4 + 4], ROW2[32:36, b * P:(b + 1) * P],
                                 mat("ident")[32:36, 32:36], start=True, stop=True)
            last.then_inc(Z.m_tp, 1)
            pe.wait_ge(Z.m_mbc, 8)
            pe.wait_ge(Z.m_tpc, 2)

            def m_scores(s):
                w, h, c, k, lo = ML_SUBS[s]
                if s >= 4:
                    pe.wait_ge(Z.m_A, s - 3)
                pe.matmul(bank(s % 4)[:, lo:], T(9 + h)[:, k * P:(k + 1) * P], T(5 + h)[:, c * HALF + lo:(c + 1) * HALF],
                          start=True, stop=True).then_inc(Z.m_S, 1)

            def m_values(w):
                h, c = w // 2, w % 2
                pe.wait_ge(Z.m_A, ML_LAST[w] + 1)
                for t in range(4):
                    i = 4 * w + t
                    if i >= 4:
                        pe.wait_ge(Z.m_U, i - 3)
                    for k in range(4 * c + t + 1):
                        last = pe.matmul(bank(4 + t)[:, 0:129], M_A[w % 2][:, k, t * P:(t + 1) * P],
                                         V2[:, k, P + h * 129:P + (h + 1) * 129], start=(k == 0), stop=(k == 4 * c + t))
                    last.then_inc(Z.m_pv, 1)

            for w in range(9):
                if w < 8:
                    for s in range(len(ML_SUBS)):
                        if ML_SUBS[s][0] == w:
                            m_scores(s)
                if w:
                    m_values(w - 1)

            pe.wait_ge(Z.m_A, len(ML_SUBS))
            for h in range(HD_ML):
                pe.wait_ge(Z.l_ch, LN_LAST)
                if h >= 2:
                    pe.wait_ge(Z.l_lo, h - 1)
                for b in range(NB):
                    last = pe.transpose(bank(2 * (h % 2), 2)[:, b * P:(b + 1) * P], U[:, 4 * b + h, 0:P], mat("ident"))
                last.then_inc(Z.l_T, 1)

            pe.wait_ge(Z.l_lo, 4)
            pe.wait_ge(Z.m_U, 32)

            def w_scores(u):
                n, g = u // 2, u % 2
                if u >= 2:
                    pe.wait_ge(Z.w_a, 5 * (u - 2) + 1)
                r = slice(DH * g, DH * (g + 1))
                a = 0 if n else P
                for j in range(4):
                    last = pe.matmul(bank(2 * (u % 2), 2)[:, j * 256 + a:(j + 1) * 256], T(j)[r, n * P:(n + 1) * P],
                                     T(4)[r, (n - 1) * P + a:(n + 1) * P], start=True, stop=True)
                last.then_inc(Z.w_qk, 1)

            def w_transposes(u):
                n = u // 2
                pe.wait_ge(Z.w_pn, u + 1)
                if u:
                    pe.wait_ge(Z.w_pt, u)
                for j in range(4):
                    for k in range(0 if n else 1, 2):
                        i = 2 * j + k
                        last = pe.transpose(bank(4, 2)[:, i * P:(i + 1) * P], W_P[u % 2][:, i * P:(i + 1) * P], mat("ident"))
                last.then_inc(Z.w_T, 1)

            def w_values(u):
                n, g = u // 2, u % 2
                pe.wait_ge(Z.w_pt, u + 1)
                if n >= 2 and g == 0:
                    pe.wait_ge(Z.w_lo, n - 1)
                for j in range(4):
                    for k in range(0 if n else 1, 2):
                        i = 2 * j + k
                        last = pe.matmul(bank(6 + n % 2)[DH * g:DH * (g + 1), j * P:(j + 1) * P],
                                         V2[:, n - 1 + k, DH * g:DH * (g + 1)], W_PT[u % 2][:, i * P:(i + 1) * P],
                                         start=(k == (0 if n else 1)), stop=(k == 1))
                last.then_inc(Z.w_pv, 1)

            for s in range(16 + 2):
                if s < 16:
                    w_scores(s)
                if 0 <= s - 2:
                    w_values(s - 2)
                if 0 <= s - 1 < 16:
                    w_transposes(s - 1)

            pe.wait_ge(Z.w_lo, 8)
            pe.wait_ge(Z.w_pt, 16)
            for f in range(KT):
                pe.wait_ge(Z.split_done, C_BR + f + 1)
                if f >= 2:
                    pe.wait_ge(Z.b_m, f - 1)
                for part in range(2):
                    for half in range(2):
                        t = slice(half * HALF, (half + 1) * HALF)
                        for k in range(4 * part, 4 * part + 4):
                            last = product(bank(4 * (f % 2) + 2 * part + half), (C_BR + f) % SL, k,
                                           hh[:, k, t], hl[:, k, t], k == 4 * part, k == 4 * part + 3)
                last.then_inc(Z.chunk_done, 1)

            pe.wait_ge(Z.b_lo, 8)
            eight_tiles(C_OUT, 2, SPLIT_A, HL_TMP)
            norm(3, HL_TMP)
            pe.wait_ge(Z.n_lo, 32)
            pe.wait_ge(Z.n_ln, 4)
            ffn(C_FFN2, 1, SPLIT_A, GATED)
            post(3, NRM2)

        @block.scalar
        def _(act):
            def square(src, dst, sem):
                act.activation(dst, src, ACT.Square).then_inc(sem, 1)

            def inverse_root(src, dst, ln_sem, sem, n, scale=1.0):
                act.activation(dst, src, ACT.Ln, bias=col("eps"), scale=scale).then_inc(ln_sem, 1)
                act.wait_ge(ln_sem, n + 1)
                act.activation(dst, dst, ACT.Exp, scale=-0.5).then_inc(sem, 1)

            def norm(use, src, ready, nrm, split, shift):
                for f in range(KT):
                    ready(f)
                    if f >= 2:
                        act.wait_ge(Z.n_ss, 8 * use + f - 1)
                    square(src[f], nrm.sq[f % 2], Z.n_sq)
                act.wait_ge(Z.n_ss, 8 * use + 8)
                inverse_root(bank(6, 2), nrm.rstd, Z.n_ln, Z.n_rstd, use)
                for f in range(KT):
                    act.wait_ge(Z.n_t, 8 * use + f + 1)
                    if shift is None:
                        act.activation(split[0][f], nrm.tmp[f % 2], ACT.Copy).then_inc(Z.n_hi, 1)
                    else:
                        act.activation(split[0][f], nrm.tmp[f % 2], ACT.Identity,
                                       bias=modc[:, shift + f:shift + f + 1]).then_inc(Z.n_hi, 1)

            def post(use, y, ready, nrm):
                for f in range(KT):
                    ready(f)
                    if f >= 2:
                        act.wait_ge(Z.f_ss, 8 * use + f - 1)
                    square(y[f], nrm.sq[f % 2], Z.f_sq)
                act.wait_ge(Z.f_ss, 8 * use + 8)
                inverse_root(bank(6, 2), nrm.rstd, Z.f_ln, Z.f_rstd, use)

            act.preload_act_table_set("natural_log_exp_and_others")
            act.dma_start(mats[:], A.mats).then_inc(Z.consts, 16)
            act.dma_start(cols[:], A.cols).then_inc(Z.consts, 16)
            x_tiles = X1.rearrange("p (f t) -> p f t", f=KT)
            act.dma_start(x_tiles, A.x.rearrange("f p t -> p f t")).then_inc(Z.x_in, 16)
            act.dma_start(T(23)[0:33, 0:ONEHOT_W], A.onehot).then_inc(Z.consts, 16)
            act.dma_start(T(23)[0:32, 512:516], A.table).then_inc(Z.tab, 16)
            act.dma_start(T(23)[0:32, 516:520], A.table31).then_inc(Z.tab, 16)
            act.wait_ge(Z.consts, 48)
            act.wait_ge(Z.lam_ps, 1)
            act.activation(small[:, 66:68], bank(4)[:, 0:2], ACT.Exp, scale=float(D)).then_inc(Z.lam_e, 1)
            act.wait_ge(Z.x_in, 16)
            norm(0, [T(8 + f) for f in range(KT)], lambda f: None, NRM1, SPLIT_H, None)

            def mod_load(i):
                g, k = i // 8, i % 8
                if i >= 4:
                    act.wait_ge(Z.mod_acc, i - 3)
                else:
                    act.wait_ge(Z.n_lo, 8)
                act.dma_start(T(16 + i % 4), A.w_ada[k, :, g * 1024:(g + 1) * 1024]).then_inc(
                    (Z.mod_in0, Z.mod_in1, Z.mod_in2, Z.mod_in3)[i % 4], 16)

            for n in range(16):
                for i in range(4 * n, min(48, 4 * n + 4)):
                    mod_load(i)
                act.wait_ge(Z.chunk_done, C_QKV + n + 1)
                if n < 8:
                    act.activation(T(n), bank(2 * (n % 3), 2), ACT.Copy, scale=DH ** -0.5).then_inc(Z.q_ev, 1)
                else:
                    act.activation(T(n), bank(2 * (n % 3), 2), ACT.Copy).then_inc(Z.q_ev, 1)
                if n == 12:
                    for h in range(HD_DIFF):
                        act.wait_ge(Z.e_ps, h + 1)
                        if h >= 1:
                            act.wait_ge(Z.e_out, 16 * h)
                        act.activation(T(23)[:, 520:520 + ONEHOT_W], bank(6)[:, 0:ONEHOT_W], ACT.Copy).then_inc(Z.e_sb, 1)
                        act.wait_ge(Z.e_sb, h + 1)
                        act.dma_start(e_dram[h], T(23)[:, 520:520 + ONEHOT_W]).then_inc(Z.e_out, 16)
            act.wait_ge(Z.mod_ps, 4)
            act.wait_ge(Z.e_out, 64)
            for h in range(HD_DIFF):
                act.dma_start(D_BIAS[:, h * 256:(h + 1) * 256],
                              bass.AP(e_dram.tensor, h * P * ONEHOT_W + 127, [[ONEHOT_W - 1, P], [1, 256]])).then_inc(Z.bias_in, 16)
            for n in range(8):
                act.wait_ge(Z.chunk_done, C_QKV + 16 + n + 1)
                for half in range(2):
                    if n:
                        act.wait_ge(Z.vT, 2 * n + half - 1)
                    t = slice(half * HALF, (half + 1) * HALF)
                    act.activation(VT1[:, t], bank(2 * ((16 + n) % 3) + half), ACT.Copy).then_inc(Z.vt_ev, 1)
            act.wait_ge(Z.chunk_done, C_WO)

            def d_exps(p):
                h, b = D_PAIRS[p]
                w = (b + 1) * P
                for m in range(2):
                    v = 2 * p + m
                    act.wait_ge(Z.d_nmx, v + 1)
                    if m == 0 and p >= 3:
                        act.wait_ge(Z.d_T, p - 2)
                    if m == 1 and p >= 2:
                        act.wait_ge(Z.d_w, p - 1)
                    dst = D_P0[p % 3] if m == 0 else D_P1[p % 2]
                    i, j = 2 * (p % 2) + m, 2 * (p % 4) + m
                    act.activation(dst[:, 0:w], bank(*D_BANKS[v])[:, 0:w], ACT.Exp,
                                   bias=D_NEG[:, i:i + 1], accum_out=D_SUM[:, j:j + 1]).then_inc(Z.d_exp, 1)

            def d_copy(p):
                w = (D_PAIRS[p][1] + 1) * P
                act.wait_ge(Z.d_T, p + 1)
                if p >= 2:
                    act.wait_ge(Z.d_pv, p - 1)
                act.activation(D_WT[p % 2][:, 0:w], bank(4, 2)[:, 0:w], ACT.Copy).then_inc(Z.d_wt, 1)

            def d_output(p):
                h, b = D_PAIRS[p]
                act.wait_ge(Z.d_pv, p + 1)
                if b == 0 and h:
                    act.wait_ge(Z.d_on, h)
                o, rec = bank(6 + p % 2)[:, 0:P], D_REC[:, 2 * (p % 4):2 * (p % 4) + 1]
                act.activation(D_O[:, b * P:(b + 1) * P], o, ACT.Copy, scale=rec).then_inc(Z.d_ln, 1)
                if p:
                    act.wait_ge(Z.d_post, p)
                act.activation(D_JUNK, o, ACT.Square, scale=rec, accum_out=D_SS[:, b:b + 1]).then_inc(Z.d_post, 1)
                if b == NB - 1:
                    act.wait_ge(Z.d_post, p + 1)
                    act.activation(D_LN, D_SS, ACT.Ln, bias=col("eps"), scale=1.0 / P).then_inc(Z.d_rs, 1)
                    act.wait_ge(Z.d_rs, 2 * h + 1)
                    act.activation(D_RS, D_LN, ACT.Exp, scale=-0.5).then_inc(Z.d_rs, 1)

            def d_high(h):
                act.wait_ge(Z.d_hT, h + 1)
                act.activation(hh[:, h], bank(4, 2), ACT.Copy, scale=foldc[:, 0:1]).then_inc(Z.d_hi, 1)

            for s in range(D_STEPS):
                if s < len(D_PAIRS):
                    d_exps(s)
                if 0 <= s - 2 < len(D_PAIRS):
                    d_copy(s - 2)
                if 0 <= s - 3 < len(D_PAIRS):
                    d_output(s - 3)
                if d_head_end(s) is not None:
                    d_high(d_head_end(s))

            def s_logs(u):
                hd, c, k, lo = SB_UNITS[u]
                act.wait_ge(Z.s_capped, u + 1)
                act.activation(S_SP[u % 2][:, lo:], S_SP[u % 2][:, lo:], ACT.Exp).then_inc(Z.s_e, 1)
                act.wait_ge(Z.s_e, u + 1)
                act.activation(S_SP[u % 2][:, lo:], S_SP[u % 2][:, lo:], ACT.Ln, bias=1.0).then_inc(Z.s_L, 1)

            def s_weights(u):
                hd, c, k, lo = SB_UNITS[u]
                act.wait_ge(Z.s_c, u + 1)
                if u >= 2:
                    act.wait_ge(Z.s_pv, u - 1)
                act.activation(S_A[u % 2][:, lo:], bank(u % 4)[:, lo:], ACT.Exp).then_inc(Z.s_a, 1)

            def s_output(chain):
                act.wait_ge(Z.s_pv, SB_CHAIN_END[chain] + 1)
                j, c = chain // 2, chain % 2
                act.activation(S_O[:, j, c * HALF:(c + 1) * HALF], bank(4 + chain % 4), ACT.Copy).then_inc(Z.s_o, 1)

            done = 0
            for u in range(len(SB_UNITS) + 6):
                if u < len(SB_UNITS):
                    s_logs(u)
                if 0 <= u - 2 < len(SB_UNITS):
                    s_weights(u - 2)
                while done < 8 and SB_CHAIN_END[done] <= u - 5:
                    s_output(done)
                    done += 1
            assert done == 8
            for j in range(4):
                act.wait_ge(Z.s_o, 2 * (j + 1))
                if j >= 2:
                    act.wait_ge(Z.s_ss, j - 1)
                if j < 2:
                    act.wait_ge(Z.s_pv, len(SB_UNITS))
                act.activation(S_SQ[j % 2], S_O[:, j], ACT.Square).then_inc(Z.s_sq, 1)

            for j in range(4):
                act.wait_ge(Z.s_ss, j + 1)
                if j >= 2:
                    act.wait_ge(Z.s_lo, j - 1)
                inverse_root(bank(2 * (j % 2), 2), S_RS[j % 2], Z.s_ln, Z.s_rs, j)
                act.wait_ge(Z.s_t, j + 1)
                act.activation(hh[:, 4 + j], S_T[j % 2], ACT.Copy).then_inc(Z.s_hi, 1)

            act.wait_ge(Z.s_lo, 4)
            act.dma_start(x_tiles, A.x.rearrange("f p t -> p f t")).then_inc(Z.x_re, 16)

            def y_copy(c0, use, y):
                def ready(f):
                    act.wait_ge(Z.chunk_done, c0 + f + 1)
                    act.activation(y[f], bank(2 * (f % 3), 2), ACT.Copy).then_inc(Z.y_cp, 1)
                    act.wait_ge(Z.y_cp, 8 * use + f + 1)
                return ready

            Y1t, X1t = [T(f) for f in range(KT)], [T(8 + f) for f in range(KT)]
            post(0, Y1t, y_copy(C_WO, 0, Y1t), NRM1)
            norm(1, X1t, lambda f: act.wait_ge(Z.f_x, f + 1), NRM1, SPLIT_H, None)

            def pace(sem, value):
                act.wait_ge(sem, value)
                act.sem_inc(Z.act_pace, 1)

            def conv_col(j, r):
                o = COLS["conv1"][0] + r
                if isinstance(j, int):
                    return cols[:, o + 8 * j:o + 8 * j + 1]
                return cols[:, bass.ds(j * 8 + o, 1)]

            def ffn1_step(j, b, first, c):
                pace(Z.chunk_done, c + 1)
                if not first:
                    pace(Z.f_prod, j - 1)
                act.activation(CG[b], bank(0, 2), ACT.Identity, bias=conv_col(j, 3), scale=conv_col(j, 2)).then_inc(Z.g_lin, 1)
                pace(Z.g_cv, j * 2 + 2)
                act.activation(CG[b], CG[b], ACT.Gelu_apprx_tanh).then_inc(Z.g_act, 1)
                pace(Z.chunk_done, c + 2)
                if not first:
                    pace(Z.a_lo, j - 1)
                act.activation(CV[b], bank(2, 2), ACT.Identity, bias=conv_col(j, 7), scale=conv_col(j, 6)).then_inc(Z.v_lin, 1)
                pace(Z.f_prod, j + 1)
                act.activation(GATED[b][0], CV[b], ACT.Copy).then_inc(Z.a_hi, 1)

            ffn1_step(0, 0, True, C_FFN1)
            ffn1_step(1, 1, True, ffn_gate(C_FFN1, 1))
            with act.Fori(0, (NJ - 2) // 2) as i:
                for u in range(2):
                    ffn1_step(i * 2 + (2 + u), u, False, i * 6 + ffn_gate(C_FFN1, 2 + u))
            act.preload_act_table_set("natural_log_exp_and_others")
            post(1, Y1t, lambda f: act.wait_ge(Z.dn_free, 4 + 16 * NJ), NRM1)

            def spill(f):
                act.wait_ge(Z.f_x, 8 + f + 1)
                act.dma_start(x2_dram[:, f * S:(f + 1) * S], X1t[f]).then_inc(Z.spill, 16)

            norm(2, X1t, spill, NRM1, SPLIT_H, 0)

            act.dma_start(ROW2.bitcast(I32), A.positions).then_inc(Z.pos_in, 16)
            act.wait_ge(Z.spill, 128)
            act.wait_ge(Z.trig, 7)
            act.activation(SIN, SIN, ACT.Sin, scale=col("sgn")).then_inc(Z.trig_sin, 1)
            act.wait_ge(Z.trig, 14)
            act.activation(COS, COS, ACT.Sin).then_inc(Z.trig_sin, 1)

            def ring_free(n):
                if n < 2:
                    return
                o = n - 2
                if o < 5:
                    act.wait_ge(Z.vT, 16 + 2 * (o + 1))
                elif 6 <= o < 14:
                    act.wait_ge(Z.cv_done, o - 5)
                elif 14 <= o < 19:
                    act.wait_ge(Z.rope_done, o - 13)
                elif o >= 19:
                    act.wait_ge((Z.sg_out0, Z.sg_out1)[o % 2], 16 * ((o - 19) // 2 + 1))

            def finish_conv(n):
                act.wait_ge(Z.cv_t, 3 * (n - 5))
                act.sem_inc(Z.if_ev, 1)
                act.activation(T(5 + n - 6), RING[n % 2][0], ACT.Silu).then_inc(Z.cv_done, 1)

            for n in range(N_IN):
                pair = bank(2 * (n % 3), 2)
                r = RING[n % 2]
                if 7 <= n < 15:
                    finish_conv(n - 1)
                ring_free(n)
                act.wait_ge(Z.chunk_done, C_IN + n + 1)
                if n < 5:
                    for half in range(2):
                        t = slice(half * HALF, (half + 1) * HALF)
                        last = act.activation(r[0][:, t], pair[:, t], ACT.Copy)
                        last.then_inc(Z.vt_ev, 1)
                    act.wait_ge(Z.vt_ev, 16 + 2 * (n + 1))
                    act.sem_inc(Z.if_ev, 1)
                elif n == 5:
                    act.wait_ge(Z.trig, 14)
                    act.activation(ROW1[0:4, :], pair[0:4, :], ACT.Identity, bias=col("b_if")[0:4, :]).then_inc(Z.if_ch, 1)
                    act.activation(ROW1[32:36, :], pair[32:36, :], ACT.Identity, bias=col("b_if")[32:36, :]).then_inc(Z.if_ev, 1)
                elif n < 14:
                    o = 5 * (n - 6)
                    act.activation(r[0], pair, ACT.Identity, bias=col("mconv", o + 4), scale=col("mconv", o + 3)).then_inc(Z.cv_lin, 1)
                elif n < 19:
                    act.activation(r[0], pair, ACT.Copy, scale=DH ** -0.5 if n < 18 else 1.0).then_inc(Z.if_ev, 1)
                    act.wait_ge(Z.if_ev, n + 1)
                    for q in range(4):
                        o = 32 * (q ^ 1)
                        act.dma_start(r[1][32 * q:32 * q + 32, :], r[0][o:o + 32, :]).then_inc((Z.rope_sw0, Z.rope_sw1)[n % 2], 16)
                else:
                    act.activation(r[0], pair, ACT.Sigmoid).then_inc(Z.if_ev, 1)
                    act.wait_ge(Z.if_ev, n + 1)
                    act.dma_start(sg_dram[n - 19], r[0]).then_inc((Z.sg_out0, Z.sg_out1)[n % 2], 16)
                if n == 5:
                    act.wait_ge(Z.if_ch, 2)
                    act.activation(ROW2[32:36, :], ROW2[32:36, :], ACT.Exp, scale=-1.0).then_inc(Z.if_act, 1)
                    act.wait_ge(Z.if_act, 1)
                    act.activation(ROW2[32:36, :], ROW2[32:36, :], ACT.Ln, bias=1.0).then_inc(Z.if_act, 1)
                if n == 7:
                    act.wait_ge(Z.if_ch, 6)
                    act.activation(ROW2[32:36, :], ROW2[0:4, :], ACT.Copy).then_inc(Z.if_act, 1)
                if n == 9:
                    act.wait_ge(Z.if_ch, 7)
                    act.activation(ROW2[32:36, :], ROW2[32:36, :], ACT.Exp, scale=-1.0).then_inc(Z.if_act, 1)

            act.preload_act_table_set("natural_log_exp_and_others")
            for i in range(8):
                act.wait_ge(Z.m_mb, i + 1)
                if i == 0:
                    act.wait_ge(Z.sg_out0, 160)
                    act.wait_ge(Z.sg_out1, 160)
                act.activation(NEGMB[:, i // 2, (i % 2) * HALF:(i % 2 + 1) * HALF], bank(i % 2), ACT.Copy).then_inc(Z.m_mbc, 1)
            act.wait_ge(Z.m_tp, 1)
            act.activation(GT, bank(2)[:, 0:32], ACT.Copy).then_inc(Z.m_tpc, 1)
            act.activation(EMT, bank(3)[:, 0:32], ACT.Copy).then_inc(Z.m_tpc, 1)
            act.wait_ge(Z.m_mbc, 8)
            act.wait_ge(Z.m_tpc, 2)

            def m_outputs(w):
                h, c = w // 2, w % 2
                for t in range(4):
                    act.wait_ge(Z.m_pv, 4 * w + t + 1)
                    act.activation(U[:, 4 * (4 * c + t) + h, :], bank(4 + t)[:, 0:129], ACT.Copy).then_inc(Z.m_U, 1)

            for s, (w, h, c, k, lo) in enumerate(ML_SUBS):
                if s >= 2:
                    act.wait_ge(Z.m_A, s - 1)
                e = M_E[s % 2]
                g = GT[:, 4 * k + h:4 * k + h + 1]
                last = None
                if k >= 4 * c:
                    act.wait_ge(Z.m_d, ML_DIAG[s] + 1)
                    last = act.activation(e[:, lo:lo + P], M_D[ML_DIAG[s] % 2], ACT.Exp, bias=g)
                    if lo + P < HALF:
                        last.then_inc(Z.m_E, 1)
                        last = act.activation(e[:, lo + P:], NEGMB[:, h, c * HALF + lo + P:(c + 1) * HALF], ACT.Exp, bias=g)
                else:
                    last = act.activation(e[:, :], NEGMB[:, h, c * HALF:(c + 1) * HALF], ACT.Exp, bias=g)
                last.then_inc(Z.m_E, 1)
                if s == ML_LAST[w] and w:
                    m_outputs(w - 1)
            m_outputs(7)
            for h in range(HD_ML):
                if h == 0:
                    act.wait_ge(Z.m_E, ML_E[-1])
                act.dma_start(NEGMB[:, h], sg_dram[h]).then_inc(Z.so_in, 16)
            act.wait_ge(Z.l_ch, 7)
            act.activation(L_SQ, U[:, :, 0:P], ACT.Square).then_inc(Z.l_act, 1)
            act.wait_ge(Z.l_ch, 8)
            act.activation(small[:, 96:128], small[:, 64:96], ACT.Ln, bias=col("eps"), scale=1.0 / P).then_inc(Z.l_act, 1)
            act.wait_ge(Z.l_act, 2)
            act.activation(small[:, 96:128], small[:, 96:128], ACT.Exp, scale=-0.5).then_inc(Z.l_act, 1)
            for h in range(HD_ML):
                act.wait_ge(Z.l_t, h + 1)
                act.activation(hh[:, 4 + h], L_T[h % 2], ACT.Copy).then_inc(Z.l_hi, 1)

            def w_exps(u):
                n = u // 2
                a = 0 if n else P
                act.wait_ge(Z.w_a, 5 * u + 5)
                for j in range(4):
                    act.activation(W_P[u % 2][:, j * 256 + a:(j + 1) * 256], W_P[u % 2][:, j * 256 + a:(j + 1) * 256], ACT.Exp,
                                   bias=W_SM[u % 2][:, 4 + j:5 + j], accum_out=W_SM[u % 2][:, 12 + j:13 + j]).then_inc(Z.w_exp, 1)
                act.activation(W_SM[u % 2][:, 8:12], W_SM[u % 2][:, 8:12], ACT.Exp).then_inc(Z.w_exp, 1)

            def w_copy(u):
                n = u // 2
                act.wait_ge(Z.w_T, u + 1)
                if u >= 2:
                    act.wait_ge(Z.w_pv, u - 1)
                if n:
                    act.activation(W_PT[u % 2], bank(4, 2), ACT.Copy).then_inc(Z.w_pt, 1)
                else:
                    v = lambda t: t.rearrange("p (j k q) -> p j k q", j=4, k=2)[:, :, 1, :]
                    act.activation(v(W_PT[u % 2]), v(bank(4, 2)), ACT.Copy).then_inc(Z.w_pt, 1)

            def w_high(n):
                act.wait_ge(Z.w_pv, 2 * n + 2)
                act.activation(hh[:, 0:4, n * P:(n + 1) * P], bank(6 + n % 2).rearrange("p (j q) -> p j q", j=4), ACT.Copy).then_inc(Z.w_hi, 1)

            for s in range(16 + 3):
                if s < 16:
                    w_exps(s)
                if 0 <= s - 1 < 16:
                    w_copy(s - 1)
                if s >= 3 and s % 2 == 1 and (s - 3) // 2 < NB:
                    w_high((s - 3) // 2)

            def gates_load(f):
                if f >= 2:
                    act.wait_ge(Z.b_m, f - 1)
                act.dma_start(B_G[f % 2][0], sg_dram[4 + f]).then_inc((Z.gate0, Z.gate1)[f % 2], 16)
                act.dma_start(B_G[f % 2][1], sg_dram[12 + f]).then_inc((Z.gate0, Z.gate1)[f % 2], 16)

            act.wait_ge(Z.l_t, 4)
            gates_load(0)
            gates_load(1)
            for f in range(KT):
                if f + 2 < KT:
                    gates_load(f + 2)
                act.wait_ge(Z.b_s, f + 1)
                act.activation(SPLIT_A[0][f], B_T[f % 2][0], ACT.Copy).then_inc(Z.b_hi, 1)
            act.wait_ge(Z.chunk_done, C_OUT)
            act.dma_start(hhf[:].rearrange("p f t -> p (f t)"), x2_dram).then_inc(Z.x2_in, 16)
            Y2t, X2t = [T(16 + f) for f in range(KT)], [hhf[:, f] for f in range(KT)]
            post(2, Y2t, y_copy(C_OUT, 1, Y2t), HL_TMP)
            norm(3, X2t, lambda f: act.wait_ge(Z.f_x, 16 + f + 1), HL_TMP, SPLIT_A, 24)

            def ffn2_step(j, b, first, c):
                pace(Z.chunk_done, c + 1)
                if not first:
                    pace(Z.f_prod, j + (NJ - 1))
                act.activation(CG[b], bank(0, 2), ACT.Silu).then_inc(Z.g_lin, 1)
                pace(Z.f_prod, j + (NJ + 1))
                act.activation(GATED[b][0], CV[b], ACT.Copy).then_inc(Z.a_hi, 1)

            ffn2_step(0, 0, True, C_FFN2)
            ffn2_step(1, 1, True, ffn_gate(C_FFN2, 1))
            with act.Fori(0, (NJ - 2) // 2) as i:
                for u in range(2):
                    ffn2_step(i * 2 + (2 + u), u, False, i * 6 + ffn_gate(C_FFN2, 2 + u))
            act.preload_act_table_set("natural_log_exp_and_others")
            post(3, [hlf[:, f] for f in range(KT)], lambda f: act.wait_ge(Z.dn_free, 4 + 32 * NJ), NRM2)
            for f in range(KT):
                act.wait_ge(Z.f_x, 24 + f + 1)
                act.dma_start(A.out[f], hhf[:, f]).then_inc(Z.out_d, 16)
            act.wait_ge(Z.out_d, 128)

        @block.vector
        def _(dve):
            def norm(use, src, gain, nrm, split, shift):
                def low(f):
                    dve.wait_ge(Z.n_hi, 8 * use + f + 1)
                    if shift is None:
                        dve.tensor_tensor(split[1][f], nrm.tmp[f % 2], split[0][f].bitcast(F32), ALU.subtract).then_inc(Z.n_lo, 1)
                    else:
                        dve.scalar_tensor_tensor(split[1][f], nrm.tmp[f % 2], modc[:, shift + f:shift + f + 1],
                                                 split[0][f].bitcast(F32), ALU.add, ALU.subtract).then_inc(Z.n_lo, 1)
                dve.wait_ge(Z.n_rstd, use + 1)
                for f in range(KT):
                    if f >= 2:
                        dve.wait_ge(Z.n_lo, 8 * use + f - 1)
                    dve.scalar_tensor_tensor(nrm.tmp[f % 2], src[f], gain(f), nrm.rstd, ALU.mult, ALU.mult).then_inc(Z.n_t, 1)
                    if f:
                        low(f - 1)
                low(KT - 1)

            def post(use, y, x, gain, nrm):
                dve.wait_ge(Z.f_rstd, use + 1)
                for f in range(KT):
                    dve.scalar_tensor_tensor(y[f], y[f], gain(f), nrm.rstd, ALU.mult, ALU.mult).then_inc(Z.f_y, 1)
                    dve.wait_ge(Z.f_y, 8 * use + f + 1)
                    dve.tensor_tensor(x[f], x[f], y[f], ALU.add).then_inc(Z.f_x, 1)

            dve.wait_ge(Z.consts, 48)
            dve.tensor_tensor(small[:, 64:66], col("lq", 0, 2), col("lk", 0, 2), ALU.mult).then_inc(Z.lam_p, 1)
            dve.wait_ge(Z.tab, 32)
            tabx = T(23)[0:33, 1000:1004]
            dve.memset(T(23)[32:33, 1000:1004], NEG).then_inc(Z.tabx, 1)
            dve.tensor_tensor(T(23)[0:32, 1000:1004], T(23)[0:32, 512:516], T(23)[0:32, 516:520], ALU.subtract).then_inc(Z.tabx, 1)
            dve.wait_ge(Z.tabx, 2)
            for h in range(HD_DIFF):
                dve.tensor_copy(T(22)[0:33, h * P:(h + 1) * P], tabx[:, h:h + 1].to_broadcast([33, P])).then_inc(Z.tb_ready, 1)
            dve.wait_ge(Z.lam_e, 1)
            dve.tensor_tensor(small[:, 68:69], small[:, 66:67], small[:, 67:68], ALU.subtract).then_inc(Z.lam_v, 1)
            dve.wait_ge(Z.lam_v, 1)
            dve.tensor_scalar(foldc[:, 1:2], small[:, 68:69], -1.0, -LAM_INIT, ALU.mult, ALU.add).then_inc(Z.lam_v, 1)
            dve.tensor_scalar(foldc[:, 0:1], col("subln"), 1.0 - LAM_INIT, None, ALU.mult).then_inc(Z.lam_v, 1)
            X1t, Y1t = [T(8 + f) for f in range(KT)], [T(f) for f in range(KT)]
            norm(0, X1t, lambda f: col("attn_pre", f), NRM1, SPLIT_H, None)

            for i in range(48):
                g, k = i // 8, i % 8
                acc = MOD_ACC[g % 4]
                dve.wait_ge((Z.mod_in0, Z.mod_in1, Z.mod_in2, Z.mod_in3)[i % 4], 16 * (i // 4 + 1))
                if k == 0:
                    if g >= 4:
                        dve.wait_ge(Z.mod_ps, g - 3)
                    dve.tensor_scalar(acc, T(16 + i % 4), col("c", k), None, ALU.mult).then_inc(Z.mod_acc, 1)
                else:
                    dve.wait_ge(Z.mod_acc, i)
                    dve.scalar_tensor_tensor(acc, T(16 + i % 4), col("c", k), acc, ALU.mult, ALU.add).then_inc(Z.mod_acc, 1)
            dve.wait_ge(Z.mod_ps, 6)
            dve.scalar_tensor_tensor(modc[:], bank(7)[:, 0:48], float(D), col("b_ada", 0, 48), ALU.mult, ALU.add).then_inc(Z.mod_col, 1)
            dve.wait_ge(Z.mod_col, 1)
            for r, (name, at, add) in enumerate((("pre_mix", 8, 1.0), ("post_mix", 16, 0.0), ("pre_ffn", 32, 1.0))):
                dve.scalar_tensor_tensor(foldc[:, 8 + 8 * r:16 + 8 * r], modc[:, at:at + 8], add, col(name, 0, 8),
                                         ALU.add, ALU.mult).then_inc(Z.fold, 1)
            dve.tensor_tensor(modc[:, 40:48], modc[:, 40:48], col("post_ffn", 0, 8), ALU.mult).then_inc(Z.fold, 1)

            for n in range(8):
                for half in range(2):
                    dve.wait_ge(Z.vT, 2 * n + half + 1)
                    if n == 0:
                        dve.wait_ge(Z.e_out, 64)
                    dve.tensor_copy(V1[:, 4 * half:4 * half + 4, n * P:(n + 1) * P],
                                    bank(6 + half).rearrange("p (b n) -> p b n", b=4)).then_inc(Z.v_cp, 1)

            dve.wait_ge(Z.bias_in, 64)

            def d_max(p, m):
                h, b = D_PAIRS[p]
                v, w, i = 2 * p + m, (b + 1) * P, 2 * (p % 2) + m
                s = bank(*D_BANKS[v])
                a = max(0, (b - 1) * P)
                dve.wait_ge(Z.d_qk, v + 1)
                dve.tensor_tensor(s[:, a:w], s[:, a:w], D_BIAS[:, h * 256 + 256 - (w - a):(h + 1) * 256], ALU.add).then_inc(Z.d_near, 1)
                dve.wait_ge(Z.d_near, v + 1)
                dve.reduce_max(D_MAX[:, i:i + 1], s[:, 0:w], AX).then_inc(Z.d_max, 1)
                dve.wait_ge(Z.d_max, v + 1)
                if p >= 2:
                    dve.wait_ge(Z.d_exp, v - 3)
                dve.tensor_scalar(D_NEG[:, i:i + 1], D_MAX[:, i:i + 1], -1.0, None, ALU.mult).then_inc(Z.d_nmx, 1)

            def d_combine(p):
                w = (D_PAIRS[p][1] + 1) * P
                j = 2 * (p % 4)
                mix = D_MIX[:, p % 4:p % 4 + 1]
                dve.wait_ge(Z.d_exp, 2 * p + 2)
                if p >= 4:
                    dve.wait_ge(Z.d_post, p - 3)
                dve.reciprocal(D_REC[:, j:j + 2], D_SUM[:, j:j + 2]).then_inc(Z.d_r, 1)
                dve.wait_ge(Z.d_r, 2 * p + 1)
                dve.scalar_tensor_tensor(mix, D_REC[:, j + 1:j + 2], foldc[:, 1:2], D_SUM[:, j:j + 1], ALU.mult, ALU.mult).then_inc(Z.d_r, 1)
                dve.wait_ge(Z.d_r, 2 * p + 2)
                p0, p1 = D_P0[p % 3][:, 0:w], D_P1[p % 2][:, 0:w]
                dve.scalar_tensor_tensor(p0, p1, mix, p0, ALU.mult, ALU.add).then_inc(Z.d_w, 1)

            def d_norm(h):
                dve.wait_ge(Z.d_rs, 2 * h + 2)
                if h:
                    dve.wait_ge(Z.d_hT, h)
                v = lambda t: t.rearrange("p (b n) -> p b n", b=NB)
                dve.tensor_tensor(v(D_ON), v(D_O), D_RS.unsqueeze(2).to_broadcast([P, NB, P]), ALU.mult).then_inc(Z.d_on, 1)

            def d_low(h):
                dve.wait_ge(Z.d_hi, h + 1)
                dve.scalar_tensor_tensor(hl[:, h], bank(4, 2), foldc[:, 0:1], hh_read[:, h], ALU.mult, ALU.subtract).then_inc(Z.d_lo, 1)

            for s in range(D_STEPS):
                if d_head_end(s) is not None:
                    d_norm(d_head_end(s))
                if s < len(D_PAIRS):
                    d_max(s, 0)
                    d_max(s, 1)
                if 0 <= s - 1 < len(D_PAIRS):
                    d_combine(s - 1)
                if d_head_end(s) is not None:
                    d_low(d_head_end(s))

            def s_cap(u):
                hd, c, k, lo = SB_UNITS[u]
                dve.wait_ge(Z.s_z, u + 1)
                if u >= 2:
                    dve.wait_ge(Z.s_m, u - 1)
                dve.tensor_scalar(S_SP[u % 2][:, lo:], bank(u % 4)[:, lo:], SP_CAP, None, ALU.min).then_inc(Z.s_capped, 1)

            def s_softplus(u):
                hd, c, k, lo = SB_UNITS[u]
                diag, first = k >= 4 * c, k == 4 * c + 3
                dve.wait_ge(Z.s_L, u + 1)
                if u >= 2:
                    dve.wait_ge(Z.s_c, u - 1)
                m = S_M[u % 2]
                ins = dve.tensor_tensor(m[:, lo:], bank(u % 4)[:, lo:], S_SP[u % 2][:, lo:], ALU.max)
                if diag:
                    ins.then_inc(Z.s_mk, 1)
                    dve.wait_ge(Z.s_mk, SB_DIAG[u] + 1)
                    ins = dve.tensor_tensor(m[:, lo:lo + P], m[:, lo:lo + P], mat("strict"), ALU.mult)
                ins.then_inc(Z.s_m, 1)
                chain = SB_CHAIN[u]
                if first:
                    if u:
                        dve.wait_ge(Z.s_c, u)
                    for i in range(2):
                        dve.memset(S_CY[i], 0.0).then_inc(Z.s_zero, 1)
                    dve.wait_ge(Z.s_zero, 2 * chain + 2)
                dve.wait_ge(Z.s_m, u + 1)
                if u:
                    dve.wait_ge(Z.s_c, u)
                    dve.wait_ge(Z.s_cy, u)
                dve.tensor_tensor(S_CY[(u + 1) % 2][:, lo:], S_CY[u % 2][:, lo:], m[:, lo:], ALU.add).then_inc(Z.s_cy, 1)

            dve.wait_ge(Z.d_qk, 64)
            for u in range(len(SB_UNITS) + 1):
                if u < len(SB_UNITS):
                    s_cap(u)
                if u:
                    s_softplus(u - 1)
            for j in range(4):
                dve.wait_ge(Z.s_rs, j + 1)
                if j >= 2:
                    dve.wait_ge(Z.s_lo, j - 1)
                dve.scalar_tensor_tensor(S_T[j % 2], S_O[:, j], col("sbnorm"), S_RS[j % 2], ALU.mult, ALU.mult).then_inc(Z.s_t, 1)
                dve.wait_ge(Z.s_hi, j + 1)
                dve.tensor_tensor(hl[:, 4 + j], S_T[j % 2], hh_read[:, 4 + j], ALU.subtract).then_inc(Z.s_lo, 1)

            dve.wait_ge(Z.x_re, 16)
            post(0, Y1t, X1t, lambda f: col("attn_post", f), NRM1)
            dve.wait_ge(Z.f_y, 8)
            norm(1, X1t, lambda f: col("ffn_pre", f), NRM1, SPLIT_H, None)

            def conv_col(j, r):
                o = COLS["conv1"][0] + r
                if isinstance(j, int):
                    return cols[:, o + 8 * j:o + 8 * j + 1]
                return cols[:, bass.ds(j * 8 + o, 1)]

            def taps(j, buf, b, r, lin, cv):
                pair = bank(b, 2)
                dve.wait_ge(lin, j + 1)
                dve.scalar_tensor_tensor(buf[:, 1:], pair[:, 0:S - 1], conv_col(j, r + 1), buf[:, 1:], ALU.mult, ALU.add).then_inc(cv, 1)
                dve.wait_ge(cv, j * 2 + 1)
                dve.scalar_tensor_tensor(buf[:, 2:], pair[:, 0:S - 2], conv_col(j, r), buf[:, 2:], ALU.mult, ALU.add).then_inc(cv, 1)

            def down_sums(y, j, use, c):
                dve.wait_ge(Z.dn_free, j * 16 + (16 * NJ * use + 4))
                for o in range(16):
                    f, half = o // 2, o % 2
                    if o < 15:
                        dve.wait_ge(Z.dn_done, j * 15 + (15 * NJ * use + o + 1))
                    else:
                        dve.wait_ge(Z.chunk_done, c + 1)
                    t = y[f][:, half * HALF:(half + 1) * HALF]
                    dve.tensor_tensor(t, bank(4 + o % 4), t, ALU.add).then_inc(Z.dn_free, 1)

            def zero(y, use):
                for f in range(KT):
                    dve.memset(y[f], 0.0).then_inc(Z.y_zero, 1)
                dve.wait_ge(Z.y_zero, 8 * (use + 1))

            def ffn1_step(j, b, c, sums):
                taps(j, CG[b], 0, 0, Z.g_lin, Z.g_cv)
                if sums is not None:
                    sums()
                taps(j, CV[b], 2, 4, Z.v_lin, Z.v_cv)
                dve.wait_ge(Z.g_act, j + 1)
                dve.wait_ge(Z.v_cv, j * 2 + 2)
                dve.tensor_tensor(CV[b], CV[b], CG[b], ALU.mult).then_inc(Z.f_prod, 1)
                dve.wait_ge(Z.a_hi, j + 1)
                dve.tensor_tensor(GATED[b][1], CV[b], GATED[b][0].bitcast(F32), ALU.subtract).then_inc(Z.a_lo, 1)

            dve.wait_ge(Z.f_y, 8)
            zero(Y1t, 0)
            dve.sem_inc(Z.dn_free, 4)
            ffn1_step(0, 0, C_FFN1, None)
            with dve.Fori(0, (NJ - 2) // 2) as i:
                for u in range(2):
                    c = i * 6 + ffn_gate(C_FFN1, 1 + u)
                    ffn1_step(i * 2 + (1 + u), (1 + u) % 2, c, lambda: down_sums(Y1t, i * 2 + u, 0, c + 2))
            j = NJ - 1
            ffn1_step(j, j % 2, ffn_gate(C_FFN1, j), lambda: down_sums(Y1t, j - 1, 0, ffn_gate(C_FFN1, j) + 2))
            down_sums(Y1t, j, 0, ffn_down_last(C_FFN1))
            dve.wait_ge(Z.dn_free, 4 + 16 * NJ)
            post(1, Y1t, X1t, lambda f: col("ffn_post", f), NRM1)
            dve.wait_ge(Z.fold, 4)
            norm(2, X1t, lambda f: foldc[:, 8 + f:9 + f], NRM1, SPLIT_H, 0)

            C1 = 6.28125
            C2 = float(np.float32(2 * math.pi - C1))
            C3 = 2 * math.pi - C1 - C2
            MAGIC = 12582912.0
            PI = float(np.float32(3.1415925))
            tr = [0]

            def trig(ins):
                ins.then_inc(Z.trig, 1)
                tr[0] += 1
                dve.wait_ge(Z.trig, tr[0])

            dve.wait_ge(Z.pos_in, 16)
            trig(dve.tensor_scalar(ROW1, ROW2.bitcast(I32), col("invf"), None, ALU.mult))
            for dst, shift in ((SIN, 0.0), (COS, 0.25)):
                trig(dve.tensor_scalar(ROW2, ROW1, float(np.float32(0.5 / math.pi)), shift, ALU.mult, ALU.add))
                trig(dve.tensor_scalar(ROW2, ROW2, MAGIC, -MAGIC, ALU.add, ALU.add))
                trig(dve.scalar_tensor_tensor(dst, ROW2, -C1, ROW1, ALU.mult, ALU.add))
                trig(dve.scalar_tensor_tensor(dst, ROW2, -C2, dst, ALU.mult, ALU.add))
                trig(dve.scalar_tensor_tensor(dst, ROW2, -C3, dst, ALU.mult, ALU.add))
                if shift == 0.0:
                    trig(dve.tensor_scalar(dst, dst, PI, -PI, ALU.min, ALU.max))
                else:
                    trig(dve.tensor_scalar(dst, dst, math.pi / 2, PI, ALU.add, ALU.min))
                    trig(dve.tensor_scalar(dst, dst, -PI, None, ALU.max))

            dve.wait_ge(Z.spill, 128)
            for h in range(HD_ML):
                o = P + h * 129 + 128
                dve.memset(V2[:, :, o:o + 1], 1.0).then_inc(Z.fold, 1)
            if_n = [0]

            def gate_rows(ins):
                ins.then_inc(Z.if_ch, 1)

            for n in range(N_IN):
                r = RING[n % 2]
                if 1 <= n < 6:
                    m = n - 1
                    for half in range(2):
                        dve.wait_ge(Z.vT, 16 + 2 * m + half + 1)
                        o = 0 if m == 0 else P + (m - 1) * 129
                        dve.tensor_copy(V2[:, 4 * half:4 * half + 4, o:o + P],
                                        bank(6 + half).rearrange("p (b n) -> p b n", b=4)).then_inc(Z.v_cp, 1)
                if n == 5:
                    dve.wait_ge(Z.if_ev, 6)
                    gate_rows(dve.scalar_tensor_tensor(ROW2[32:36, :], ROW1[32:36, :], -1.0, ROW1[32:36, :], ALU.mult, ALU.max))
                if n == 6:
                    dve.wait_ge(Z.if_act, 2)
                    gate_rows(dve.scalar_tensor_tensor(ROW2[0:4, :], ROW1[32:36, :], 0.0, ROW2[32:36, :], ALU.min, ALU.subtract))
                    dve.wait_ge(Z.if_ch, 3)
                    gate_rows(dve.tensor_tensor_scan(ROW2[0:4, :], ROW2[0:4, :], ROW2[0:4, :], 0.0, ALU.add, ALU.min))
                    dve.wait_ge(Z.if_ch, 4)
                    gate_rows(dve.tensor_tensor(ROW1[0:4, :], ROW1[0:4, :], ROW2[0:4, :], ALU.subtract))
                    dve.wait_ge(Z.if_ch, 5)
                    gate_rows(dve.tensor_tensor_scan(ROW1[32:36, :], ROW1[0:4, :], ROW1[0:4, :], 0.0, ALU.max, ALU.max))
                if n == 8:
                    dve.wait_ge(Z.if_act, 3)
                    gate_rows(dve.tensor_tensor(ROW2[32:36, :], ROW2[32:36, :], ROW1[32:36, :], ALU.add))
                if 6 <= n < 14:
                    o = 5 * (n - 6)
                    pair = bank(2 * (n % 3), 2)
                    dve.wait_ge(Z.cv_lin, n - 5)
                    for tap in range(1, 4):
                        if tap > 1:
                            dve.wait_ge(Z.cv_t, 3 * (n - 6) + tap - 1)
                        dve.scalar_tensor_tensor(r[0][:, tap:], pair[:, 0:S - tap], col("mconv", o + 3 - tap), r[0][:, tap:],
                                                 ALU.mult, ALU.add).then_inc(Z.cv_t, 1)
                if 14 <= n < 19:
                    i = n - 14
                    dst = T(i)
                    if i == 0:
                        dve.wait_ge(Z.trig_sin, 2)
                    dve.wait_ge((Z.rope_sw0, Z.rope_sw1)[n % 2], 64 * (i // 2 + 1))
                    dve.tensor_tensor(dst, r[0], COS, ALU.mult).then_inc(Z.rope_t, 1)
                    dve.tensor_tensor(r[1], r[1], SIN, ALU.mult).then_inc(Z.rope_t, 1)
                    dve.wait_ge(Z.rope_t, 2 * (i + 1))
                    dve.tensor_tensor(dst, dst, r[1], ALU.add).then_inc(Z.rope_done, 1)

            dve.wait_ge(Z.chunk_done, C_BR)
            for h in range(HD_ML):
                ins = dve.tensor_scalar(M_SEL[32:36, h * P:(h + 1) * P], mat("ident")[32:36, 32 + h:33 + h].to_broadcast([4, P]),
                                        -1.0, None, ALU.mult)
            ins.then_inc(Z.m_sel, 1)

            def m_diag(s):
                w, h, c, k, lo = ML_SUBS[s]
                i = ML_DIAG[s]
                if i >= 2:
                    dve.wait_ge(Z.m_E, ML_E[ML_DIAG_OF[i - 2]])
                dve.tensor_tensor(M_D[i % 2], NEGMB[:, h, k * P:(k + 1) * P], mat("negcausal"), ALU.add).then_inc(Z.m_d, 1)

            dve.wait_ge(Z.m_mbc, 8)
            m_diag(ML_DIAG_OF[0])
            di = 1
            for s, (w, h, c, k, lo) in enumerate(ML_SUBS):
                if di < len(ML_DIAG_OF) and ML_DIAG_OF[di] <= s + 1:
                    m_diag(ML_DIAG_OF[di])
                    di += 1
                dve.wait_ge(Z.m_E, ML_E[s])
                dve.wait_ge(Z.m_S, s + 1)
                if w >= 2:
                    dve.wait_ge(Z.m_pv, 4 * (w - 1))
                dve.scalar_tensor_tensor(M_A[w % 2][:, k, lo:], bank(s % 4)[:, lo:], ML_D ** -0.5, M_E[s % 2][:, lo:],
                                         ALU.mult, ALU.mult).then_inc(Z.m_A, 1)
            ln = [0]

            def step(ins):
                ins.then_inc(Z.l_ch, 1)
                ln[0] += 1
                dve.wait_ge(Z.l_ch, ln[0])

            def over(t):
                return t.unsqueeze(2).to_broadcast([P, 32, P])

            dve.wait_ge(Z.m_U, 32)
            body = U[:, :, 0:P]
            den, raw_den = small[:, 64:96], U[:, :, P:P + 1].rearrange("p i o -> p (i o)")
            step(dve.scalar_tensor_tensor(den, raw_den, -1.0, raw_den, ALU.mult, ALU.max))
            step(dve.tensor_tensor(den, den, EMT, ALU.max))
            step(dve.reciprocal(den, den))
            step(dve.tensor_tensor(body, body, over(den), ALU.mult))
            step(dve.tensor_reduce(den, body, AX, ALU.add))
            step(dve.tensor_scalar(den, den, -1.0 / P, None, ALU.mult))
            step(dve.tensor_tensor(body, body, over(den), ALU.add))
            dve.wait_ge(Z.l_act, 1)
            step(dve.tensor_reduce(den, L_SQ, AX, ALU.add))
            dve.wait_ge(Z.l_act, 3)
            step(dve.tensor_tensor(body, body, over(small[:, 96:128]), ALU.mult))
            assert ln[0] == LN_LAST
            dve.wait_ge(Z.so_in, 64)
            for h in range(HD_ML):
                dve.wait_ge(Z.l_T, h + 1)
                if h >= 2:
                    dve.wait_ge(Z.l_lo, h - 1)
                dve.scalar_tensor_tensor(L_T[h % 2], bank(2 * (h % 2), 2), col("mnorm", h), NEGMB[:, h], ALU.mult, ALU.mult).then_inc(Z.l_t, 1)
                dve.wait_ge(Z.l_hi, h + 1)
                dve.tensor_tensor(hl[:, 4 + h], L_T[h % 2], hh_read[:, 4 + h], ALU.subtract).then_inc(Z.l_lo, 1)

            def w_mask(u):
                n, g = u // 2, u % 2
                a = 0 if n else P
                v = lambda t: t.rearrange("p (j k) -> p j k", j=4)[:, :, a:]
                sm = W_SM[u % 2]
                sink = col("sinks", 4 * g, 4)

                def did(ins, i):
                    ins.then_inc(Z.w_a, 1)
                    dve.wait_ge(Z.w_a, 5 * u + i)
                dve.wait_ge(Z.w_qk, u + 1)
                if u >= 2:
                    dve.wait_ge(Z.w_T, u - 1)
                mask = mat("band")[:, a:].unsqueeze(1).to_broadcast([P, 4, 2 * P - a])
                did(dve.tensor_tensor(v(W_P[u % 2]), v(bank(2 * (u % 2), 2)), mask, ALU.add), 1)
                did(dve.tensor_reduce(sm[:, 0:4], v(W_P[u % 2]), AX, ALU.max), 2)
                did(dve.tensor_tensor(sm[:, 0:4], sm[:, 0:4], sink, ALU.max), 3)
                did(dve.tensor_scalar(sm[:, 4:8], sm[:, 0:4], -1.0, None, ALU.mult), 4)
                dve.tensor_tensor(sm[:, 8:12], sink, sm[:, 0:4], ALU.subtract).then_inc(Z.w_a, 1)

            def w_norm(u):
                n = u // 2
                a = 0 if n else P
                sm = W_SM[u % 2]
                dve.wait_ge(Z.w_exp, 5 * u + 5)
                dve.tensor_tensor(sm[:, 12:16], sm[:, 12:16], sm[:, 8:12], ALU.add).then_inc(Z.w_b, 1)
                dve.wait_ge(Z.w_b, 2 * u + 1)
                dve.reciprocal(sm[:, 16:20], sm[:, 12:16]).then_inc(Z.w_b, 1)
                dve.wait_ge(Z.w_b, 2 * u + 2)
                v = W_P[u % 2].rearrange("p (j k) -> p j k", j=4)[:, :, a:]
                dve.tensor_tensor(v, v, sm[:, 16:20].unsqueeze(2).to_broadcast([P, 4, 2 * P - a]), ALU.mult).then_inc(Z.w_pn, 1)

            def w_low(n):
                dve.wait_ge(Z.w_hi, n + 1)
                t = slice(n * P, (n + 1) * P)
                dve.tensor_tensor(hl[:, 0:4, t], bank(6 + n % 2).rearrange("p (j q) -> p j q", j=4), hh_read[:, 0:4, t], ALU.subtract).then_inc(Z.w_lo, 1)

            for s in range(16 + 3):
                if s < 16:
                    w_mask(s)
                if 0 <= s - 1 < 16:
                    w_norm(s - 1)
                if s >= 3 and s % 2 == 1 and (s - 3) // 2 < NB:
                    w_low((s - 3) // 2)

            for f in range(KT):
                t, u = B_T[f % 2]
                dve.wait_ge((Z.gate0, Z.gate1)[f % 2], 32 * (f // 2 + 1))
                dve.wait_ge(Z.chunk_done, C_BR + f + 1)
                if f >= 2:
                    dve.wait_ge(Z.b_lo, f - 1)
                dve.tensor_tensor(t, bank(4 * (f % 2), 2), B_G[f % 2][0], ALU.mult).then_inc(Z.b_a, 1)
                dve.tensor_tensor(u, bank(4 * (f % 2) + 2, 2), B_G[f % 2][1], ALU.mult).then_inc(Z.b_m, 1)
                dve.wait_ge(Z.b_a, f + 1)
                dve.wait_ge(Z.b_m, f + 1)
                dve.tensor_tensor(t, t, u, ALU.add).then_inc(Z.b_s, 1)
                dve.wait_ge(Z.b_hi, f + 1)
                dve.tensor_tensor(SPLIT_A[1][f], t, SPLIT_A[0][f].bitcast(F32), ALU.subtract).then_inc(Z.b_lo, 1)

            Y2t, X2t = [T(16 + f) for f in range(KT)], [hhf[:, f] for f in range(KT)]
            YF2 = [hlf[:, f] for f in range(KT)]
            dve.wait_ge(Z.x2_in, 16)
            post(2, Y2t, X2t, lambda f: foldc[:, 16 + f:17 + f], HL_TMP)
            norm(3, X2t, lambda f: foldc[:, 24 + f:25 + f], HL_TMP, SPLIT_A, 24)

            def ffn2_step(j, b, c, sums):
                if sums is not None:
                    sums()
                dve.wait_ge(Z.g_lin, j + (NJ + 1))
                dve.wait_ge(Z.chunk_done, c + 2)
                dve.tensor_tensor(CV[b], bank(2, 2), CG[b], ALU.mult).then_inc(Z.f_prod, 1)
                dve.wait_ge(Z.a_hi, j + (NJ + 1))
                dve.tensor_tensor(GATED[b][1], CV[b], GATED[b][0].bitcast(F32), ALU.subtract).then_inc(Z.a_lo, 1)

            dve.wait_ge(Z.n_lo, 32)
            zero(YF2, 1)
            ffn2_step(0, 0, C_FFN2, None)
            with dve.Fori(0, (NJ - 2) // 2) as i:
                for u in range(2):
                    c = i * 6 + ffn_gate(C_FFN2, 1 + u)
                    ffn2_step(i * 2 + (1 + u), (1 + u) % 2, c, lambda: down_sums(YF2, i * 2 + u, 1, c + 2))
            j = NJ - 1
            ffn2_step(j, j % 2, ffn_gate(C_FFN2, j), lambda: down_sums(YF2, j - 1, 1, ffn_gate(C_FFN2, j) + 2))
            down_sums(YF2, j, 1, ffn_down_last(C_FFN2))
            dve.wait_ge(Z.dn_free, 4 + 32 * NJ)
            post(3, YF2, X2t, lambda f: modc[:, 40 + f:41 + f], NRM2)




_OUT = (KT, P, S)


def columns(v):
    v = np.asarray(v).reshape(-1)
    return v.reshape(-1, P).T


def chunks(w, feature_tiles):
    k = w.shape[0] // P
    return w.reshape(k, P, feature_tiles, P).transpose(2, 1, 0, 3).reshape(feature_tiles, P, k * P)


def ffn_chunks(gate, value, down):
    out = [gate[0], value[0]]
    for j in range(1, NJ):
        out += [gate[j], value[j], down[j - 1]]
    return np.stack(out + [down[NJ - 1]])


def kernel(**a):
    import concourse.bacc as bacc
    from concourse.bass_utils import run_bass_kernel_spmd

    a = {n: np.asarray(v) for n, v in a.items()}
    x = np.ascontiguousarray(a["x"][0].T.reshape(KT, P, S))

    dq, dk, dv, sq, sk, sv = np.split(a["w_qkv"][0], 6, axis=1)
    qkv = chunks(np.concatenate([dq, sq, dk, sk, dv, sv], axis=1), N_QKV)
    up = chunks(a["w_up"][0], 2 * NJ)
    ffn1 = ffn_chunks(up[:NJ], up[NJ:], a["w_down"][0].reshape(NJ, P, D))
    sizes = np.cumsum((512, 128, 128, 512, 512, 512, 512, 4, 4, 1024))
    q_a, k_a, v_a, q_m, k_m, v_m, o_m, i_m, f_m, g_a, g_m = np.split(a["w_in_2"][0], sizes, axis=1)
    q_a = q_a.reshape(D, 2, 4, DH).transpose(0, 2, 1, 3).reshape(D, 512)
    rows = np.zeros((D, P), np.float32)
    rows[:, 0:4], rows[:, 32:36] = i_m, f_m
    w_in = chunks(np.concatenate([v_a, v_m, rows, q_m, k_m, q_a, k_a, o_m, g_a, g_m], axis=1), N_IN)
    w_ba = a["w_branch_attn_2"][0].reshape(2, 4, DH, D).transpose(1, 0, 2, 3).reshape(512, D)
    branch = chunks(np.concatenate([w_ba, a["w_branch_mlstm_2"][0]], axis=0), N_MIX)
    ffn2 = ffn_chunks(chunks(a["w_ffn_gate_2"][0], NJ), chunks(a["w_ffn_up_2"][0], NJ), a["w_ffn_down_2"][0].reshape(NJ, P, D))
    w = np.concatenate([qkv, chunks(a["w_o"][0], N_MIX), ffn1, w_in, branch, chunks(a["w_out_2"][0], N_MIX), ffn2])

    c = np.zeros((P, N_COLS), np.float32)

    def put(name, v):
        o, n = COLS[name]
        c[:, o:o + n] = v

    for name, key in (("attn_pre", "attn_pre_norm"), ("attn_post", "attn_post_norm"), ("ffn_pre", "ffn_pre_norm"),
                      ("ffn_post", "ffn_post_norm"), ("subln", "diff_subln"), ("b_ada", "b_ada_2"), ("c", "c_2"),
                      ("pre_mix", "g_pre_mix_2"), ("post_mix", "g_post_mix_2"), ("pre_ffn", "g_pre_ffn_2"),
                      ("post_ffn", "g_post_ffn_2"), ("mnorm", "mlstm_norm_w_2")):
        put(name, columns(a[key]))
    put("sbnorm", np.concatenate([a["sb_norm"][0]] * 2)[:, None])
    taps = np.concatenate([a["conv_w"][0], a["conv_b"]]).reshape(4, 2, NJ, P)
    put("conv1", taps.transpose(3, 2, 1, 0).reshape(P, NJ * 8))
    taps = np.concatenate([a["conv_w_2"][0], a["conv_b_2"]]).reshape(5, 8, P)
    put("mconv", taps.transpose(2, 1, 0).reshape(P, 40))
    for name, k1, k2 in (("lq", "lambda_q1", "lambda_q2"), ("lk", "lambda_k1", "lambda_k2")):
        o, _ = COLS[name]
        c[0:DH, o], c[0:DH, o + 1] = a[k1][0], a[k2][0]
    o, _ = COLS["b_if"]
    c[0:4, o], c[32:36, o] = a["b_if_2"][0, 0:4], a["b_if_2"][0, 4:8]
    put("sinks", np.broadcast_to(a["attn_sinks_2"], (P, 8)))
    put("eps", EPS)
    i = np.arange(P)
    put("invf", (np.float32(10000.0) ** (np.float32(-2.0) * (i % 32).astype(np.float32) / np.float32(DH)))[:, None])
    put("sgn", np.where(i % DH < 32, -1.0, 1.0)[:, None])
    mats, onehot = host_matrices()
    arrays = {
        "x_t": x, "weights": w, "columns": c, "matrices": mats, "onehot": onehot,
        "table": np.ascontiguousarray(a["rel_bias"]),
        "table_last": np.ascontiguousarray(np.broadcast_to(a["rel_bias"][31:32], (32, HD_DIFF))),
        "w_ada": np.ascontiguousarray(a["w_ada_2"][0].reshape(KT, P, 6 * D)),
        "positions": np.ascontiguousarray(np.broadcast_to(a["positions_2"], (P, S))),
    }
    nc = bacc.Bacc("TRN2", target_bir_lowering=False, num_devices=1)
    d = {n: nc.dram_tensor(n, v.shape, mybir.dt.from_np(v.dtype), kind="ExternalInput").ap() for n, v in arrays.items()}
    out = nc.dram_tensor("out_t", _OUT, F32, kind="ExternalOutput").ap()
    build(nc, Arrays(x=d["x_t"], w=d["weights"], cols=d["columns"], mats=d["matrices"], onehot=d["onehot"],
                              table=d["table"], table31=d["table_last"], w_ada=d["w_ada"], positions=d["positions"], out=out))
    r = run_bass_kernel_spmd(nc, [arrays], core_ids=[0])
    y = r.results[0]["out_t"]
    return np.ascontiguousarray(y.reshape(D, S).T).reshape(1, S, D)
```

```python
import math
from contextlib import ExitStack
from collections import namedtuple

import numpy as np

import concourse.bass as bass
from concourse import mybir

F32 = mybir.dt.float32
F32R = mybir.dt.float32r
I32 = mybir.dt.int32
ALU = mybir.AluOpType
ACT = mybir.ActivationFunctionType
AX = mybir.AxisListType.X

P = 128
S = 1024
D = 1024
HALF = 512
KT = D // P
NB = S // P
DFF = 2816
NJ = DFF // P
EPS = 1e-6
NEG = -1e30
SP_CAP = 30.0
LAM_INIT = 0.8 - 0.6 * math.exp(0.0)
DH = 64
HD_DIFF = 4
HD_SB = 8
HD_ML = 4
ML_D = 128

NormBuffers = namedtuple("NormBuffers", "sq rstd tmp whole total")
Arrays = namedtuple("Arrays", "x w cols mats onehot table table31 w_ada positions out")

N_QKV, N_MIX, N_FFN, N_IN = 24, 8, 3 * NJ, 39
C_QKV = 0
C_WO = C_QKV + N_QKV
C_FFN1 = C_WO + N_MIX
C_IN = C_FFN1 + N_FFN
C_BR = C_IN + N_IN
C_OUT = C_BR + N_MIX
C_FFN2 = C_OUT + N_MIX
N_CHUNKS = C_FFN2 + N_FFN
RAW = 2
SL = 3

COLS, _at = {}, 0
for _name, _n in (
    ("attn_pre", KT), ("attn_post", KT), ("ffn_pre", KT), ("ffn_post", KT), ("subln", 1), ("sbnorm", 1),
    ("conv1", NJ * 8), ("b_ada", 48), ("c", KT), ("lq", 2), ("lk", 2), ("pre_mix", KT), ("post_mix", KT),
    ("pre_ffn", KT), ("post_ffn", KT), ("mconv", 8 * 5), ("mnorm", 4), ("b_if", 1), ("sinks", 8),
    ("eps", 1), ("invf", 1), ("sgn", 1),
):
    COLS[_name] = (_at, _n)
    _at += _n
N_COLS = _at
MATS, _at = {}, 0
for _name, _n in (("ident", P), ("mean", P), ("negtri", P), ("negones", P), ("mean64", P),
                  ("strict", P), ("negstrict", P), ("negcausal", P), ("band", 2 * P)):
    MATS[_name] = (_at, _n)
    _at += _n
N_MATS = _at
ONEHOT_W = 384


def host_matrices():
    i = np.arange(P)
    q, k = i[:, None], i[None, :]
    m = np.zeros((P, N_MATS), np.float32)

    def put(name, value):
        o, n = MATS[name]
        m[:, o:o + n] = value

    put("ident", np.eye(P))
    put("mean", 1.0 / D)
    put("negtri", -(q >= k).astype(np.float32))
    put("negones", -1.0)
    put("mean64", (q // DH == k // DH) / float(DH))
    put("strict", (q < k))
    put("negstrict", np.where(q < k, 0.0, NEG))
    put("negcausal", np.where(q <= k, 0.0, NEG))
    j = np.arange(2 * P)[None, :] - P
    put("band", np.where((j <= q) & (q - j < P), 0.0, NEG))
    rel = 255 - np.arange(ONEHOT_W)
    n = np.maximum(rel, 0)
    large = 16 + (np.log(np.maximum(n, 1).astype(np.float32) / np.float32(16))
                  / np.float32(math.log(8.0)) * np.float32(16)).astype(np.int32)
    bucket = np.where(n < 16, n, np.minimum(large, 31))
    bucket = np.where(rel < 0, 32, bucket)
    onehot = (np.arange(33)[:, None] == bucket[None, :]).astype(np.float32)
    return m, onehot


def build(nc, A):
    ctx = ExitStack()
    with ctx:
        at = [-(-nc.sbuf_base // 32) * 32]

        def place(name, shape, dt=F32, offset=None):
            if offset is None:
                offset = at[0]
                at[0] += -(-4 * int(np.prod(shape[1:])) // 32) * 32
            return nc.alloc_sbuf_tensor_at(name, shape, dt, offset=offset, align_bytes=32)

        raw = place("raw", [P, RAW, 1024])
        wh = place("wh", [P, SL, 1024], F32R)
        wl = place("wl", [P, SL, 1024], F32R)
        HH_AT = at[0]
        hh = place("hh", [P, KT, S], F32R)
        hl = place("hl", [P, KT, S], F32R)
        hhf = place("hhf", [P, KT, S], F32, HH_AT)
        hlf = place("hlf", [P, KT, S], F32, HH_AT + 4 * KT * S)
        hh_read = hh[:].bitcast(F32)
        ARENA = 26 * S + 64
        ARENA_AT = at[0]
        arena = place("arena", [P, ARENA])
        ah = place("ah", [P, KT, S], F32R, ARENA_AT)
        al = place("al", [P, KT, S], F32R, ARENA_AT + 4 * KT * S)
        gated = place("gated", [P, 2, 2, S], F32R, ARENA_AT + 4 * 16 * S)
        masks = place("masks", [P, 3, P], F32R, ARENA_AT + 4 * 24 * S)
        cols = place("cols", [P, N_COLS])
        mats = place("mats", [P, N_MATS])
        modc = place("modc", [P, 48])
        foldc = place("foldc", [P, 32])
        small = place("small", [P, P])
        dsm = place("dsm", [P, 64])
        ps = ctx.enter_context(nc.psum_tensor("ps", [P, 8 * HALF], F32))

        def T(n, k=1):
            return arena[:, n * S:(n + k) * S]

        def col(name, i=0, n=1):
            o, _ = COLS[name]
            return cols[:, o + i:o + i + n]

        def mat(name):
            o, n = MATS[name]
            return mats[:, o:o + n]

        def bank(b, n=1):
            return ps[:, b * HALF:(b + n) * HALF]


        names = """
        raw0 raw1 wt_hi split_done chunk_done pace
        consts x_in0 x_in1 tab setup tb_ready e_ps e_sb e_out bias_in
        mod_in0 mod_in1 mod_in2 mod_in3 mod_acc mod_ps mod_col fold lam_p lam_ps lam_e
        n_sq n_ss n_ln n_rstd n_t n_hi n_lo f_sq f_ss f_ln f_rstd f_y f_x y_sq y_sum y_ss
        q_ev vt_ev vT v_cp
        d_qk d_near d_max d_nmx d_exp d_r d_w d_T d_wt d_pv d_post d_rs d_on d_hT d_hi d_lo
        s_z s_capped s_L s_m s_mk s_mhi s_mlo s_cy s_c s_a s_pv s_o s_sq s_ss s_ln s_rs s_t s_hi s_lo
        y_cp x_re
        g_lin g_act v_lin g_cv v_cv f_prod a_hi a_lo dn_done dn_free y_zero
        pos_in trig trig_sin spill if_ev if_ch if_act rope_sw0 rope_sw1 rope_t rope_done cv_lin cv_t cv_done sg_out0 sg_out1
        m_sel m_mb m_mbc m_tp m_tpc m_S m_d m_E m_A m_pv m_U l_mu l_den l_sq l_v l_rs l_s l_y l_T l_g l_hi l_lo so_in0 so_in1 so_in2 so_in3
        w_qk w_a w_exp w_b w_pn w_T w_pt w_pv w_hi w_lo
        gate0 gate1 b_a b_m b_s b_hi b_lo x2_in out_d
        """.split()
        Z = namedtuple("Semaphores", names)(*[ctx.enter_context(nc.semaphore(n)) for n in names])

        e_dram = nc.dram_tensor("e_scratch", (HD_DIFF, P, ONEHOT_W), F32, kind="Internal").ap()
        x2_dram = nc.dram_tensor("x2_scratch", (P, KT * S), F32, kind="Internal").ap()
        sg_dram = nc.dram_tensor("gate_scratch", (20, P, S), F32, kind="Internal").ap()

        block = ctx.enter_context(nc.Block())

        X1 = T(8, 8)
        Y1 = T(0, 8)
        strips = lambda t: [t[:, i * HALF:(i + 1) * HALF] for i in range(t.shape[1] // HALF)]
        NRM1 = NormBuffers(sq=strips(T(16, 2)), rstd=strips(T(18)), tmp=strips(T(19, 2)),
                           whole=[T(16), T(17)], total=T(19))
        flat = lambda t: t.rearrange("p f t -> p (f t)")
        HL_TMP = NormBuffers(sq=strips(flat(hlf[:, 0:2])), rstd=strips(hlf[:, 2]), tmp=strips(flat(hlf[:, 3:5])),
                             whole=[hlf[:, 0], hlf[:, 1]], total=hlf[:, 3])
        SPLIT_H = ([hh[:, f] for f in range(KT)], [hl[:, f] for f in range(KT)])
        SPLIT_A = ([ah[:, f] for f in range(KT)], [al[:, f] for f in range(KT)])
        V1 = T(16, 8).rearrange("p (b n) -> p b n", b=NB)
        VT1 = T(24)
        MOD_ACC = [T(20), T(21), T(25), T(24)]
        V2_AT, V2_W = 13 * S, P + HD_ML * (ML_D + 1)
        V2 = arena[:, V2_AT:V2_AT + NB * V2_W].rearrange("p (b n) -> p b n", b=NB)
        R4 = V2_AT + NB * V2_W
        COS, SIN = arena[:, R4:R4 + S], arena[:, R4 + S:R4 + 2 * S]
        RING = [[arena[:, R4 + (2 + 2 * r + i) * S:R4 + (3 + 2 * r + i) * S] for i in range(2)] for r in range(2)]
        ROW1, ROW2 = arena[:, R4 + 6 * S:R4 + 7 * S], arena[:, R4 + 7 * S:R4 + 8 * S]
        NEGMB = arena[:, R4:R4 + 4 * S].rearrange("p (h t) -> p h t", h=HD_ML)
        U_AT = R4 + 4 * S
        U = arena[:, U_AT:U_AT + 32 * 129].rearrange("p (i n) -> p i n", n=129)
        GT, EMT = small[:, 0:32], small[:, 32:64]
        D_PAIRS = [(h, b) for h in range(HD_DIFF) for b in range(NB)]
        D_P0, D_P1 = [hhf[:, 4], hhf[:, 5], hhf[:, 6]], [hhf[:, 7], hlf[:, 4]]
        D_WT = [hlf[:, 5], hlf[:, 6]]
        D_O, D_ON = T(24), hlf[:, 7]
        D_BIAS, D_JUNK = T(25), small[:, 0:P]
        D_MAX, D_NEG = dsm[:, 0:4], dsm[:, 4:8]
        D_SUM, D_REC = dsm[:, 8:16], dsm[:, 16:24]
        D_MIX = dsm[:, 24:28]
        D_SS, D_LN, D_RS = dsm[:, 32:40], dsm[:, 40:48], dsm[:, 48:56]
        D_BANKS = [(v % 4, 1) if D_PAIRS[v // 2][1] < 4 else (2 * (v % 2), 2) for v in range(2 * len(D_PAIRS))]
        D_BEFORE = [max([u + 1 for u in range(v) if max(D_BANKS[u][0], D_BANKS[v][0])
                         < min(sum(D_BANKS[u]), sum(D_BANKS[v]))], default=0) for v in range(len(D_BANKS))]
        D_STEPS = len(D_PAIRS) + 5

        def d_head_end(s):
            return (s - 12) // NB if s >= 12 and (s - 12) % NB == 0 else None

        SB_UNITS = [(2 * j + i, c, k, max(0, (k - 4 * c) * P)) for j in range(HD_SB // 2) for c in range(2)
                    for i in range(2) for k in range(4 * c + 3, -1, -1)]
        SB_Z = 6
        SB_DIAG = np.cumsum([0] + [k >= 4 * c for hd, c, k, lo in SB_UNITS]).tolist()
        SB_CHAIN_END = [max(u for u, (hd, c, k, lo) in enumerate(SB_UNITS) if 2 * (hd // 2) + c == n) for n in range(8)]
        SB_SUMS = np.cumsum([0] + [(k > 0) * ((k < 4 * c + 3) + (k >= 4 * c)) for hd, c, k, lo in SB_UNITS]).tolist()
        quads = lambda t, f: [t[:, f + i // 2, i % 2 * HALF:(i % 2 + 1) * HALF] for i in range(4)]
        S_MH, S_ML, S_MH_READ, S_CY = quads(hh, 4), quads(hl, 4), quads(hh_read, 4), quads(hhf, 6)
        halves = lambda n: [T(n)[:, 0:HALF], T(n)[:, HALF:S]]
        S_SP, S_M, S_A = halves(0), halves(1), halves(3)
        S_O = T(8, 4).rearrange("p (j t) -> p j t", j=4)
        S_SQ, S_RS, S_T = [T(12), T(13)], [T(14), T(15)], [T(4), T(5)]
        GATED = [(gated[:, b, 0], gated[:, b, 1]) for b in range(2)]
        CG, CV = [T(20), T(21)], [T(22), T(23)]
        NRM2 = NRM1
        ML_SUBS = [(2 * h + c, h, c, k, max(0, (k - 4 * c) * P)) for h in range(HD_ML) for c in range(2)
                   for k in range(4 * c + 4)]
        ML_LAST = [max(s for s, x in enumerate(ML_SUBS) if x[0] == w) for w in range(8)]
        ML_DIAG_OF = [s for s, (w, h, c, k, lo) in enumerate(ML_SUBS) if k >= 4 * c]
        ML_DIAG = {s: i for i, s in enumerate(ML_DIAG_OF)}
        ML_E = np.cumsum([1 + (k >= 4 * c and lo + P < HALF) for w, h, c, k, lo in ML_SUBS]).tolist()
        ML_QUARTERS = [[[s for s in range(ML_LAST[w] + 1) if ML_SUBS[s][0] == w and ML_SUBS[s][3] // (w % 2 + 1) == t]
                        for t in range(4)] for w in range(8)]
        M_E = [hhf[:, 2, 0:HALF], hhf[:, 2, HALF:S]]
        M_D = [hhf[:, 3, 0:P], hhf[:, 3, P:2 * P]]
        M_JUNK, M_SEL = hhf[:, 3, 2 * P:3 * P], hhf[:, 3, HALF:S]
        M_A = [flat(hhf[:, 0:2]).rearrange("p (k t) -> p k t", t=HALF), flat(hlf[:, 0:4]).rearrange("p (k t) -> p k t", t=HALF)]
        ML_N = 8
        L_DEN, L_SUM, L_MU, L_SS = small[:, 64:96], small[:, 96:128], dsm[:, 0:32], dsm[:, 32:64]

        def unit_columns(t, w):
            h, c = w // 2, w % 2
            return t.rearrange("p (b h) -> p b h", h=HD_ML)[:, 4 * c:4 * c + 4, h]

        def unit_rows(w):
            h, c = w // 2, w % 2
            return [4 * (4 * c + t) + h for t in range(4)]

        W_P, W_PT = [T(5), T(6), T(9)], [T(7), T(8)]
        W_SM = [T(10)[:, i * 20:(i + 1) * 20] for i in range(3)]
        W_UNITS = 2 * NB
        W_STEPS = ML_N + W_UNITS + 5
        B_G = [[arena[:, R4 + (2 * r + i) * S:R4 + (2 * r + i + 1) * S] for i in range(2)] for r in range(2)]
        B_T = [[arena[:, U_AT + (2 * r + i) * S:U_AT + (2 * r + i + 1) * S] for i in range(2)] for r in range(2)]

        def ffn_gate(c0, j):
            return c0 + 3 * j - 1

        def ffn_down_last(c0):
            return c0 + 3 * NJ - 1


        def half_of(half):
            return slice(half * HALF, (half + 1) * HALF)

        BY_HALF = [(f, half) for half in range(2) for f in range(KT)]

        @block.sync
        def _(sp):
            sp.dma_start(X1.rearrange("p (f t) -> p f t", f=KT)[:, :, half_of(0)],
                         A.x.rearrange("f p t -> p f t")[:, :, half_of(0)]).then_inc(Z.x_in0, 16)
            for c in range(RAW):
                sp.dma_start(raw[:, c], A.w[c]).then_inc((Z.raw0, Z.raw1)[c], 16)

            def load(c, s, n):
                sp.wait_ge(Z.split_done, n)
                sp.dma_start(raw[:, s], A.w[bass.ds(c, 1)].rearrange("a p n -> p (a n)")).then_inc(
                    (Z.raw0, Z.raw1)[s], 16)

            loops = (N_CHUNKS - RAW) // RAW
            with sp.Fori(0, loops) as i:
                for s in range(RAW):
                    load(i * RAW + (RAW + s), s, i * RAW + (s + 1))
            for c in range(RAW + loops * RAW, N_CHUNKS):
                sp.wait_ge(Z.split_done, c - RAW + 1)
                sp.dma_start(raw[:, c % RAW], A.w[c]).then_inc((Z.raw0, Z.raw1)[c % RAW], 16)

        @block.gpsimd
        def _(pool):
            def split(r, s, loaded, n):
                pool.wait_ge((Z.raw0, Z.raw1)[r], loaded)
                pool.sem_inc(Z.pace, 1)
                pool.tensor_copy(wh[:, s], raw[:, r]).then_inc(Z.wt_hi, 1)
                pool.wait_ge(Z.wt_hi, n + 1)
                pool.tensor_tensor(wl[:, s], raw[:, r], wh[:, s].bitcast(F32), ALU.subtract).then_inc(Z.split_done, 1)

            for c in range(SL):
                split(c % RAW, c % SL, 16 * (c // RAW + 1), c)
            def split_chunks(first, end):
                with pool.Fori(0, (end - first) // (RAW * SL)) as i:
                    for u in range(RAW * SL):
                        c = first + u
                        pool.wait_ge(Z.chunk_done, i * (RAW * SL) + (c - SL + 1))
                        split(c % RAW, c % SL, i * (16 * SL) + 16 * (c // RAW + 1), i * (RAW * SL) + c)

            def s_low(u):
                lo = SB_UNITS[u][3]
                pool.wait_ge(Z.s_mhi, 3 + u + 1)
                if u >= 4:
                    pool.wait_ge(Z.s_c, u - 3)
                pool.tensor_tensor(S_ML[u % 4][:, lo:], S_M[u % 2][:, lo:], S_MH_READ[u % 4][:, lo:], ALU.subtract).then_inc(Z.s_mlo, 1)

            split_chunks(SL, C_WO + SL)
            for u in range(len(SB_UNITS)):
                s_low(u)
            split_chunks(C_WO + SL, N_CHUNKS)
            assert (C_WO + SL - SL) % (RAW * SL) == 0 and (N_CHUNKS - C_WO - SL) % (RAW * SL) == 0

        @block.tensor
        def _(pe):
            def product(out, slot, k, xh, xl, start, stop):
                w = slice(k * P, (k + 1) * P)
                pe.matmul(out, wh[:, slot, w], xh, start=start, stop=False)
                pe.matmul(out, wh[:, slot, w], xl, start=False, stop=False)
                return pe.matmul(out, wl[:, slot, w], xh, start=False, stop=stop)

            def tile(slot, b, x, ready=None):
                for half in range(2):
                    t = half_of(half)
                    for k in range(KT):
                        if ready and half == 0:
                            ready(k)
                        last = product(bank(b + half), slot, k, x[0][k][:, t], x[1][k][:, t], k == 0, k == KT - 1)
                last.then_inc(Z.chunk_done, 1)

            def mean_of_squares(sq_sem, ss_sem, sq, n, f, half, at=6):
                pe.wait_ge(sq_sem, n + 1)
                pe.matmul(bank(at + half), mat("mean"), sq[n % 4], start=(f == 0), stop=(f == KT - 1)).then_inc(ss_sem, 1)

            def norm(use, nrm, half):
                for f in range(KT):
                    mean_of_squares(Z.n_sq, Z.n_ss, nrm.sq, 16 * use + 8 * half + f, f, half)

            def post(use, nrm):
                for i, (f, half) in enumerate(BY_HALF):
                    mean_of_squares(Z.f_sq, Z.f_ss, nrm.sq, 16 * (use // 2) + i, f, half, 0)

            def start(use, nrm, c0, tiles, x):
                norm(use, nrm, 0)
                for half in range(2):
                    for n in range(tiles):
                        if half == 0:
                            pe.wait_ge(Z.split_done, c0 + n + 1)
                        for k in range(KT):
                            if n == 0:
                                pe.wait_ge(Z.n_lo, 16 * use + 8 * half + k + 1)
                            last = product(bank(2 * n + half), (c0 + n) % SL, k, x[0][k][:, half_of(half)],
                                           x[1][k][:, half_of(half)], k == 0, k == KT - 1)
                        if half:
                            last.then_inc(Z.chunk_done, 1)
                        elif n == 0:
                            norm(use, nrm, 1)

            pe.wait_ge(Z.consts, 32)
            pe.wait_ge(Z.lam_p, 1)
            pe.matmul(bank(4)[:, 0:2], mat("mean"), small[:, 64:66], start=True, stop=True).then_inc(Z.lam_ps, 1)

            pe.wait_ge(Z.lam_e, 1)
            start(0, NRM1, C_QKV, 3, SPLIT_H)

            def qkv_loop(first):
                with pe.Fori(0, 2) as i:
                    for u in range(3):
                        n = first + u
                        pe.wait_ge(Z.split_done, i * 3 + (C_QKV + n + 1))
                        pe.wait_ge(Z.q_ev, i * 3 + (n - 2))
                        tile((C_QKV + n) % SL, 2 * (n % 3), SPLIT_H)

            def modulation(g):
                pe.wait_ge(Z.mod_acc, 8 * (g + 1))
                for f in range(8):
                    last = pe.matmul(bank(7)[:, g * 8 + f:g * 8 + f + 1], MOD_ACC[g % 4][:, f * P:(f + 1) * P],
                                     mat("mean")[:, 0:1], start=True, stop=True)
                last.then_inc(Z.mod_ps, 1)

            qkv_loop(3)
            pe.wait_ge(Z.n_ln, 2)
            modulation(0)
            modulation(1)
            qkv_loop(9)
            for h in range(HD_DIFF):
                pe.wait_ge(Z.tb_ready, h + 1)
                if h:
                    pe.wait_ge(Z.e_sb, h)
                pe.matmul(bank(6)[:, 0:ONEHOT_W], T(22)[0:33, h * P:(h + 1) * P], T(23)[0:33, 0:ONEHOT_W],
                          start=True, stop=True).then_inc(Z.e_ps, 1)
            for g in range(2, 6):
                modulation(g)
            pe.wait_ge(Z.mod_col, 1)
            pe.wait_ge(Z.e_sb, 4)

            def v_transposes(n, vt, sem_ev, sem_T, sem_cp):
                for half in range(2):
                    pe.wait_ge(sem_ev, 2 * n + half + 1)
                    if n:
                        pe.wait_ge(sem_cp, 2 * n + half - 1)
                    for b in range(4):
                        t = slice(half * HALF + b * P, half * HALF + (b + 1) * P)
                        last = pe.transpose(bank(6 + half)[:, b * P:(b + 1) * P], vt[:, t], mat("ident"))
                    last.then_inc(sem_T, 1)

            for n in range(15, N_QKV):
                pe.wait_ge(Z.split_done, C_QKV + n + 1)
                if n <= 18:
                    pe.wait_ge(Z.q_ev, n - 2)
                else:
                    pe.wait_ge(Z.vt_ev, 2 * (n - 18))
                tile((C_QKV + n) % SL, 2 * (n % 3), SPLIT_H)
                if n > 16:
                    v_transposes(n - 17, VT1, Z.vt_ev, Z.vT, Z.v_cp)
            v_transposes(7, VT1, Z.vt_ev, Z.vT, Z.v_cp)

            pe.wait_ge(Z.vt_ev, 16)
            pe.wait_ge(Z.v_cp, 16)

            def d_scores(p, m):
                h, b = D_PAIRS[p]
                v = 2 * p + m
                if D_BEFORE[v]:
                    pe.wait_ge(Z.d_exp, D_BEFORE[v])
                w = (b + 1) * P
                r = slice(DH * m, DH * (m + 1))
                for c in range(0, w, HALF):
                    e = min(w, c + HALF)
                    last = pe.matmul(bank(*D_BANKS[v])[:, c:e], T(h)[r, b * P:(b + 1) * P], T(8 + h)[r, c:e],
                                     start=True, stop=True)
                last.then_inc(Z.d_qk, 1)

            def d_transposes(p):
                h, b = D_PAIRS[p]
                pe.wait_ge(Z.d_w, p + 1)
                if p:
                    pe.wait_ge(Z.d_wt, p)
                if d_head_end(p + 1) is not None:
                    pe.wait_ge(Z.d_lo, d_head_end(p + 1) + 1)
                for k in range(b + 1):
                    last = pe.transpose(bank(4, 2)[:, k * P:(k + 1) * P], D_P0[p % 3][:, k * P:(k + 1) * P], mat("ident"))
                last.then_inc(Z.d_T, 1)

            def d_values(p):
                h, b = D_PAIRS[p]
                pe.wait_ge(Z.d_wt, p + 1)
                if p >= 2:
                    pe.wait_ge(Z.d_post, p - 1)
                for k in range(b + 1):
                    last = pe.matmul(bank(6 + p % 2)[:, 0:P], D_WT[p % 2][:, k * P:(k + 1) * P],
                                     V1[:, k, h * P:(h + 1) * P], start=(k == 0), stop=(k == b))
                last.then_inc(Z.d_pv, 1)

            def d_out_transposes(h):
                pe.wait_ge(Z.d_on, h + 1)
                pe.wait_ge(Z.d_wt, min(len(D_PAIRS), NB * h + 11))
                for b in range(NB):
                    last = pe.transpose(bank(4, 2)[:, b * P:(b + 1) * P], D_ON[:, b * P:(b + 1) * P], mat("ident"))
                last.then_inc(Z.d_hT, 1)

            for s in range(D_STEPS):
                if s < len(D_PAIRS):
                    d_scores(s, 0)
                    d_scores(s, 1)
                if 0 <= s - 2 < len(D_PAIRS):
                    d_transposes(s - 2)
                if 0 <= s - 3 < len(D_PAIRS):
                    d_values(s - 3)
                if d_head_end(s) is not None:
                    d_out_transposes(d_head_end(s))

            pe.wait_ge(Z.d_exp, 64)
            pe.wait_ge(Z.d_lo, 4)
            pe.wait_ge(Z.d_post, 32)

            def s_scores(u):
                hd, c, k, lo = SB_UNITS[u]
                if u >= SB_Z:
                    pe.wait_ge(Z.s_a, u - SB_Z + 1)
                r = slice(DH * (hd % 2), DH * (hd % 2) + DH)
                pe.matmul(bank(u % SB_Z)[:, lo:], T(12 + hd // 2)[r, k * P:(k + 1) * P],
                          T(4 + hd // 2)[r, c * HALF + lo:(c + 1) * HALF],
                          start=True, stop=False, skip_group_check=True).then_inc(Z.s_z, 1)

            def s_sums(u):
                hd, c, k, lo = SB_UNITS[u]
                z = bank(u % SB_Z)
                diag, first = k >= 4 * c, k == 4 * c + 3
                neg_tri, neg_ones = masks[:, 2], mat("negones")
                pe.wait_ge(Z.s_mhi, 3 + u + 1)
                if not first:
                    before = SB_UNITS[u - 1][3]
                    pe.wait_ge(Z.s_cy, SB_SUMS[u])
                    pe.matmul(z[:, before:], neg_ones, S_CY[u % 4][:, before:], start=False, stop=False,
                              skip_group_check=True)
                if diag:
                    pe.matmul(z[:, lo:lo + P], masks[:, 0], masks[:, 1], start=False, stop=False, skip_group_check=True)
                pe.matmul(z[:, lo:], neg_tri, S_MH[u % 4][:, lo:], start=False, stop=False, skip_group_check=True)
                pe.wait_ge(Z.s_mlo, u + 1)
                last = pe.matmul(z[:, lo:], neg_tri, S_ML[u % 4][:, lo:], start=False, stop=True, skip_group_check=True)
                last.then_inc(Z.s_c, 1)

            def s_values(u):
                hd, c, k, lo = SB_UNITS[u]
                pe.wait_ge(Z.s_a, u + 1)
                chain = 2 * (hd // 2) + c
                r = DH * (hd % 2)
                first = k == 4 * c + 3
                if first and chain >= 2:
                    pe.wait_ge(Z.s_o, chain - 1)
                pe.matmul(bank(SB_Z + chain % 2)[r:r + DH, lo:], V1[:, k, HD_DIFF * P + hd * DH:HD_DIFF * P + (hd + 1) * DH],
                          S_A[u % 2][:, lo:], start=first, stop=(k == 0), skip_group_check=True).then_inc(Z.s_pv, 1)

            for u in range(len(SB_UNITS) + 5):
                if u < len(SB_UNITS):
                    s_scores(u)
                if 0 <= u - 3 < len(SB_UNITS):
                    s_sums(u - 3)
                if 0 <= u - 5:
                    s_values(u - 5)
            for j in range(4):
                pe.wait_ge(Z.s_sq, j + 1)
                if j == 0:
                    pe.wait_ge(Z.s_a, len(SB_UNITS))
                if j >= 2:
                    pe.wait_ge(Z.s_ln, j - 1)
                for half in range(2):
                    last = pe.matmul(bank(2 * (j % 2) + half), mat("mean64"),
                                     S_SQ[j % 2][:, half * HALF:(half + 1) * HALF], start=True, stop=True)
                last.then_inc(Z.s_ss, 1)

            pe.wait_ge(Z.s_ln, 4)
            pe.wait_ge(Z.s_o, 8)
            pe.wait_ge(Z.d_lo, 4)

            def eight_tiles(c0, use, x, nrm, ready):
                for f in range(KT):
                    pe.wait_ge(Z.split_done, c0 + f + 1)
                    if f >= 3:
                        pe.wait_ge(Z.y_cp, 8 * (use // 2) + f - 2)
                    tile((c0 + f) % SL, 2 * (f % 3), x, ready if f == 0 else None)
                pe.wait_ge(Z.y_sum, (KT - 1) * (use // 2 + 1))
                for half in range(2):
                    pe.matmul(bank(6 + half), mat("mean"), nrm.total[:, half_of(half)], start=True, stop=True).then_inc(Z.y_ss, 1)

            eight_tiles(C_WO, 0, SPLIT_H, NRM1, lambda k: pe.wait_ge(Z.s_lo, k - 3) if k >= 4 else None)

            def ffn(c0, use, x, act, nrm):
                fb = NJ * use
                gate_free = (Z.g_cv, 2) if use == 0 else (Z.g_lin, 1)
                val_free = (Z.v_cv, 2) if use == 0 else (Z.f_prod, 1)
                gate_base, val_base = (0, 0) if use == 0 else (fb, fb)

                def up(j, c):
                    pe.wait_ge(Z.split_done, c + 1)
                    pe.wait_ge(gate_free[0], j * gate_free[1] + gate_base)
                    tile(slot_of[0], 0, x)
                    pe.wait_ge(Z.split_done, c + 2)
                    pe.wait_ge(val_free[0], j * val_free[1] + val_base)
                    tile(slot_of[1], 2, x)

                def down(j, b, c, slot):
                    pe.wait_ge(Z.split_done, c + 1)
                    pe.wait_ge(Z.a_lo, j + (fb + 1))
                    for o in range(16):
                        f, half = o % KT, o // KT
                        pe.wait_ge(Z.dn_free, j * 16 + (16 * fb + o + 1))
                        t = slice(half * HALF, (half + 1) * HALF)
                        last = product(bank(4 + o % 4), slot, f, act[b][0][:, t], act[b][1][:, t], True, True)
                        last.then_inc(Z.dn_done if o < 15 else Z.chunk_done, 1)

                start(1 + 2 * use, nrm, c0, 2, x)
                pe.wait_ge(Z.n_ln, 4 + 4 * use)
                slot_of = [(c0 + 2) % SL, (c0 + 3) % SL]
                down_slot = (c0 + 4) % SL
                with pe.Fori(0, (NJ - 2) // 2) as i:
                    for u in range(2):
                        j = i * 2 + (1 + u)
                        c = i * 6 + (c0 + 2 + 3 * u)
                        up(j, c)
                        down(i * 2 + u, u, c + 2, down_slot)
                up(NJ - 1, ffn_gate(c0, NJ - 1))
                down(NJ - 2, 0, ffn_gate(c0, NJ - 1) + 2, down_slot)
                down(NJ - 1, 1, ffn_down_last(c0), ffn_down_last(c0) % SL)

            pe.wait_ge(Z.y_cp, 8)
            ffn(C_FFN1, 0, SPLIT_H, GATED, NRM1)
            post(1, NRM1)

            pe.wait_ge(Z.f_ln, 4)
            pe.wait_ge(Z.dn_free, 4 + 16 * NJ)
            start(2, NRM1, C_IN, 3, SPLIT_H)
            pe.wait_ge(Z.n_ln, 6)
            for n in range(5):
                v_transposes(8 + n, RING[n % 2][0], Z.vt_ev, Z.vT, Z.v_cp)
                if n + 3 < 6:
                    pe.wait_ge(Z.split_done, C_IN + n + 4)
                    tile((C_IN + n + 3) % SL, 2 * (n % 3), SPLIT_H)
            with pe.Fori(0, (N_IN - 6) // 3) as i:
                for u in range(3):
                    n = 6 + u
                    pe.wait_ge(Z.split_done, i * 3 + (C_IN + n + 1))
                    pe.wait_ge(Z.if_ev, i * 3 + (n - 2))
                    tile((C_IN + n) % SL, 2 * u, SPLIT_H)

            pe.wait_ge(Z.if_ev, N_IN)
            pe.wait_ge(Z.m_sel, 1)
            pe.wait_ge(Z.if_act, 4)
            for h in range(HD_ML):
                for half in range(2):
                    i = 2 * h + half
                    if i >= 2:
                        pe.wait_ge(Z.m_mbc, i - 1)
                    pe.matmul(bank(i % 2), M_SEL[32:36, h * P:(h + 1) * P], ROW1[32:36, half * HALF:(half + 1) * HALF],
                              start=True, stop=True).then_inc(Z.m_mb, 1)
            for b in range(NB):
                pe.matmul(bank(2)[:, b * 4:b * 4 + 4], ROW1[0:4, b * P:(b + 1) * P], mat("ident")[0:4, 0:4],
                          start=True, stop=True)
                last = pe.matmul(bank(3)[:, b * 4:b * 4 + 4], ROW2[32:36, b * P:(b + 1) * P],
                                 mat("ident")[32:36, 32:36], start=True, stop=True)
            last.then_inc(Z.m_tp, 1)
            pe.wait_ge(Z.m_mbc, 8)
            pe.wait_ge(Z.m_tpc, 2)

            def m_scores(s):
                w, h, c, k, lo = ML_SUBS[s]
                if s >= 4:
                    pe.wait_ge(Z.m_A, s - 3)
                pe.matmul(bank(s % 4)[:, lo:], T(9 + h)[:, k * P:(k + 1) * P], T(5 + h)[:, c * HALF + lo:(c + 1) * HALF],
                          start=True, stop=True).then_inc(Z.m_S, 1)

            def m_values(w, t):
                h, c, i = w // 2, w % 2, 4 * w + t
                if t == 0:
                    pe.wait_ge(Z.m_A, ML_LAST[w] + 1)
                if i >= 3:
                    pe.wait_ge(Z.m_U, 2 * (i - 2))
                for k in range(4 * c + t + 1):
                    last = pe.matmul(bank(4 + i % 3)[:, 0:129], M_A[w % 2][:, k, t * P:(t + 1) * P],
                                     V2[:, k, P + h * 129:P + (h + 1) * 129], start=(k == 0), stop=(k == 4 * c + t))
                last.then_inc(Z.m_pv, 1)

            def l_transposes(w):
                pe.wait_ge(Z.l_y, 4 * (w + 1))
                if w:
                    pe.wait_ge(Z.l_g, w)
                for t, i in enumerate(unit_rows(w)):
                    last = pe.transpose(bank(7)[:, t * P:(t + 1) * P], U[:, i, 0:P], mat("ident"))
                last.then_inc(Z.l_T, 1)

            def w_scores(u):
                n, g = u // 2, u % 2
                if u >= 2:
                    pe.wait_ge(Z.w_a, 5 * (u - 2) + 1)
                r = slice(DH * g, DH * (g + 1))
                a = 0 if n else P
                for j in range(4):
                    last = pe.matmul(bank(2 * (u % 2), 2)[:, j * 256 + a:(j + 1) * 256], T(j)[r, n * P:(n + 1) * P],
                                     T(4)[r, (n - 1) * P + a:(n + 1) * P], start=True, stop=True)
                last.then_inc(Z.w_qk, 1)

            def w_transposes(u):
                n = u // 2
                pe.wait_ge(Z.w_pn, u + 1)
                if u:
                    pe.wait_ge(Z.w_pt, u)
                for j in range(4):
                    for k in range(0 if n else 1, 2):
                        i = 2 * j + k
                        last = pe.transpose(bank(4, 2)[:, i * P:(i + 1) * P], W_P[u % 3][:, i * P:(i + 1) * P], mat("ident"))
                last.then_inc(Z.w_T, 1)

            def w_values(u):
                n, g = u // 2, u % 2
                pe.wait_ge(Z.w_pt, u + 1)
                if n >= 2 and g == 0:
                    pe.wait_ge(Z.w_lo, n - 1)
                for j in range(4):
                    for k in range(0 if n else 1, 2):
                        i = 2 * j + k
                        last = pe.matmul(bank(6 + n % 2)[DH * g:DH * (g + 1), j * P:(j + 1) * P],
                                         V2[:, n - 1 + k, DH * g:DH * (g + 1)], W_PT[u % 2][:, i * P:(i + 1) * P],
                                         start=(k == (0 if n else 1)), stop=(k == 1))
                last.then_inc(Z.w_pv, 1)

            for s in range(W_STEPS):
                u = s - ML_N
                for t in range(4):
                    if s < ML_N:
                        for i in ML_QUARTERS[s][t]:
                            m_scores(i)
                    if 0 <= s - 1 < ML_N:
                        m_values(s - 1, t)
                if 0 <= u < W_UNITS:
                    if u == 0:
                        pe.wait_ge(Z.m_A, len(ML_SUBS))
                    w_scores(u)
                if 0 <= u - 2 < W_UNITS:
                    if u == 2:
                        pe.wait_ge(Z.m_U, 8 * ML_N)
                    w_transposes(u - 2)
                if 0 <= u - 3 < W_UNITS:
                    if u == 5:
                        pe.wait_ge(Z.l_g, ML_N)
                    w_values(u - 3)
                if 0 <= s - 5 < ML_N:
                    l_transposes(s - 5)

            pe.wait_ge(Z.l_lo, ML_N)
            for f in range(KT):
                pe.wait_ge(Z.split_done, C_BR + f + 1)
                if f == 1:
                    pe.wait_ge(Z.w_pt, W_UNITS)
                if f >= 2:
                    pe.wait_ge(Z.b_m, f - 1)
                for part in (1, 0):
                    if f == 0 and part == 0:
                        pe.wait_ge(Z.w_lo, NB)
                    for half in range(2):
                        t = half_of(half)
                        for k in range(4 * part, 4 * part + 4):
                            last = product(bank(4 * (f % 2) + 2 * part + half), (C_BR + f) % SL, k,
                                           hh[:, k, t], hl[:, k, t], k == 4 * part, k == 4 * part + 3)
                last.then_inc(Z.chunk_done, 1)

            pe.wait_ge(Z.b_lo, 8)
            eight_tiles(C_OUT, 2, SPLIT_A, HL_TMP, None)
            pe.wait_ge(Z.y_cp, 16)
            ffn(C_FFN2, 1, SPLIT_A, GATED, HL_TMP)
            post(3, NRM2)

        @block.scalar
        def _(act):
            def square(src, dst, sem):
                act.activation(dst, src, ACT.Square).then_inc(sem, 1)

            def inverse_root(src, dst, ln_sem, sem, n, scale=1.0):
                act.activation(dst, src, ACT.Ln, bias=col("eps"), scale=scale).then_inc(ln_sem, 1)
                act.wait_ge(ln_sem, n + 1)
                act.activation(dst, dst, ACT.Exp, scale=-0.5).then_inc(sem, 1)

            def norm(use, src, ready, nrm, split, shift):
                for i, (f, half) in enumerate(BY_HALF):
                    n, t = 16 * use + i, half_of(half)
                    ready(f, half)
                    if i >= 4:
                        act.wait_ge(Z.n_ss, n - 3)
                    square(src[f][:, t], nrm.sq[n % 4], Z.n_sq)
                    if f < KT - 1:
                        continue
                    act.wait_ge(Z.n_ss, n + 1)
                    inverse_root(bank(6 + half), nrm.rstd[half], Z.n_ln, Z.n_rstd, 2 * use + half)
                    for k in range(KT):
                        n = 16 * use + 8 * half + k
                        act.wait_ge(Z.n_t, n + 1)
                        if shift is None:
                            act.activation(split[0][k][:, t], nrm.tmp[n % 4], ACT.Copy).then_inc(Z.n_hi, 1)
                        else:
                            act.activation(split[0][k][:, t], nrm.tmp[n % 4], ACT.Identity,
                                           bias=modc[:, shift + k:shift + k + 1]).then_inc(Z.n_hi, 1)

            def post_roots(use, nrm, ss_sem, n, at):
                for half in range(2):
                    act.wait_ge(ss_sem, n[half])
                    inverse_root(bank(at + half), nrm.rstd[half], Z.f_ln, Z.f_rstd, 2 * use + half)

            def post(use, y, ready, nrm):
                for i, (f, half) in enumerate(BY_HALF):
                    n = 16 * (use // 2) + i
                    ready(f, half)
                    if i >= 4:
                        act.wait_ge(Z.f_ss, n - 3)
                    square(y[f][:, half_of(half)], nrm.sq[n % 4], Z.f_sq)
                post_roots(use, nrm, Z.f_ss, [16 * (use // 2) + 8, 16 * (use // 2) + 16], 0)

            def projected(c0, use, y, nrm):
                u = use // 2
                for f in range(KT):
                    act.wait_ge(Z.chunk_done, c0 + f + 1)
                    act.activation(y[f], bank(2 * (f % 3), 2), ACT.Copy).then_inc(Z.y_cp, 1)
                    act.wait_ge(Z.y_cp, 8 * u + f + 1)
                    if f >= 2:
                        act.wait_ge(Z.y_sum, (KT - 1) * u + max(1, f - 2))
                    square(y[f], nrm.whole[f % 2], Z.y_sq)
                post_roots(use, nrm, Z.y_ss, [2 * u + 1, 2 * u + 2], 6)

            act.preload_act_table_set("natural_log_exp_and_others")
            act.dma_start(cols[:], A.cols).then_inc(Z.consts, 16)
            act.dma_start(mats[:], A.mats).then_inc(Z.consts, 16)
            x_tiles = X1.rearrange("p (f t) -> p f t", f=KT)
            act.dma_start(x_tiles[:, :, half_of(1)], A.x.rearrange("f p t -> p f t")[:, :, half_of(1)]).then_inc(Z.x_in1, 16)
            act.dma_start(T(23)[0:33, 0:ONEHOT_W], A.onehot).then_inc(Z.tab, 16)
            act.dma_start(T(23)[0:32, 512:516], A.table).then_inc(Z.tab, 16)
            act.dma_start(T(23)[0:32, 516:520], A.table31).then_inc(Z.tab, 16)
            act.wait_ge(Z.consts, 32)
            act.wait_ge(Z.lam_ps, 1)
            act.activation(small[:, 66:68], bank(4)[:, 0:2], ACT.Exp, scale=float(D)).then_inc(Z.lam_e, 1)
            norm(0, [T(8 + f) for f in range(KT)],
                 lambda f, half: act.wait_ge((Z.x_in0, Z.x_in1)[half], 16), NRM1, SPLIT_H, None)

            def mod_load(i):
                g, k = i // 8, i % 8
                if i >= 4:
                    act.wait_ge(Z.mod_acc, i - 3)
                else:
                    act.wait_ge(Z.n_lo, 16)
                act.dma_start(T(16 + i % 4), A.w_ada[k, :, g * 1024:(g + 1) * 1024]).then_inc(
                    (Z.mod_in0, Z.mod_in1, Z.mod_in2, Z.mod_in3)[i % 4], 16)

            for n in range(16):
                for i in range(4 * n, min(48, 4 * n + 4)):
                    mod_load(i)
                act.wait_ge(Z.chunk_done, C_QKV + n + 1)
                if n < 8:
                    act.activation(T(n), bank(2 * (n % 3), 2), ACT.Copy, scale=DH ** -0.5).then_inc(Z.q_ev, 1)
                else:
                    act.activation(T(n), bank(2 * (n % 3), 2), ACT.Copy).then_inc(Z.q_ev, 1)
                if n == 12:
                    for h in range(HD_DIFF):
                        act.wait_ge(Z.e_ps, h + 1)
                        if h >= 1:
                            act.wait_ge(Z.e_out, 16 * h)
                        act.activation(T(23)[:, 520:520 + ONEHOT_W], bank(6)[:, 0:ONEHOT_W], ACT.Copy).then_inc(Z.e_sb, 1)
                        act.wait_ge(Z.e_sb, h + 1)
                        act.dma_start(e_dram[h], T(23)[:, 520:520 + ONEHOT_W]).then_inc(Z.e_out, 16)
            act.wait_ge(Z.mod_ps, 4)
            act.wait_ge(Z.e_out, 64)
            for h in range(HD_DIFF):
                act.dma_start(D_BIAS[:, h * 256:(h + 1) * 256],
                              bass.AP(e_dram.tensor, h * P * ONEHOT_W + 127, [[ONEHOT_W - 1, P], [1, 256]])).then_inc(Z.bias_in, 16)
            for n in range(8):
                act.wait_ge(Z.chunk_done, C_QKV + 16 + n + 1)
                for half in range(2):
                    if n:
                        act.wait_ge(Z.vT, 2 * n + half - 1)
                    t = slice(half * HALF, (half + 1) * HALF)
                    act.activation(VT1[:, t], bank(2 * ((16 + n) % 3) + half), ACT.Copy).then_inc(Z.vt_ev, 1)
            act.wait_ge(Z.chunk_done, C_WO)

            def d_exps(p):
                h, b = D_PAIRS[p]
                w = (b + 1) * P
                for m in range(2):
                    v = 2 * p + m
                    act.wait_ge(Z.d_nmx, v + 1)
                    if m == 0 and p >= 3:
                        act.wait_ge(Z.d_T, p - 2)
                    if m == 1 and p >= 2:
                        act.wait_ge(Z.d_w, p - 1)
                    dst = D_P0[p % 3] if m == 0 else D_P1[p % 2]
                    i, j = 2 * (p % 2) + m, 2 * (p % 4) + m
                    act.activation(dst[:, 0:w], bank(*D_BANKS[v])[:, 0:w], ACT.Exp,
                                   bias=D_NEG[:, i:i + 1], accum_out=D_SUM[:, j:j + 1]).then_inc(Z.d_exp, 1)

            def d_copy(p):
                w = (D_PAIRS[p][1] + 1) * P
                act.wait_ge(Z.d_T, p + 1)
                if p >= 2:
                    act.wait_ge(Z.d_pv, p - 1)
                act.activation(D_WT[p % 2][:, 0:w], bank(4, 2)[:, 0:w], ACT.Copy).then_inc(Z.d_wt, 1)

            def d_output(p):
                h, b = D_PAIRS[p]
                act.wait_ge(Z.d_pv, p + 1)
                if b == 0 and h:
                    act.wait_ge(Z.d_on, h)
                o, rec = bank(6 + p % 2)[:, 0:P], D_REC[:, 2 * (p % 4):2 * (p % 4) + 1]
                act.activation(D_O[:, b * P:(b + 1) * P], o, ACT.Copy, scale=rec)
                if p:
                    act.wait_ge(Z.d_post, p)
                act.activation(D_JUNK, o, ACT.Square, scale=rec, accum_out=D_SS[:, b:b + 1]).then_inc(Z.d_post, 1)
                if b == NB - 1:
                    act.wait_ge(Z.d_post, p + 1)
                    act.activation(D_LN, D_SS, ACT.Ln, bias=col("eps"), scale=1.0 / P).then_inc(Z.d_rs, 1)
                    act.wait_ge(Z.d_rs, 2 * h + 1)
                    act.activation(D_RS, D_LN, ACT.Exp, scale=-0.5).then_inc(Z.d_rs, 1)

            def d_high(h):
                act.wait_ge(Z.d_hT, h + 1)
                act.activation(hh[:, h], bank(4, 2), ACT.Copy, scale=foldc[:, 0:1]).then_inc(Z.d_hi, 1)

            for s in range(D_STEPS):
                if s < len(D_PAIRS):
                    d_exps(s)
                if 0 <= s - 2 < len(D_PAIRS):
                    d_copy(s - 2)
                if 0 <= s - 3 < len(D_PAIRS):
                    d_output(s - 3)
                if d_head_end(s) is not None:
                    d_high(d_head_end(s))

            act.wait_ge(Z.d_on, HD_DIFF)
            for i, name in enumerate(("ident", "negstrict", "negtri")):
                act.activation(masks[:, i], mat(name), ACT.Copy).then_inc(Z.s_mhi, 1)

            def s_logs(u):
                hd, c, k, lo = SB_UNITS[u]
                act.wait_ge(Z.s_capped, u + 1)
                act.activation(S_SP[u % 2][:, lo:], S_SP[u % 2][:, lo:], ACT.Exp).then_inc(Z.s_L, 1)
                act.wait_ge(Z.s_L, 2 * u + 1)
                act.activation(S_SP[u % 2][:, lo:], S_SP[u % 2][:, lo:], ACT.Ln, bias=1.0).then_inc(Z.s_L, 1)

            def s_high(u):
                lo = SB_UNITS[u][3]
                act.wait_ge(Z.s_m, u + 1)
                if u >= 4:
                    act.wait_ge(Z.s_c, u - 3)
                act.activation(S_MH[u % 4][:, lo:], S_M[u % 2][:, lo:], ACT.Copy).then_inc(Z.s_mhi, 1)

            def s_weights(u):
                hd, c, k, lo = SB_UNITS[u]
                act.wait_ge(Z.s_c, u + 1)
                if u >= 2:
                    act.wait_ge(Z.s_pv, u - 1)
                act.activation(S_A[u % 2][:, lo:], bank(u % SB_Z)[:, lo:], ACT.Exp).then_inc(Z.s_a, 1)

            def s_output(chain):
                act.wait_ge(Z.s_pv, SB_CHAIN_END[chain] + 1)
                j, c = chain // 2, chain % 2
                act.activation(S_O[:, j, c * HALF:(c + 1) * HALF], bank(SB_Z + chain % 2), ACT.Copy).then_inc(Z.s_o, 1)

            done = 0
            for u in range(len(SB_UNITS) + 7):
                if 0 <= u - 4 < len(SB_UNITS):
                    s_weights(u - 4)
                if u < len(SB_UNITS):
                    s_logs(u)
                if 0 <= u - 1 < len(SB_UNITS):
                    s_high(u - 1)
                while done < 8 and SB_CHAIN_END[done] <= u - 6:
                    s_output(done)
                    done += 1
            assert done == 8
            for j in range(4):
                act.wait_ge(Z.s_o, 2 * (j + 1))
                if j >= 2:
                    act.wait_ge(Z.s_ss, j - 1)
                if j < 2:
                    act.wait_ge(Z.s_pv, len(SB_UNITS))
                act.activation(S_SQ[j % 2], S_O[:, j], ACT.Square).then_inc(Z.s_sq, 1)

            for j in range(4):
                act.wait_ge(Z.s_ss, j + 1)
                if j >= 2:
                    act.wait_ge(Z.s_lo, j - 1)
                inverse_root(bank(2 * (j % 2), 2), S_RS[j % 2], Z.s_ln, Z.s_rs, j)
                act.wait_ge(Z.s_t, j + 1)
                act.activation(hh[:, 4 + j], S_T[j % 2], ACT.Copy).then_inc(Z.s_hi, 1)

            act.wait_ge(Z.s_lo, 4)
            act.dma_start(x_tiles, A.x.rearrange("f p t -> p f t")).then_inc(Z.x_re, 16)

            Y1t, X1t = [T(f) for f in range(KT)], [T(8 + f) for f in range(KT)]
            projected(C_WO, 0, Y1t, NRM1)

            def residual(use):
                return lambda f, half: act.wait_ge(Z.f_x, 16 * use + 8 * half + f + 1)

            def down_sum(use):
                return lambda f, half: act.wait_ge(Z.dn_free, 4 + 16 * (NJ * (use + 1) - 1) + 8 * half + f + 1)

            norm(1, X1t, residual(0), NRM1, SPLIT_H, None)

            def pace(sem, value):
                act.wait_ge(sem, value)
                act.sem_inc(Z.pace, 1)

            def conv_col(j, r):
                o = COLS["conv1"][0] + r
                if isinstance(j, int):
                    return cols[:, o + 8 * j:o + 8 * j + 1]
                return cols[:, bass.ds(j * 8 + o, 1)]

            def ffn1_step(j, b, first, c):
                pace(Z.chunk_done, c + 1)
                if not first:
                    pace(Z.f_prod, j - 1)
                act.activation(CG[b], bank(0, 2), ACT.Identity, bias=conv_col(j, 3), scale=conv_col(j, 2)).then_inc(Z.g_lin, 1)
                pace(Z.g_cv, j * 2 + 2)
                act.activation(CG[b], CG[b], ACT.Gelu_apprx_tanh).then_inc(Z.g_act, 1)
                pace(Z.chunk_done, c + 2)
                if not first:
                    pace(Z.a_lo, j - 1)
                act.activation(CV[b], bank(2, 2), ACT.Identity, bias=conv_col(j, 7), scale=conv_col(j, 6)).then_inc(Z.v_lin, 1)
                pace(Z.f_prod, j + 1)
                act.activation(GATED[b][0], CV[b], ACT.Copy).then_inc(Z.a_hi, 1)

            ffn1_step(0, 0, True, C_FFN1)
            ffn1_step(1, 1, True, ffn_gate(C_FFN1, 1))
            with act.Fori(0, (NJ - 2) // 2) as i:
                for u in range(2):
                    ffn1_step(i * 2 + (2 + u), u, False, i * 6 + ffn_gate(C_FFN1, 2 + u))
            act.preload_act_table_set("natural_log_exp_and_others")
            post(1, Y1t, down_sum(0), NRM1)
            norm(2, X1t, residual(1), NRM1, SPLIT_H, 0)
            act.wait_ge(Z.f_x, 32)
            act.dma_start(x2_dram, T(8, 8)).then_inc(Z.spill, 16)

            act.dma_start(ROW2.bitcast(I32), A.positions).then_inc(Z.pos_in, 16)

            def ring_free(n):
                if n < 2:
                    return
                o = n - 2
                if o < 5:
                    act.wait_ge(Z.vT, 16 + 2 * (o + 1))
                elif 6 <= o < 14:
                    act.wait_ge(Z.cv_done, o - 5)
                elif 14 <= o < 19:
                    act.wait_ge(Z.rope_done, o - 13)
                elif o >= 19:
                    act.wait_ge((Z.sg_out0, Z.sg_out1)[o % 2], 16 * ((o - 19) // 2 + 1))

            def finish_conv(n):
                act.wait_ge(Z.cv_t, 3 * (n - 5))
                act.sem_inc(Z.if_ev, 1)
                act.activation(T(5 + n - 6), RING[n % 2][0], ACT.Silu).then_inc(Z.cv_done, 1)

            for n in range(N_IN):
                pair = bank(2 * (n % 3), 2)
                r = RING[n % 2]
                if 7 <= n < 15:
                    finish_conv(n - 1)
                ring_free(n)
                act.wait_ge(Z.chunk_done, C_IN + n + 1)
                if n < 5:
                    for half in range(2):
                        t = slice(half * HALF, (half + 1) * HALF)
                        last = act.activation(r[0][:, t], pair[:, t], ACT.Copy)
                        last.then_inc(Z.vt_ev, 1)
                    act.wait_ge(Z.vt_ev, 16 + 2 * (n + 1))
                    act.sem_inc(Z.if_ev, 1)
                elif n == 5:
                    act.wait_ge(Z.trig, 14)
                    act.activation(ROW1[0:4, :], pair[0:4, :], ACT.Identity, bias=col("b_if")[0:4, :]).then_inc(Z.if_ch, 1)
                    act.activation(ROW1[32:36, :], pair[32:36, :], ACT.Identity, bias=col("b_if")[32:36, :]).then_inc(Z.if_ev, 1)
                elif n < 14:
                    o = 5 * (n - 6)
                    act.activation(r[0], pair, ACT.Identity, bias=col("mconv", o + 4), scale=col("mconv", o + 3)).then_inc(Z.cv_lin, 1)
                elif n < 19:
                    act.activation(r[0], pair, ACT.Copy, scale=DH ** -0.5 if n < 18 else 1.0).then_inc(Z.if_ev, 1)
                    act.wait_ge(Z.if_ev, n + 1)
                    for q in range(4):
                        o = 32 * (q ^ 1)
                        act.dma_start(r[1][32 * q:32 * q + 32, :], r[0][o:o + 32, :]).then_inc((Z.rope_sw0, Z.rope_sw1)[n % 2], 16)
                else:
                    act.activation(r[0], pair, ACT.Sigmoid).then_inc(Z.if_ev, 1)
                    act.wait_ge(Z.if_ev, n + 1)
                    act.dma_start(sg_dram[n - 19], r[0]).then_inc((Z.sg_out0, Z.sg_out1)[n % 2], 16)
                if n == 3:
                    act.wait_ge(Z.trig, 14)
                    act.activation(SIN, SIN, ACT.Sin, scale=col("sgn")).then_inc(Z.trig_sin, 1)
                    act.activation(COS, COS, ACT.Sin).then_inc(Z.trig_sin, 1)
                if n == 5:
                    act.wait_ge(Z.if_ch, 2)
                    act.activation(ROW2[32:36, :], ROW2[32:36, :], ACT.Exp, scale=-1.0).then_inc(Z.if_act, 1)
                    act.wait_ge(Z.if_act, 1)
                    act.activation(ROW2[32:36, :], ROW2[32:36, :], ACT.Ln, bias=1.0).then_inc(Z.if_act, 1)
                if n == 7:
                    act.wait_ge(Z.if_ch, 6)
                    act.activation(ROW2[32:36, :], ROW2[0:4, :], ACT.Copy).then_inc(Z.if_act, 1)
                if n == 9:
                    act.wait_ge(Z.if_ch, 7)
                    act.activation(ROW2[32:36, :], ROW2[32:36, :], ACT.Exp, scale=-1.0).then_inc(Z.if_act, 1)

            act.preload_act_table_set("natural_log_exp_and_others")
            for i in range(8):
                act.wait_ge(Z.m_mb, i + 1)
                if i == 0:
                    act.wait_ge(Z.sg_out0, 160)
                    act.wait_ge(Z.sg_out1, 160)
                act.activation(NEGMB[:, i // 2, (i % 2) * HALF:(i % 2 + 1) * HALF], bank(i % 2), ACT.Copy).then_inc(Z.m_mbc, 1)
            act.wait_ge(Z.m_tp, 1)
            act.activation(GT, bank(2)[:, 0:32], ACT.Copy).then_inc(Z.m_tpc, 1)
            act.activation(EMT, bank(3)[:, 0:32], ACT.Copy).then_inc(Z.m_tpc, 1)
            act.wait_ge(Z.m_mbc, 8)
            act.wait_ge(Z.m_tpc, 2)

            def m_weights(steps):
                for s in steps:
                    w, h, c, k, lo = ML_SUBS[s]
                    if s >= 2:
                        act.wait_ge(Z.m_A, s - 1)
                    e = M_E[s % 2]
                    g = GT[:, 4 * k + h:4 * k + h + 1]
                    if k >= 4 * c:
                        act.wait_ge(Z.m_d, ML_DIAG[s] + 1)
                        last = act.activation(e[:, lo:lo + P], M_D[ML_DIAG[s] % 2], ACT.Exp, bias=g)
                        if lo + P < HALF:
                            last.then_inc(Z.m_E, 1)
                            last = act.activation(e[:, lo + P:], NEGMB[:, h, c * HALF + lo + P:(c + 1) * HALF], ACT.Exp, bias=g)
                    else:
                        last = act.activation(e[:, :], NEGMB[:, h, c * HALF:(c + 1) * HALF], ACT.Exp, bias=g)
                    last.then_inc(Z.m_E, 1)

            def m_gate(h):
                act.wait_ge(Z.m_E, ML_E[ML_LAST[2 * h + 1]])
                act.dma_start(NEGMB[:, h], sg_dram[h]).then_inc((Z.so_in0, Z.so_in1, Z.so_in2, Z.so_in3)[h], 16)

            def m_outputs(w, t):
                i = unit_rows(w)[t]
                act.wait_ge(Z.m_pv, 4 * w + t + 1)
                b = bank(4 + (4 * w + t) % 3)
                act.activation(U[:, i, 0:P], b[:, 0:P], ACT.Copy, accum_out=L_SUM[:, i:i + 1]).then_inc(Z.m_U, 1)
                act.activation(L_DEN[:, i:i + 1], b[:, P:P + 1], ACT.Copy).then_inc(Z.m_U, 1)

            def l_squares(w):
                act.wait_ge(Z.l_mu, w + 1)
                for t, i in enumerate(unit_rows(w)):
                    if w or t:
                        act.wait_ge(Z.l_sq, 4 * w + t)
                    act.activation(M_JUNK, U[:, i, 0:P], ACT.Square, bias=L_MU[:, i:i + 1], accum_out=L_SS[:, i:i + 1]).then_inc(Z.l_sq, 1)

            def l_roots(w):
                v = unit_columns(L_SS, w)
                act.wait_ge(Z.l_v, 2 * (w + 1))
                act.activation(v, v, ACT.Ln, bias=col("eps"), scale=1.0 / P).then_inc(Z.l_rs, 1)
                act.wait_ge(Z.l_rs, 2 * w + 1)
                act.activation(v, v, ACT.Exp, scale=-0.5).then_inc(Z.l_rs, 1)

            def l_high(w):
                h, c = w // 2, w % 2
                act.wait_ge(Z.l_g, w + 1)
                act.activation(hh[:, 4 + h, half_of(c)], NEGMB[:, h, half_of(c)], ACT.Copy).then_inc(Z.l_hi, 1)

            def w_exps(u):
                n = u // 2
                a = 0 if n else P
                sm = W_SM[u % 3]
                act.wait_ge(Z.w_a, 5 * u + 5)
                for j in range(4):
                    act.activation(W_P[u % 3][:, j * 256 + a:(j + 1) * 256], W_P[u % 3][:, j * 256 + a:(j + 1) * 256], ACT.Exp,
                                   bias=sm[:, 4 + j:5 + j], accum_out=sm[:, 12 + j:13 + j]).then_inc(Z.w_exp, 1)
                act.activation(sm[:, 8:12], sm[:, 8:12], ACT.Exp).then_inc(Z.w_exp, 1)

            def w_copy(u):
                n = u // 2
                act.wait_ge(Z.w_T, u + 1)
                if u >= 2:
                    act.wait_ge(Z.w_pv, u - 1)
                if n:
                    act.activation(W_PT[u % 2], bank(4, 2), ACT.Copy).then_inc(Z.w_pt, 1)
                else:
                    v = lambda t: t.rearrange("p (j k q) -> p j k q", j=4, k=2)[:, :, 1, :]
                    act.activation(v(W_PT[u % 2]), v(bank(4, 2)), ACT.Copy).then_inc(Z.w_pt, 1)

            def w_high(n):
                act.wait_ge(Z.w_pv, 2 * n + 2)
                act.activation(hh[:, 0:4, n * P:(n + 1) * P], bank(6 + n % 2).rearrange("p (j q) -> p j q", j=4), ACT.Copy).then_inc(Z.w_hi, 1)

            for s in range(W_STEPS):
                u = s - ML_N
                for t in range(4):
                    if s < ML_N:
                        m_weights(ML_QUARTERS[s][t])
                    if t and 0 <= s - 1 < ML_N:
                        m_outputs(s - 1, t - 1)
                if 0 <= s - 1 < ML_N:
                    m_outputs(s - 1, 3)
                if 0 <= u - 2 < W_UNITS:
                    w_copy(u - 2)
                if 0 <= u < W_UNITS:
                    w_exps(u)
                if u >= 5 and u % 2 == 1:
                    w_high((u - 5) // 2)
                if s >= 2 and s % 2 == 0 and s <= ML_N:
                    m_gate(s // 2 - 1)
                if 0 <= s - 3 < ML_N:
                    l_squares(s - 3)
                if 0 <= s - 4 < ML_N:
                    l_roots(s - 4)
                if 0 <= s - 6 < ML_N:
                    l_high(s - 6)

            def gates_load(f):
                if f >= 2:
                    act.wait_ge(Z.b_m, f - 1)
                act.dma_start(B_G[f % 2][0], sg_dram[4 + f]).then_inc((Z.gate0, Z.gate1)[f % 2], 16)
                act.dma_start(B_G[f % 2][1], sg_dram[12 + f]).then_inc((Z.gate0, Z.gate1)[f % 2], 16)

            act.wait_ge(Z.l_lo, ML_N)
            gates_load(0)
            gates_load(1)
            for f in range(KT):
                if f + 2 < KT:
                    gates_load(f + 2)
                act.wait_ge(Z.b_s, f + 1)
                act.activation(SPLIT_A[0][f], B_T[f % 2][0], ACT.Copy).then_inc(Z.b_hi, 1)
            act.wait_ge(Z.chunk_done, C_OUT)
            act.dma_start(hhf[:].rearrange("p f t -> p (f t)"), x2_dram).then_inc(Z.x2_in, 16)
            Y2t, X2t = [T(16 + f) for f in range(KT)], [hhf[:, f] for f in range(KT)]
            projected(C_OUT, 2, Y2t, HL_TMP)
            norm(3, X2t, residual(2), HL_TMP, SPLIT_A, 24)

            def ffn2_step(j, b, first, c):
                pace(Z.chunk_done, c + 1)
                if not first:
                    pace(Z.f_prod, j + (NJ - 1))
                act.activation(CG[b], bank(0, 2), ACT.Silu).then_inc(Z.g_lin, 1)
                pace(Z.f_prod, j + (NJ + 1))
                act.activation(GATED[b][0], CV[b], ACT.Copy).then_inc(Z.a_hi, 1)

            ffn2_step(0, 0, True, C_FFN2)
            ffn2_step(1, 1, True, ffn_gate(C_FFN2, 1))
            with act.Fori(0, (NJ - 2) // 2) as i:
                for u in range(2):
                    ffn2_step(i * 2 + (2 + u), u, False, i * 6 + ffn_gate(C_FFN2, 2 + u))
            act.preload_act_table_set("natural_log_exp_and_others")
            post(3, [hlf[:, f] for f in range(KT)], down_sum(1), NRM2)
            for half in range(2):
                for f in range(0, KT, 4):
                    act.wait_ge(Z.f_x, 48 + 8 * half + f + 4)
                    act.dma_start(A.out.rearrange("f p t -> p f t")[:, f:f + 4, half_of(half)],
                                  hhf[:, f:f + 4, half_of(half)]).then_inc(Z.out_d, 16)
            act.wait_ge(Z.out_d, 64)

        @block.vector
        def _(dve):
            def norm(use, src, gain, nrm, split, shift, half):
                t = half_of(half)

                def low(f):
                    n = 16 * use + 8 * half + f
                    dve.wait_ge(Z.n_hi, n + 1)
                    if shift is None:
                        dve.tensor_tensor(split[1][f][:, t], nrm.tmp[n % 4], split[0][f][:, t].bitcast(F32), ALU.subtract).then_inc(Z.n_lo, 1)
                    else:
                        dve.scalar_tensor_tensor(split[1][f][:, t], nrm.tmp[n % 4], modc[:, shift + f:shift + f + 1],
                                                 split[0][f][:, t].bitcast(F32), ALU.add, ALU.subtract).then_inc(Z.n_lo, 1)
                dve.wait_ge(Z.n_rstd, 2 * use + half + 1)
                for f in range(KT):
                    n = 16 * use + 8 * half + f
                    if n % 16 >= 4:
                        dve.wait_ge(Z.n_lo, n - 3)
                    dve.scalar_tensor_tensor(nrm.tmp[n % 4], src[f][:, t], gain(f), nrm.rstd[half], ALU.mult, ALU.mult).then_inc(Z.n_t, 1)
                    if f >= 2:
                        low(f - 2)
                low(KT - 2)
                low(KT - 1)

            def post(use, y, x, gain, nrm, half, first=0, end=KT):
                t = half_of(half)

                def add(f):
                    dve.wait_ge(Z.f_y, 16 * use + 8 * half + f + 1)
                    dve.tensor_tensor(x[f][:, t], x[f][:, t], y[f][:, t], ALU.add).then_inc(Z.f_x, 1)
                dve.wait_ge(Z.f_rstd, 2 * use + half + 1)
                for f in range(first, end):
                    dve.scalar_tensor_tensor(y[f][:, t], y[f][:, t], gain(f), nrm.rstd[half], ALU.mult, ALU.mult).then_inc(Z.f_y, 1)
                    if f > first:
                        add(f - 1)
                add(end - 1)

            def post_and_norm(f_use, y, f_gain, n_use, x, n_gain, nrm, split, shift):
                part = 3
                post(f_use, y, x, f_gain, nrm, 0)
                post(f_use, y, x, f_gain, nrm, 1, 0, part)
                norm(n_use, x, n_gain, nrm, split, shift, 0)
                post(f_use, y, x, f_gain, nrm, 1, part, KT)
                norm(n_use, x, n_gain, nrm, split, shift, 1)

            def add_squares(use, nrm):
                u = use // 2
                for f in range(1, KT):
                    n = (KT - 1) * u + f
                    dve.wait_ge(Z.y_sq, KT * u + f + 1)
                    if f > 1:
                        dve.wait_ge(Z.y_sum, n - 1)
                    dve.tensor_tensor(nrm.total, nrm.whole[0] if f == 1 else nrm.total, nrm.whole[f % 2], ALU.add).then_inc(Z.y_sum, 1)

            dve.wait_ge(Z.consts, 32)
            dve.tensor_tensor(small[:, 64:66], col("lq", 0, 2), col("lk", 0, 2), ALU.mult).then_inc(Z.lam_p, 1)
            dve.wait_ge(Z.tab, 48)
            tabx = T(23)[0:33, 1000:1004]
            dve.memset(T(23)[32:33, 1000:1004], NEG).then_inc(Z.setup, 1)
            dve.tensor_tensor(T(23)[0:32, 1000:1004], T(23)[0:32, 512:516], T(23)[0:32, 516:520], ALU.subtract).then_inc(Z.setup, 1)
            dve.wait_ge(Z.setup, 2)
            for h in range(HD_DIFF):
                dve.tensor_copy(T(22)[0:33, h * P:(h + 1) * P], tabx[:, h:h + 1].to_broadcast([33, P])).then_inc(Z.tb_ready, 1)
            dve.wait_ge(Z.lam_e, 1)
            dve.tensor_tensor(small[:, 68:69], small[:, 66:67], small[:, 67:68], ALU.subtract).then_inc(Z.setup, 1)
            dve.wait_ge(Z.setup, 3)
            dve.tensor_scalar(foldc[:, 1:2], small[:, 68:69], -1.0, -LAM_INIT, ALU.mult, ALU.add).then_inc(Z.setup, 1)
            dve.tensor_scalar(foldc[:, 0:1], col("subln"), 1.0 - LAM_INIT, None, ALU.mult).then_inc(Z.setup, 1)
            X1t, Y1t = [T(8 + f) for f in range(KT)], [T(f) for f in range(KT)]
            for half in range(2):
                norm(0, X1t, lambda f: col("attn_pre", f), NRM1, SPLIT_H, None, half)

            for i in range(48):
                g, k = i // 8, i % 8
                acc = MOD_ACC[g % 4]
                dve.wait_ge((Z.mod_in0, Z.mod_in1, Z.mod_in2, Z.mod_in3)[i % 4], 16 * (i // 4 + 1))
                if k == 0:
                    if g >= 4:
                        dve.wait_ge(Z.mod_ps, g - 3)
                    dve.tensor_scalar(acc, T(16 + i % 4), col("c", k), None, ALU.mult).then_inc(Z.mod_acc, 1)
                else:
                    dve.wait_ge(Z.mod_acc, i)
                    dve.scalar_tensor_tensor(acc, T(16 + i % 4), col("c", k), acc, ALU.mult, ALU.add).then_inc(Z.mod_acc, 1)
            dve.wait_ge(Z.mod_ps, 6)
            dve.scalar_tensor_tensor(modc[:], bank(7)[:, 0:48], float(D), col("b_ada", 0, 48), ALU.mult, ALU.add).then_inc(Z.mod_col, 1)
            dve.wait_ge(Z.mod_col, 1)
            for r, (name, at, add) in enumerate((("pre_mix", 8, 1.0), ("post_mix", 16, 0.0), ("pre_ffn", 32, 1.0))):
                dve.scalar_tensor_tensor(foldc[:, 8 + 8 * r:16 + 8 * r], modc[:, at:at + 8], add, col(name, 0, 8),
                                         ALU.add, ALU.mult).then_inc(Z.fold, 1)
            dve.tensor_tensor(modc[:, 40:48], modc[:, 40:48], col("post_ffn", 0, 8), ALU.mult).then_inc(Z.fold, 1)

            for n in range(8):
                for half in range(2):
                    dve.wait_ge(Z.vT, 2 * n + half + 1)
                    if n == 0:
                        dve.wait_ge(Z.e_out, 64)
                    dve.tensor_copy(V1[:, 4 * half:4 * half + 4, n * P:(n + 1) * P],
                                    bank(6 + half).rearrange("p (b n) -> p b n", b=4)).then_inc(Z.v_cp, 1)

            dve.wait_ge(Z.bias_in, 64)

            def d_max(p, m):
                h, b = D_PAIRS[p]
                v, w, i = 2 * p + m, (b + 1) * P, 2 * (p % 2) + m
                s = bank(*D_BANKS[v])
                a = max(0, (b - 1) * P)
                dve.wait_ge(Z.d_qk, v + 1)
                dve.tensor_tensor(s[:, a:w], s[:, a:w], D_BIAS[:, h * 256 + 256 - (w - a):(h + 1) * 256], ALU.add).then_inc(Z.d_near, 1)
                dve.wait_ge(Z.d_near, v + 1)
                dve.reduce_max(D_MAX[:, i:i + 1], s[:, 0:w], AX).then_inc(Z.d_max, 1)
                dve.wait_ge(Z.d_max, v + 1)
                if p >= 2:
                    dve.wait_ge(Z.d_exp, v - 3)
                dve.tensor_scalar(D_NEG[:, i:i + 1], D_MAX[:, i:i + 1], -1.0, None, ALU.mult).then_inc(Z.d_nmx, 1)

            def d_combine(p):
                w = (D_PAIRS[p][1] + 1) * P
                j = 2 * (p % 4)
                mix = D_MIX[:, p % 4:p % 4 + 1]
                dve.wait_ge(Z.d_exp, 2 * p + 2)
                if p >= 4:
                    dve.wait_ge(Z.d_post, p - 3)
                dve.reciprocal(D_REC[:, j:j + 2], D_SUM[:, j:j + 2]).then_inc(Z.d_r, 1)
                dve.wait_ge(Z.d_r, 2 * p + 1)
                dve.scalar_tensor_tensor(mix, D_REC[:, j + 1:j + 2], foldc[:, 1:2], D_SUM[:, j:j + 1], ALU.mult, ALU.mult).then_inc(Z.d_r, 1)
                dve.wait_ge(Z.d_r, 2 * p + 2)
                p0, p1 = D_P0[p % 3][:, 0:w], D_P1[p % 2][:, 0:w]
                dve.scalar_tensor_tensor(p0, p1, mix, p0, ALU.mult, ALU.add).then_inc(Z.d_w, 1)

            def d_norm(h):
                dve.wait_ge(Z.d_rs, 2 * h + 2)
                if h:
                    dve.wait_ge(Z.d_hT, h)
                v = lambda t: t.rearrange("p (b n) -> p b n", b=NB)
                dve.tensor_tensor(v(D_ON), v(D_O), D_RS.unsqueeze(2).to_broadcast([P, NB, P]), ALU.mult).then_inc(Z.d_on, 1)

            def d_low(h):
                dve.wait_ge(Z.d_hi, h + 1)
                dve.scalar_tensor_tensor(hl[:, h], bank(4, 2), foldc[:, 0:1], hh_read[:, h], ALU.mult, ALU.subtract).then_inc(Z.d_lo, 1)

            for s in range(D_STEPS):
                if d_head_end(s + 1) is not None:
                    d_norm(d_head_end(s + 1))
                if s < len(D_PAIRS):
                    d_max(s, 0)
                    d_max(s, 1)
                if 0 <= s - 1 < len(D_PAIRS):
                    d_combine(s - 1)
                if d_head_end(s) is not None:
                    d_low(d_head_end(s))

            def s_cap(u):
                hd, c, k, lo = SB_UNITS[u]
                dve.wait_ge(Z.s_z, u + 1)
                if u >= 2:
                    dve.wait_ge(Z.s_m, u - 1)
                dve.tensor_scalar(S_SP[u % 2][:, lo:], bank(u % SB_Z)[:, lo:], SP_CAP, None, ALU.min).then_inc(Z.s_capped, 1)

            def s_softplus(u):
                hd, c, k, lo = SB_UNITS[u]
                diag, first = k >= 4 * c, k == 4 * c + 3
                dve.wait_ge(Z.s_L, 2 * u + 2)
                if u >= 2:
                    dve.wait_ge(Z.s_mlo, u - 1)
                m = S_M[u % 2]
                ins = dve.tensor_tensor(m[:, lo:], bank(u % SB_Z)[:, lo:], S_SP[u % 2][:, lo:], ALU.max)
                if diag:
                    ins.then_inc(Z.s_mk, 1)
                    dve.wait_ge(Z.s_mk, SB_DIAG[u] + 1)
                    ins = dve.tensor_tensor(m[:, lo:lo + P], m[:, lo:lo + P], mat("strict"), ALU.mult)
                ins.then_inc(Z.s_m, 1)
                if k:
                    dve.wait_ge(Z.s_m, u + 1)
                    if u >= 3:
                        dve.wait_ge(Z.s_c, u - 2)
                    old, new, seen = S_CY[u % 4], S_CY[(u + 1) % 4], lo
                    if diag:
                        dve.tensor_copy(new[:, lo:lo + P], m[:, lo:lo + P]).then_inc(Z.s_cy, 1)
                        seen = lo + P
                    if not first:
                        dve.wait_ge(Z.s_cy, SB_SUMS[u])
                        dve.tensor_tensor(new[:, seen:], old[:, seen:], m[:, seen:], ALU.add).then_inc(Z.s_cy, 1)

            dve.wait_ge(Z.d_qk, 64)
            for u in range(len(SB_UNITS) + 1):
                if u < len(SB_UNITS):
                    s_cap(u)
                if u:
                    s_softplus(u - 1)
            for j in range(4):
                dve.wait_ge(Z.s_rs, j + 1)
                if j >= 2:
                    dve.wait_ge(Z.s_lo, j - 1)
                dve.scalar_tensor_tensor(S_T[j % 2], S_O[:, j], col("sbnorm"), S_RS[j % 2], ALU.mult, ALU.mult).then_inc(Z.s_t, 1)
                dve.wait_ge(Z.s_hi, j + 1)
                dve.tensor_tensor(hl[:, 4 + j], S_T[j % 2], hh_read[:, 4 + j], ALU.subtract).then_inc(Z.s_lo, 1)

            dve.wait_ge(Z.x_re, 16)
            add_squares(0, NRM1)
            post_and_norm(0, Y1t, lambda f: col("attn_post", f), 1, X1t, lambda f: col("ffn_pre", f), NRM1, SPLIT_H, None)

            def conv_col(j, r):
                o = COLS["conv1"][0] + r
                if isinstance(j, int):
                    return cols[:, o + 8 * j:o + 8 * j + 1]
                return cols[:, bass.ds(j * 8 + o, 1)]

            def taps(j, buf, b, r, lin, cv):
                pair = bank(b, 2)
                dve.wait_ge(lin, j + 1)
                dve.scalar_tensor_tensor(buf[:, 1:], pair[:, 0:S - 1], conv_col(j, r + 1), buf[:, 1:], ALU.mult, ALU.add).then_inc(cv, 1)
                dve.wait_ge(cv, j * 2 + 1)
                dve.scalar_tensor_tensor(buf[:, 2:], pair[:, 0:S - 2], conv_col(j, r), buf[:, 2:], ALU.mult, ALU.add).then_inc(cv, 1)

            def down_sums(y, j, use, c):
                dve.wait_ge(Z.dn_free, j * 16 + (16 * NJ * use + 4))
                for o in range(16):
                    f, half = o % KT, o // KT
                    if o < 15:
                        dve.wait_ge(Z.dn_done, j * 15 + (15 * NJ * use + o + 1))
                    else:
                        dve.wait_ge(Z.chunk_done, c + 1)
                    t = y[f][:, half * HALF:(half + 1) * HALF]
                    dve.tensor_tensor(t, bank(4 + o % 4), t, ALU.add).then_inc(Z.dn_free, 1)

            def zero(y, use):
                for f in range(KT):
                    dve.memset(y[f], 0.0).then_inc(Z.y_zero, 1)
                dve.wait_ge(Z.y_zero, 8 * (use + 1))

            def ffn1_step(j, b, c, sums):
                taps(j, CG[b], 0, 0, Z.g_lin, Z.g_cv)
                if sums is not None:
                    sums()
                taps(j, CV[b], 2, 4, Z.v_lin, Z.v_cv)
                dve.wait_ge(Z.g_act, j + 1)
                dve.wait_ge(Z.v_cv, j * 2 + 2)
                dve.tensor_tensor(CV[b], CV[b], CG[b], ALU.mult).then_inc(Z.f_prod, 1)
                dve.wait_ge(Z.a_hi, j + 1)
                dve.tensor_tensor(GATED[b][1], CV[b], GATED[b][0].bitcast(F32), ALU.subtract).then_inc(Z.a_lo, 1)

            dve.wait_ge(Z.f_x, 16)
            ffn1_step(0, 0, C_FFN1, None)
            zero(Y1t, 0)
            dve.sem_inc(Z.dn_free, 4)
            with dve.Fori(0, (NJ - 2) // 2) as i:
                for u in range(2):
                    c = i * 6 + ffn_gate(C_FFN1, 1 + u)
                    ffn1_step(i * 2 + (1 + u), (1 + u) % 2, c, lambda: down_sums(Y1t, i * 2 + u, 0, c + 2))
            j = NJ - 1
            ffn1_step(j, j % 2, ffn_gate(C_FFN1, j), lambda: down_sums(Y1t, j - 1, 0, ffn_gate(C_FFN1, j) + 2))
            down_sums(Y1t, j, 0, ffn_down_last(C_FFN1))
            dve.wait_ge(Z.dn_free, 4 + 16 * NJ)
            dve.wait_ge(Z.fold, 4)
            post_and_norm(1, Y1t, lambda f: col("ffn_post", f), 2, X1t, lambda f: foldc[:, 8 + f:9 + f], NRM1, SPLIT_H, 0)

            C1 = 6.28125
            C2 = float(np.float32(2 * math.pi - C1))
            C3 = 2 * math.pi - C1 - C2
            MAGIC = 12582912.0
            PI = float(np.float32(3.1415925))
            tr = [0]

            def trig(ins):
                ins.then_inc(Z.trig, 1)
                tr[0] += 1
                dve.wait_ge(Z.trig, tr[0])

            dve.wait_ge(Z.pos_in, 16)
            trig(dve.tensor_scalar(ROW1, ROW2.bitcast(I32), col("invf"), None, ALU.mult))
            for dst, shift in ((SIN, 0.0), (COS, 0.25)):
                trig(dve.tensor_scalar(ROW2, ROW1, float(np.float32(0.5 / math.pi)), shift, ALU.mult, ALU.add))
                trig(dve.tensor_scalar(ROW2, ROW2, MAGIC, -MAGIC, ALU.add, ALU.add))
                trig(dve.scalar_tensor_tensor(dst, ROW2, -C1, ROW1, ALU.mult, ALU.add))
                trig(dve.scalar_tensor_tensor(dst, ROW2, -C2, dst, ALU.mult, ALU.add))
                trig(dve.scalar_tensor_tensor(dst, ROW2, -C3, dst, ALU.mult, ALU.add))
                if shift == 0.0:
                    trig(dve.tensor_scalar(dst, dst, PI, -PI, ALU.min, ALU.max))
                else:
                    trig(dve.tensor_scalar(dst, dst, math.pi / 2, PI, ALU.add, ALU.min))
                    trig(dve.tensor_scalar(dst, dst, -PI, None, ALU.max))

            dve.wait_ge(Z.spill, 16)
            for h in range(HD_ML):
                o = P + h * 129 + 128
                dve.memset(V2[:, :, o:o + 1], 1.0).then_inc(Z.fold, 1)
            if_n = [0]

            def gate_rows(ins):
                ins.then_inc(Z.if_ch, 1)

            for n in range(N_IN):
                r = RING[n % 2]
                if 1 <= n < 6:
                    m = n - 1
                    for half in range(2):
                        dve.wait_ge(Z.vT, 16 + 2 * m + half + 1)
                        o = 0 if m == 0 else P + (m - 1) * 129
                        dve.tensor_copy(V2[:, 4 * half:4 * half + 4, o:o + P],
                                        bank(6 + half).rearrange("p (b n) -> p b n", b=4)).then_inc(Z.v_cp, 1)
                if n == 5:
                    dve.wait_ge(Z.if_ev, 6)
                    gate_rows(dve.scalar_tensor_tensor(ROW2[32:36, :], ROW1[32:36, :], -1.0, ROW1[32:36, :], ALU.mult, ALU.max))
                if n == 6:
                    dve.wait_ge(Z.if_act, 2)
                    gate_rows(dve.scalar_tensor_tensor(ROW2[0:4, :], ROW1[32:36, :], 0.0, ROW2[32:36, :], ALU.min, ALU.subtract))
                    dve.wait_ge(Z.if_ch, 3)
                    gate_rows(dve.tensor_tensor_scan(ROW2[0:4, :], ROW2[0:4, :], ROW2[0:4, :], 0.0, ALU.add, ALU.min))
                    dve.wait_ge(Z.if_ch, 4)
                    gate_rows(dve.tensor_tensor(ROW1[0:4, :], ROW1[0:4, :], ROW2[0:4, :], ALU.subtract))
                    dve.wait_ge(Z.if_ch, 5)
                    gate_rows(dve.tensor_tensor_scan(ROW1[32:36, :], ROW1[0:4, :], ROW1[0:4, :], 0.0, ALU.max, ALU.max))
                if n == 8:
                    dve.wait_ge(Z.if_act, 3)
                    gate_rows(dve.tensor_tensor(ROW2[32:36, :], ROW2[32:36, :], ROW1[32:36, :], ALU.add))
                if 6 <= n < 14:
                    o = 5 * (n - 6)
                    pair = bank(2 * (n % 3), 2)
                    dve.wait_ge(Z.cv_lin, n - 5)
                    for tap in range(1, 4):
                        if tap > 1:
                            dve.wait_ge(Z.cv_t, 3 * (n - 6) + tap - 1)
                        dve.scalar_tensor_tensor(r[0][:, tap:], pair[:, 0:S - tap], col("mconv", o + 3 - tap), r[0][:, tap:],
                                                 ALU.mult, ALU.add).then_inc(Z.cv_t, 1)
                if 14 <= n < 19:
                    i = n - 14
                    dst = T(i)
                    if i == 0:
                        dve.wait_ge(Z.trig_sin, 2)
                    dve.wait_ge((Z.rope_sw0, Z.rope_sw1)[n % 2], 64 * (i // 2 + 1))
                    dve.tensor_tensor(dst, r[0], COS, ALU.mult).then_inc(Z.rope_t, 1)
                    dve.tensor_tensor(r[1], r[1], SIN, ALU.mult).then_inc(Z.rope_t, 1)
                    dve.wait_ge(Z.rope_t, 2 * (i + 1))
                    dve.tensor_tensor(dst, dst, r[1], ALU.add).then_inc(Z.rope_done, 1)

            dve.wait_ge(Z.chunk_done, C_BR)
            for h in range(HD_ML):
                ins = dve.tensor_scalar(M_SEL[32:36, h * P:(h + 1) * P], mat("ident")[32:36, 32 + h:33 + h].to_broadcast([4, P]),
                                        -1.0, None, ALU.mult)
            ins.then_inc(Z.m_sel, 1)

            def m_diag(s):
                w, h, c, k, lo = ML_SUBS[s]
                i = ML_DIAG[s]
                if i >= 2:
                    dve.wait_ge(Z.m_E, ML_E[ML_DIAG_OF[i - 2]])
                dve.tensor_tensor(M_D[i % 2], NEGMB[:, h, k * P:(k + 1) * P], mat("negcausal"), ALU.add).then_inc(Z.m_d, 1)

            dve.wait_ge(Z.m_mbc, 8)
            m_diag(ML_DIAG_OF[0])
            diagonals = [1]

            def m_weigh(x):
                for s, (w, h, c, k, lo) in enumerate(ML_SUBS):
                    if w != x:
                        continue
                    if diagonals[0] < len(ML_DIAG_OF) and ML_DIAG_OF[diagonals[0]] <= s + 1:
                        m_diag(ML_DIAG_OF[diagonals[0]])
                        diagonals[0] += 1
                    dve.wait_ge(Z.m_E, ML_E[s])
                    dve.wait_ge(Z.m_S, s + 1)
                    if w >= 2:
                        dve.wait_ge(Z.m_pv, 4 * (w - 1))
                    dve.scalar_tensor_tensor(M_A[w % 2][:, k, lo:], bank(s % 4)[:, lo:], ML_D ** -0.5, M_E[s % 2][:, lo:],
                                             ALU.mult, ALU.mult).then_inc(Z.m_A, 1)

            def l_means(w):
                den, em = unit_columns(L_DEN, w), unit_columns(EMT, w)
                dve.wait_ge(Z.m_U, 8 * (w + 1))
                dve.tensor_scalar(unit_columns(L_MU, w), unit_columns(L_SUM, w), -1.0 / P, None, ALU.mult).then_inc(Z.l_mu, 1)
                dve.scalar_tensor_tensor(den, den, -1.0, den, ALU.mult, ALU.max).then_inc(Z.l_den, 1)
                dve.wait_ge(Z.l_den, 3 * w + 1)
                dve.tensor_tensor(den, den, em, ALU.max).then_inc(Z.l_den, 1)
                dve.wait_ge(Z.l_den, 3 * w + 2)
                dve.reciprocal(den, den).then_inc(Z.l_den, 1)

            def l_variances(w):
                ss, rec = unit_columns(L_SS, w), unit_columns(L_DEN, w)
                dve.wait_ge(Z.l_sq, 4 * (w + 1))
                dve.wait_ge(Z.l_den, 3 * w + 3)
                dve.tensor_tensor(ss, ss, rec, ALU.mult).then_inc(Z.l_v, 1)
                dve.wait_ge(Z.l_v, 2 * w + 1)
                dve.tensor_tensor(ss, ss, rec, ALU.mult).then_inc(Z.l_v, 1)

            def l_rows(w):
                dve.wait_ge(Z.l_rs, 2 * (w + 1))
                dve.tensor_tensor(unit_columns(L_DEN, w), unit_columns(L_DEN, w), unit_columns(L_SS, w), ALU.mult).then_inc(Z.l_s, 1)
                dve.wait_ge(Z.l_s, w + 1)
                for i in unit_rows(w):
                    dve.tensor_scalar(U[:, i, 0:P], U[:, i, 0:P], L_MU[:, i:i + 1], L_DEN[:, i:i + 1], ALU.add, ALU.mult).then_inc(Z.l_y, 1)

            def l_gate(w):
                h, c = w // 2, w % 2
                g = NEGMB[:, h, half_of(c)]
                dve.wait_ge((Z.so_in0, Z.so_in1, Z.so_in2, Z.so_in3)[h], 16)
                dve.wait_ge(Z.l_T, w + 1)
                dve.scalar_tensor_tensor(g, bank(7), col("mnorm", h), g, ALU.mult, ALU.mult).then_inc(Z.l_g, 1)

            def l_low(w):
                h, c = w // 2, w % 2
                dve.wait_ge(Z.l_hi, w + 1)
                dve.tensor_tensor(hl[:, 4 + h, half_of(c)], NEGMB[:, h, half_of(c)], hh_read[:, 4 + h, half_of(c)], ALU.subtract).then_inc(Z.l_lo, 1)

            def w_mask(u):
                n, g = u // 2, u % 2
                a = 0 if n else P
                v = lambda t: t.rearrange("p (j k) -> p j k", j=4)[:, :, a:]
                sm = W_SM[u % 3]
                sink = col("sinks", 4 * g, 4)

                def did(ins, i):
                    ins.then_inc(Z.w_a, 1)
                    dve.wait_ge(Z.w_a, 5 * u + i)
                dve.wait_ge(Z.w_qk, u + 1)
                if u >= 3:
                    dve.wait_ge(Z.w_T, u - 2)
                mask = mat("band")[:, a:].unsqueeze(1).to_broadcast([P, 4, 2 * P - a])
                did(dve.tensor_tensor(v(W_P[u % 3]), v(bank(2 * (u % 2), 2)), mask, ALU.add), 1)
                did(dve.tensor_reduce(sm[:, 0:4], v(W_P[u % 3]), AX, ALU.max), 2)
                did(dve.tensor_tensor(sm[:, 0:4], sm[:, 0:4], sink, ALU.max), 3)
                did(dve.tensor_scalar(sm[:, 4:8], sm[:, 0:4], -1.0, None, ALU.mult), 4)
                dve.tensor_tensor(sm[:, 8:12], sink, sm[:, 0:4], ALU.subtract).then_inc(Z.w_a, 1)

            def w_norm(u):
                n = u // 2
                a = 0 if n else P
                sm = W_SM[u % 3]
                dve.wait_ge(Z.w_exp, 5 * u + 5)
                dve.tensor_tensor(sm[:, 12:16], sm[:, 12:16], sm[:, 8:12], ALU.add).then_inc(Z.w_b, 1)
                dve.wait_ge(Z.w_b, 2 * u + 1)
                dve.reciprocal(sm[:, 16:20], sm[:, 12:16]).then_inc(Z.w_b, 1)
                dve.wait_ge(Z.w_b, 2 * u + 2)
                v = W_P[u % 3].rearrange("p (j k) -> p j k", j=4)[:, :, a:]
                dve.tensor_tensor(v, v, sm[:, 16:20].unsqueeze(2).to_broadcast([P, 4, 2 * P - a]), ALU.mult).then_inc(Z.w_pn, 1)

            def w_low(n):
                dve.wait_ge(Z.w_hi, n + 1)
                t = slice(n * P, (n + 1) * P)
                dve.tensor_tensor(hl[:, 0:4, t], bank(6 + n % 2).rearrange("p (j q) -> p j q", j=4), hh_read[:, 0:4, t], ALU.subtract).then_inc(Z.w_lo, 1)

            for s in range(W_STEPS):
                u = s - ML_N
                if s < ML_N:
                    m_weigh(s)
                elif u < W_UNITS:
                    w_mask(u)
                if u >= 6 and u % 2 == 0:
                    w_low((u - 6) // 2)
                if 0 <= u - 1 < W_UNITS:
                    w_norm(u - 1)
                if 0 <= s - 4 < ML_N:
                    l_rows(s - 4)
                if 0 <= s - 3 < ML_N:
                    l_variances(s - 3)
                if 0 <= s - 2 < ML_N:
                    l_means(s - 2)
                if 0 <= s - 5 < ML_N:
                    l_gate(s - 5)
                if 0 <= s - 6 < ML_N:
                    l_low(s - 6)

            for f in range(KT):
                t, u = B_T[f % 2]
                dve.wait_ge((Z.gate0, Z.gate1)[f % 2], 32 * (f // 2 + 1))
                dve.wait_ge(Z.chunk_done, C_BR + f + 1)
                if f >= 2:
                    dve.wait_ge(Z.b_lo, f - 1)
                dve.tensor_tensor(t, bank(4 * (f % 2), 2), B_G[f % 2][0], ALU.mult).then_inc(Z.b_a, 1)
                dve.tensor_tensor(u, bank(4 * (f % 2) + 2, 2), B_G[f % 2][1], ALU.mult).then_inc(Z.b_m, 1)
                dve.wait_ge(Z.b_a, f + 1)
                dve.wait_ge(Z.b_m, f + 1)
                dve.tensor_tensor(t, t, u, ALU.add).then_inc(Z.b_s, 1)
                dve.wait_ge(Z.b_hi, f + 1)
                dve.tensor_tensor(SPLIT_A[1][f], t, SPLIT_A[0][f].bitcast(F32), ALU.subtract).then_inc(Z.b_lo, 1)

            Y2t, X2t = [T(16 + f) for f in range(KT)], [hhf[:, f] for f in range(KT)]
            YF2 = [hlf[:, f] for f in range(KT)]
            dve.wait_ge(Z.x2_in, 16)
            add_squares(2, HL_TMP)
            post_and_norm(2, Y2t, lambda f: foldc[:, 16 + f:17 + f], 3, X2t, lambda f: foldc[:, 24 + f:25 + f], HL_TMP, SPLIT_A, 24)

            def ffn2_step(j, b, c, sums):
                if sums is not None:
                    sums()
                dve.wait_ge(Z.g_lin, j + (NJ + 1))
                dve.wait_ge(Z.chunk_done, c + 2)
                dve.tensor_tensor(CV[b], bank(2, 2), CG[b], ALU.mult).then_inc(Z.f_prod, 1)
                dve.wait_ge(Z.a_hi, j + (NJ + 1))
                dve.tensor_tensor(GATED[b][1], CV[b], GATED[b][0].bitcast(F32), ALU.subtract).then_inc(Z.a_lo, 1)

            dve.wait_ge(Z.n_lo, 64)
            ffn2_step(0, 0, C_FFN2, None)
            zero(YF2, 1)
            with dve.Fori(0, (NJ - 2) // 2) as i:
                for u in range(2):
                    c = i * 6 + ffn_gate(C_FFN2, 1 + u)
                    ffn2_step(i * 2 + (1 + u), (1 + u) % 2, c, lambda: down_sums(YF2, i * 2 + u, 1, c + 2))
            j = NJ - 1
            ffn2_step(j, j % 2, ffn_gate(C_FFN2, j), lambda: down_sums(YF2, j - 1, 1, ffn_gate(C_FFN2, j) + 2))
            down_sums(YF2, j, 1, ffn_down_last(C_FFN2))
            dve.wait_ge(Z.dn_free, 4 + 32 * NJ)
            for half in range(2):
                post(3, YF2, X2t, lambda f: modc[:, 40 + f:41 + f], NRM2, half)




_OUT = (KT, P, S)


def columns(v):
    v = np.asarray(v).reshape(-1)
    return v.reshape(-1, P).T


def chunks(w, feature_tiles):
    k = w.shape[0] // P
    return w.reshape(k, P, feature_tiles, P).transpose(2, 1, 0, 3).reshape(feature_tiles, P, k * P)


def ffn_chunks(gate, value, down):
    out = [gate[0], value[0]]
    for j in range(1, NJ):
        out += [gate[j], value[j], down[j - 1]]
    return np.stack(out + [down[NJ - 1]])


def kernel(**a):
    import concourse.bacc as bacc
    from concourse.bass_utils import run_bass_kernel_spmd

    a = {n: np.asarray(v) for n, v in a.items()}
    x = np.ascontiguousarray(a["x"][0].T.reshape(KT, P, S))

    dq, dk, dv, sq, sk, sv = np.split(a["w_qkv"][0], 6, axis=1)
    qkv = chunks(np.concatenate([dq, sq, dk, sk, dv, sv], axis=1), N_QKV)
    up = chunks(a["w_up"][0], 2 * NJ)
    ffn1 = ffn_chunks(up[:NJ], up[NJ:], a["w_down"][0].reshape(NJ, P, D))
    sizes = np.cumsum((512, 128, 128, 512, 512, 512, 512, 4, 4, 1024))
    q_a, k_a, v_a, q_m, k_m, v_m, o_m, i_m, f_m, g_a, g_m = np.split(a["w_in_2"][0], sizes, axis=1)
    q_a = q_a.reshape(D, 2, 4, DH).transpose(0, 2, 1, 3).reshape(D, 512)
    rows = np.zeros((D, P), np.float32)
    rows[:, 0:4], rows[:, 32:36] = i_m, f_m
    w_in = chunks(np.concatenate([v_a, v_m, rows, q_m, k_m, q_a, k_a, o_m, g_a, g_m], axis=1), N_IN)
    w_ba = a["w_branch_attn_2"][0].reshape(2, 4, DH, D).transpose(1, 0, 2, 3).reshape(512, D)
    branch = chunks(np.concatenate([w_ba, a["w_branch_mlstm_2"][0]], axis=0), N_MIX)
    ffn2 = ffn_chunks(chunks(a["w_ffn_gate_2"][0], NJ), chunks(a["w_ffn_up_2"][0], NJ), a["w_ffn_down_2"][0].reshape(NJ, P, D))
    w = np.concatenate([qkv, chunks(a["w_o"][0], N_MIX), ffn1, w_in, branch, chunks(a["w_out_2"][0], N_MIX), ffn2])

    c = np.zeros((P, N_COLS), np.float32)

    def put(name, v):
        o, n = COLS[name]
        c[:, o:o + n] = v

    for name, key in (("attn_pre", "attn_pre_norm"), ("attn_post", "attn_post_norm"), ("ffn_pre", "ffn_pre_norm"),
                      ("ffn_post", "ffn_post_norm"), ("subln", "diff_subln"), ("b_ada", "b_ada_2"), ("c", "c_2"),
                      ("pre_mix", "g_pre_mix_2"), ("post_mix", "g_post_mix_2"), ("pre_ffn", "g_pre_ffn_2"),
                      ("post_ffn", "g_post_ffn_2"), ("mnorm", "mlstm_norm_w_2")):
        put(name, columns(a[key]))
    put("sbnorm", np.concatenate([a["sb_norm"][0]] * 2)[:, None])
    taps = np.concatenate([a["conv_w"][0], a["conv_b"]]).reshape(4, 2, NJ, P)
    put("conv1", taps.transpose(3, 2, 1, 0).reshape(P, NJ * 8))
    taps = np.concatenate([a["conv_w_2"][0], a["conv_b_2"]]).reshape(5, 8, P)
    put("mconv", taps.transpose(2, 1, 0).reshape(P, 40))
    for name, k1, k2 in (("lq", "lambda_q1", "lambda_q2"), ("lk", "lambda_k1", "lambda_k2")):
        o, _ = COLS[name]
        c[0:DH, o], c[0:DH, o + 1] = a[k1][0], a[k2][0]
    o, _ = COLS["b_if"]
    c[0:4, o], c[32:36, o] = a["b_if_2"][0, 0:4], a["b_if_2"][0, 4:8]
    put("sinks", np.broadcast_to(a["attn_sinks_2"], (P, 8)))
    put("eps", EPS)
    i = np.arange(P)
    put("invf", (np.float32(10000.0) ** (np.float32(-2.0) * (i % 32).astype(np.float32) / np.float32(DH)))[:, None])
    put("sgn", np.where(i % DH < 32, -1.0, 1.0)[:, None])
    mats, onehot = host_matrices()
    arrays = {
        "x_t": x, "weights": w, "columns": c, "matrices": mats, "onehot": onehot,
        "table": np.ascontiguousarray(a["rel_bias"]),
        "table_last": np.ascontiguousarray(np.broadcast_to(a["rel_bias"][31:32], (32, HD_DIFF))),
        "w_ada": np.ascontiguousarray(a["w_ada_2"][0].reshape(KT, P, 6 * D)),
        "positions": np.ascontiguousarray(np.broadcast_to(a["positions_2"], (P, S))),
    }
    nc = bacc.Bacc("TRN2", target_bir_lowering=False, num_devices=1)
    d = {n: nc.dram_tensor(n, v.shape, mybir.dt.from_np(v.dtype), kind="ExternalInput").ap() for n, v in arrays.items()}
    out = nc.dram_tensor("out_t", _OUT, F32, kind="ExternalOutput").ap()
    build(nc, Arrays(x=d["x_t"], w=d["weights"], cols=d["columns"], mats=d["matrices"], onehot=d["onehot"],
                              table=d["table"], table31=d["table_last"], w_ada=d["w_ada"], positions=d["positions"], out=out))
    r = run_bass_kernel_spmd(nc, [arrays], core_ids=[0])
    y = r.results[0]["out_t"]
    return np.ascontiguousarray(y.reshape(D, S).T).reshape(1, S, D)
```
